# Optimizing a Trainium2 kernel written in Bass

```python
import jax
import jax.numpy as jnp
from jax import lax
import numpy as np

D_MODEL = 1024
BATCH = 1
SEQ = 256
DEPTH = 2
DEC_BATCH = 8
DEC_SEQ = 8
PAST_LEN = 256
PAGE_SIZE = 128

N_EVEN = (DEPTH + 1) // 2
N_ODD = DEPTH // 2
A_HEADS = 8
A_KV_HEADS = 2
A_HEAD_DIM = D_MODEL // 16
A_WIDTH = A_HEADS * A_HEAD_DIM
ROT_DIM = A_HEAD_DIM // 4
ROPE_THETA = 500000.0
IDX_HEADS = 4
IDX_DIM = A_HEAD_DIM
TOPK_MAX = 256
Q_BLOCK = 128
RET_HEADS = 4
RET_HEAD_DIM = D_MODEL // 8
RET_WIDTH = RET_HEADS * RET_HEAD_DIM
RET_THETA = 10000.0
RET_CHUNK = 128
D_RNN = D_MODEL
RG_BLOCKS = 8
RG_BLOCK_W = D_RNN // RG_BLOCKS
CONV_W = 4
RG_C = 8.0
D_FF = 128 * ((8 * D_MODEL // 3 + 127) // 128)
EPS = 1e-6
N_MOD = 9
EVEN_SIZES = (A_WIDTH, A_KV_HEADS * A_HEAD_DIM, A_KV_HEADS * A_HEAD_DIM, IDX_HEADS * IDX_DIM, IDX_HEADS, IDX_DIM,
              RET_WIDTH, RET_WIDTH, RET_WIDTH, RET_WIDTH)
P_EVEN = sum(EVEN_SIZES)

kernel_name = 'hybrid_dsa_retention_rglru_step'

def rmsnorm(x, g=None):
    xf = x.astype(jnp.float32)
    y = xf * lax.rsqrt(jnp.mean(xf * xf, axis=-1, keepdims=True) + EPS)
    if g is not None:
        y = y * g.astype(jnp.float32)
    return y.astype(x.dtype)

def modulate(h, shift, scale):
    return h * (1 + scale) + shift

def rope(x, pos, inv_freq):
    half = inv_freq.shape[0]
    rot = 2 * half
    ang = pos.astype(jnp.float32)[:, None] * inv_freq[None, :]
    cos = jnp.cos(ang)[None, :, None, :]
    sin = jnp.sin(ang)[None, :, None, :]
    xf = x.astype(jnp.float32)
    x1 = xf[..., :half]
    x2 = xf[..., half:rot]
    out = jnp.concatenate([x1 * cos - x2 * sin, x2 * cos + x1 * sin, xf[..., rot:]], axis=-1)
    return out.astype(x.dtype)

def partial_inv_freq():
    return jnp.power(jnp.float32(ROPE_THETA), -jnp.arange(0, ROT_DIM, 2, dtype=jnp.float32) / ROT_DIM)

def retention_inv_freq():
    return jnp.power(jnp.float32(RET_THETA), -jnp.linspace(0.0, 1.0, RET_HEAD_DIM // 2, dtype=jnp.float32))

def swiglu(h, wg, wu, wd):
    return (jax.nn.silu(h @ wg) * (h @ wu)) @ wd

def dsa_block(q, qi, wi, qpos, k, v, ki, kpos, topk):
    B, T, H, Dh = q.shape
    hkv = k.shape[2]
    raw = jnp.einsum('bthd,bsd->bths', qi, ki).astype(jnp.float32) * (IDX_DIM ** -0.5)
    score = jnp.einsum('bths,bth->bts', jax.nn.relu(raw), wi.astype(jnp.float32)) * (IDX_HEADS ** -0.5)
    visible = kpos[None, :] <= qpos[:, None]
    score = jnp.where(visible[None], score, -jnp.inf)
    _, idx = lax.top_k(score, topk)
    valid = kpos[idx] <= qpos[None, :, None]
    gather = jax.vmap(lambda a, i: a[i])
    k_sel = gather(k, idx)
    v_sel = gather(v, idx)
    qg = q.reshape(B, T, hkv, H // hkv, Dh)
    logits = jnp.einsum('btgrd,btkgd->btgrk', qg, k_sel).astype(jnp.float32) * (Dh ** -0.5)
    logits = jnp.where(valid[:, :, None, None, :], logits, -jnp.inf)
    prob = jax.nn.softmax(logits, axis=-1).astype(v.dtype)
    o = jnp.einsum('btgrk,btkgd->btgrd', prob, v_sel)
    return o.reshape(B, T, H * Dh)

def dsa_attention(q, qi, wi, qpos, k, v, ki, kpos, topk):
    B, T = q.shape[:2]
    if T <= Q_BLOCK or T % Q_BLOCK != 0:
        return dsa_block(q, qi, wi, qpos, k, v, ki, kpos, topk)
    n = T // Q_BLOCK

    def split(a):
        return jnp.swapaxes(a.reshape(B, n, Q_BLOCK, *a.shape[2:]), 0, 1)

    def one_block(args):
        qb, qib, wb, pb = args
        return dsa_block(qb, qib, wb, pb, k, v, ki, kpos, topk)

    out = lax.map(one_block, (split(q), split(qi), split(wi), qpos.reshape(n, Q_BLOCK)))
    return jnp.swapaxes(out, 0, 1).reshape(B, T, -1)

def retention(q, k, v, s0):
    B, L, H, DK = q.shape
    DV = v.shape[-1]
    C = RET_CHUNK if L % RET_CHUNK == 0 else L
    n = L // C
    log_g = jnp.log1p(-jnp.power(2.0, -5.0 - jnp.arange(H, dtype=jnp.float32)))
    idx = jnp.arange(C, dtype=jnp.float32)
    diff = idx[:, None] - idx[None, :]
    decay = jnp.where(diff >= 0, jnp.exp(jnp.maximum(diff, 0.0)[None] * log_g[:, None, None]), 0.0)
    q_dec = jnp.exp((idx[:, None] + 1.0) * log_g[None, :])
    k_dec = jnp.exp((C - 1.0 - idx[:, None]) * log_g[None, :])
    c_dec = jnp.exp(C * log_g)

    def blocks(a):
        return jnp.moveaxis(a.astype(jnp.float32).reshape(B, n, C, H, a.shape[-1]), 1, 0)

    def step(s, inp):
        qb, kb, vb = inp
        att = jnp.einsum('bihd,bjhd->bhij', qb, kb) * decay[None]
        inner = jnp.einsum('bhij,bjhv->bihv', att, vb)
        cross = jnp.einsum('bihd,bhdv->bihv', qb, s) * q_dec[None, :, :, None]
        s = s * c_dec[None, :, None, None] + jnp.einsum('bjhd,bjhv->bhdv', kb * k_dec[None, :, :, None], vb)
        return s, inner + cross

    s, out = lax.scan(step, s0.astype(jnp.float32), (blocks(q), blocks(k), blocks(v)))
    out = jnp.moveaxis(out, 0, 1).reshape(B, L, H, DV)
    return out, s

def linear_scan(a, b, h0):
    b = b.at[:, 0].add(a[:, 0] * h0)

    def comb(x, y):
        a1, b1 = x
        a2, b2 = y
        return a1 * a2, a2 * b1 + b2

    _, h = lax.associative_scan(comb, (a, b), axis=1)
    return h

def even_mixer(h, pos, e, past, p):
    B, L, _ = h.shape
    proj = h @ p['w_in_even'][e]
    points = [int(s) for s in np.cumsum(EVEN_SIZES)[:-1]]
    q, k, v, qi, wi, ki, rq, rk, rv, rg = jnp.split(proj, points, axis=-1)
    inv_a = partial_inv_freq()
    q = rope(q.reshape(B, L, A_HEADS, A_HEAD_DIM), pos, inv_a)
    k = rope(k.reshape(B, L, A_KV_HEADS, A_HEAD_DIM), pos, inv_a)
    v = v.reshape(B, L, A_KV_HEADS, A_HEAD_DIM)
    qi = rope(qi.reshape(B, L, IDX_HEADS, IDX_DIM), pos, inv_a)
    ki = rope(ki.reshape(B, L, 1, IDX_DIM), pos, inv_a)[:, :, 0]
    if past is None:
        k_all, v_all, ki_all, kpos = k, v, ki, pos
        s0 = jnp.zeros((B, RET_HEADS, RET_HEAD_DIM, RET_HEAD_DIM), jnp.float32)
    else:
        page_table = past['page_table']

        def gather_pages(pool):
            g = pool[e][page_table]
            return g.reshape(B, g.shape[1] * g.shape[2], *g.shape[3:])

        k_all = jnp.concatenate([gather_pages(past['cache_k']).astype(k.dtype), k], axis=1)
        v_all = jnp.concatenate([gather_pages(past['cache_v']).astype(v.dtype), v], axis=1)
        ki_all = jnp.concatenate([gather_pages(past['cache_kidx']).astype(ki.dtype), ki], axis=1)
        kpos = jnp.arange(k_all.shape[1], dtype=jnp.int32)
        s0 = past['state_ret'][e]
    topk = min(TOPK_MAX, k_all.shape[1] // 4)
    o_a = dsa_attention(q, qi, wi, pos, k_all, v_all, ki_all, kpos, topk)
    inv_r = retention_inv_freq()
    rq = rope(rq.reshape(B, L, RET_HEADS, RET_HEAD_DIM), pos, inv_r)
    rk = rope(rk.reshape(B, L, RET_HEADS, RET_HEAD_DIM) * (RET_HEAD_DIM ** -0.5), pos, inv_r)
    rv = rv.reshape(B, L, RET_HEADS, RET_HEAD_DIM)
    o_r, s_new = retention(rq, rk, rv, s0)
    o_r = rmsnorm(o_r).reshape(B, L, RET_WIDTH).astype(h.dtype) * jax.nn.silu(rg)
    out = jnp.concatenate([o_a, o_r], axis=-1) @ p['w_out_even'][e]
    return out, (k, v, ki, s_new.astype(h.dtype))

def odd_mixer(h, pos, o, past, p):
    B, L, _ = h.shape
    proj = h @ p['w_in_odd'][o]
    gate_br, xb = jnp.split(proj, 2, axis=-1)
    if past is None:
        buf = jnp.zeros((B, CONV_W - 1, D_RNN), xb.dtype)
        h0 = jnp.zeros((B, D_RNN), jnp.float32)
    else:
        buf = past['state_conv'][o].astype(xb.dtype)
        h0 = past['state_rglru'][o].astype(jnp.float32)
    xc = jnp.concatenate([buf, xb], axis=1)
    cw = p['conv_w'][o]
    conv = sum(xc[:, j:j + L] * cw[j] for j in range(CONV_W)) + p['conv_b'][o]
    new_buf = xc[:, L:]
    xg = conv.reshape(B, L, RG_BLOCKS, RG_BLOCK_W)
    r = jax.nn.sigmoid(jnp.einsum('blnd,nde->blne', xg, p['w_rg_a'][o]).reshape(B, L, D_RNN) + p['b_rg_a'][o])
    i = jax.nn.sigmoid(jnp.einsum('blnd,nde->blne', xg, p['w_rg_x'][o]).reshape(B, L, D_RNN) + p['b_rg_x'][o])
    log_a = -RG_C * r.astype(jnp.float32) * jax.nn.softplus(-p['rg_lambda'][o].astype(jnp.float32))
    a = jnp.exp(log_a)
    mult = jnp.sqrt(-jnp.expm1(2.0 * log_a))
    mult = jnp.where((pos == 0)[None, :, None], 1.0, mult)
    b = mult * (i * conv).astype(jnp.float32)
    hs = linear_scan(a, b, h0)
    y = hs.astype(h.dtype) * jax.nn.gelu(gate_br)
    out = y @ p['w_out_odd'][o]
    return out, (new_buf, hs[:, -1].astype(h.dtype))

def trunk(x, c, pos, past, p):
    B, L, D = x.shape
    silu_c = jax.nn.silu(c)
    ks, vs, kis, rets, convs, hs = [], [], [], [], [], []
    for l in range(DEPTH):
        mod = (silu_c @ p['w_ada'][l] + p['b_ada'][l]).reshape(B, N_MOD, D)
        m = [mod[:, j][:, None, :] for j in range(N_MOD)]
        hh = modulate(rmsnorm(x, p['g_pre'][l, 0]), m[0], m[1])
        f = swiglu(hh, p['w_ffn_gate'][l, 0], p['w_ffn_up'][l, 0], p['w_ffn_down'][l, 0])
        x = x + 0.5 * m[2] * rmsnorm(f, p['g_post'][l, 0])
        hh = modulate(rmsnorm(x, p['g_pre'][l, 1]), m[3], m[4])
        if l % 2 == 0:
            y, (k_new, v_new, ki_new, s_new) = even_mixer(hh, pos, l // 2, past, p)
            ks.append(k_new)
            vs.append(v_new)
            kis.append(ki_new)
            rets.append(s_new)
        else:
            y, (buf_new, h_new) = odd_mixer(hh, pos, l // 2, past, p)
            convs.append(buf_new)
            hs.append(h_new)
        x = x + m[5] * rmsnorm(y, p['g_post'][l, 1])
        hh = modulate(rmsnorm(x, p['g_pre'][l, 2]), m[6], m[7])
        f = swiglu(hh, p['w_ffn_gate'][l, 1], p['w_ffn_up'][l, 1], p['w_ffn_down'][l, 1])
        x = x + 0.5 * m[8] * rmsnorm(f, p['g_post'][l, 2])
    return x, (jnp.stack(ks), jnp.stack(vs), jnp.stack(kis), jnp.stack(rets), jnp.stack(convs), jnp.stack(hs))

def setup_inputs(seed: int = 0) -> dict:
    key = jax.random.key(seed)
    it = iter(jax.random.split(key, 32))

    def nrm(shape, s):
        return jax.random.normal(next(it), shape, jnp.float32) * s

    n_pages = PAST_LEN // PAGE_SIZE
    n_phys = (DEC_BATCH * n_pages * 5) // 4
    x_prompt = nrm((BATCH, SEQ, D_MODEL), 1.0)
    x_sample = nrm((DEC_BATCH, DEC_SEQ, D_MODEL), 1.0)
    cache_k = nrm((N_EVEN, n_phys, PAGE_SIZE, A_KV_HEADS, A_HEAD_DIM), 1.0)
    cache_v = nrm((N_EVEN, n_phys, PAGE_SIZE, A_KV_HEADS, A_HEAD_DIM), 1.0)
    cache_kidx = nrm((N_EVEN, n_phys, PAGE_SIZE, IDX_DIM), 1.0)
    state_ret = nrm((N_EVEN, DEC_BATCH, RET_HEADS, RET_HEAD_DIM, RET_HEAD_DIM), 0.1)
    state_conv = nrm((N_ODD, DEC_BATCH, CONV_W - 1, D_RNN), 1.0)
    state_rglru = nrm((N_ODD, DEC_BATCH, D_RNN), 0.5)
    page_table = jax.random.permutation(next(it), n_phys)[: DEC_BATCH * n_pages].reshape(DEC_BATCH, n_pages).astype(jnp.int32)
    c_prompt = nrm((BATCH, D_MODEL), 1.0)
    c_sample = nrm((DEC_BATCH, D_MODEL), 1.0)
    w_ada = nrm((DEPTH, D_MODEL, N_MOD * D_MODEL), 0.5 * D_MODEL ** -0.5)
    b_ada = nrm((DEPTH, N_MOD * D_MODEL), 0.02)
    g_pre = 1.0 + nrm((DEPTH, 3, D_MODEL), 0.02)
    g_post = 1.0 + nrm((DEPTH, 3, D_MODEL), 0.02)
    w_ffn_gate = nrm((DEPTH, 2, D_MODEL, D_FF), D_MODEL ** -0.5)
    w_ffn_up = nrm((DEPTH, 2, D_MODEL, D_FF), D_MODEL ** -0.5)
    w_ffn_down = nrm((DEPTH, 2, D_FF, D_MODEL), D_FF ** -0.5)
    w_in_even = nrm((N_EVEN, D_MODEL, P_EVEN), D_MODEL ** -0.5)
    w_out_even = nrm((N_EVEN, A_WIDTH + RET_WIDTH, D_MODEL), (A_WIDTH + RET_WIDTH) ** -0.5)
    w_in_odd = nrm((N_ODD, D_MODEL, 2 * D_RNN), D_MODEL ** -0.5)
    w_out_odd = nrm((N_ODD, D_RNN, D_MODEL), D_RNN ** -0.5)
    conv_w = nrm((N_ODD, CONV_W, D_RNN), 0.5)
    conv_b = nrm((N_ODD, D_RNN), 0.02)
    w_rg_a = nrm((N_ODD, RG_BLOCKS, RG_BLOCK_W, RG_BLOCK_W), RG_BLOCK_W ** -0.5)
    b_rg_a = nrm((N_ODD, D_RNN), 0.02)
    w_rg_x = nrm((N_ODD, RG_BLOCKS, RG_BLOCK_W, RG_BLOCK_W), RG_BLOCK_W ** -0.5)
    b_rg_x = nrm((N_ODD, D_RNN), 0.02)
    a0 = jax.random.uniform(next(it), (N_ODD, D_RNN), jnp.float32, minval=0.9, maxval=0.999)
    rg_lambda = jnp.log(a0) - jnp.log1p(-a0)
    return {'x_prompt': x_prompt, 'x_sample': x_sample, 'cache_k': cache_k, 'cache_v': cache_v,
            'cache_kidx': cache_kidx, 'state_ret': state_ret, 'state_conv': state_conv, 'state_rglru': state_rglru,
            'page_table': page_table, 'c_prompt': c_prompt, 'c_sample': c_sample, 'w_ada': w_ada, 'b_ada': b_ada,
            'g_pre': g_pre, 'g_post': g_post, 'w_ffn_gate': w_ffn_gate, 'w_ffn_up': w_ffn_up, 'w_ffn_down': w_ffn_down,
            'w_in_even': w_in_even, 'w_out_even': w_out_even, 'w_in_odd': w_in_odd, 'w_out_odd': w_out_odd,
            'conv_w': conv_w, 'conv_b': conv_b, 'w_rg_a': w_rg_a, 'b_rg_a': b_rg_a, 'w_rg_x': w_rg_x, 'b_rg_x': b_rg_x,
            'rg_lambda': rg_lambda}

def reference(x_prompt, x_sample, cache_k, cache_v, cache_kidx, state_ret, state_conv, state_rglru, page_table,
              c_prompt, c_sample, w_ada, b_ada, g_pre, g_post, w_ffn_gate, w_ffn_up, w_ffn_down,
              w_in_even, w_out_even, w_in_odd, w_out_odd, conv_w, conv_b, w_rg_a, b_rg_a, w_rg_x, b_rg_x, rg_lambda):
    p = {'w_ada': w_ada, 'b_ada': b_ada, 'g_pre': g_pre, 'g_post': g_post, 'w_ffn_gate': w_ffn_gate,
         'w_ffn_up': w_ffn_up, 'w_ffn_down': w_ffn_down, 'w_in_even': w_in_even, 'w_out_even': w_out_even,
         'w_in_odd': w_in_odd, 'w_out_odd': w_out_odd, 'conv_w': conv_w, 'conv_b': conv_b, 'w_rg_a': w_rg_a,
         'b_rg_a': b_rg_a, 'w_rg_x': w_rg_x, 'b_rg_x': b_rg_x, 'rg_lambda': rg_lambda}
    past_len = page_table.shape[1] * cache_k.shape[2]
    pos_prompt = jnp.arange(x_prompt.shape[1], dtype=jnp.int32)
    pos_sample = past_len + jnp.arange(x_sample.shape[1], dtype=jnp.int32)
    past = {'cache_k': cache_k, 'cache_v': cache_v, 'cache_kidx': cache_kidx, 'page_table': page_table,
            'state_ret': state_ret, 'state_conv': state_conv, 'state_rglru': state_rglru}
    y_prompt, st_p = trunk(x_prompt, c_prompt, pos_prompt, None, p)
    y_sample, st_s = trunk(x_sample, c_sample, pos_sample, past, p)
    k_p, v_p, ki_p, ret_p, conv_p, h_p = st_p
    k_s, v_s, ki_s, ret_s, conv_s, h_s = st_s
    return (y_prompt, y_sample, k_p, v_p, ki_p, ret_p, conv_p, h_p, k_s, v_s, ki_s, ret_s, conv_s, h_s)


_drawn_inputs = setup_inputs


def setup_inputs(seed=0):
    import zlib

    import numpy as np

    out = dict(_drawn_inputs(seed))
    spreads = {}
    factors = {'g_post': 4.597, 'b_rg_a': 8.0, 'b_rg_x': 7.733}
    for name, (base, spread) in spreads.items():
        noise = np.random.default_rng([zlib.crc32(name.encode()), seed]).standard_normal(out[name].shape)
        drawn = base * np.exp(spread * noise) if base else spread * noise
        out[name] = jnp.asarray(drawn.astype(out[name].dtype))
    for name, factor in factors.items():
        out[name] = (out[name] * factor).astype(out[name].dtype)
    return out
```

```python
from contextlib import ExitStack

import numpy as np
import concourse.bass as bass
from concourse import mybir

P = 128
F32 = mybir.dt.float32
F32R = mybir.dt.float32r
I32 = mybir.dt.int32
ALU = mybir.AluOpType
ACT = mybir.ActivationFunctionType
AX = mybir.AxisListType.X

D = 1024
KC = D // P
PTOK = 256
NB, NT = 8, 8
STOK = NB * NT
TOK = PTOK + STOK
NCOND = 1 + NB
FF = 2816
FC = FF // P
HFC = FC // 2
N_FFN = 4
NMOD = 9
ADA_COLS = 256
GROUPS = NMOD * D // ADA_COLS
CH_L = NMOD * KC
EPS = 1e-6
PAST = 256
PAGE = 128
N_PHYS = 20
HD = 64
NH, NKV = 8, 2
NR = NH // NKV
NIH = 4
RH = 4
TOPK_P = 64
TOPK_S = 66
KEYS_S = PAST + STOK
PAD_S = -TOPK_S % 8
NEG, TAKEN, WINS = -1.0e30, -3.0e38, 3.0e38
LN_G = [float(np.log1p(-(2.0 ** (-5.0 - h)))) for h in range(RH)]
CDEC_P = [float(np.exp(np.float32(128 * g))) for g in LN_G]
CDEC_S = [float(np.exp(np.float32(NT * g))) for g in LN_G]
CONVW = 4
XW = (PTOK + 3) + NB * (NT + 3)
GELU_SCALE = 2.0 * float(np.sqrt(2.0 / np.pi))

B_Q, B_K, B_QI, B_KI = 0, 4, 5, 7
B_RQK = 8
B_V, B_WI, B_RV, B_RG = 16, 17, 18, 22
EVEN_BLOCKS = 26

EVEN_IN_TILES = EVEN_BLOCKS // 2
OUT_TILES = KC // 2
ODD_IN_TILES = KC
W_BASE = {}
_n = 0
for _stage, _count in (("gate0", FC), ("down0", 2 * KC), ("even_in", EVEN_IN_TILES),
                       ("even_out", OUT_TILES), ("gate1", FC), ("down1", 2 * KC),
                       ("gate2", FC), ("down2", 2 * KC), ("odd_in", ODD_IN_TILES),
                       ("odd_out", OUT_TILES), ("gate3", FC), ("down3", 2 * KC)):
    W_BASE[_stage] = _n
    _n += _count
W_TILES = _n
A_FRONT = 8
A_BASE = {"gate0": 8, "down0": 30, "gate1": 38, "down1": 60, "down2": 68}
A_PER = {"gate0": 2, "down0": 2, "gate1": 2, "down1": 2, "down2": 1}
A_GROUPS = 2 * GROUPS
CR = 2


class Steps:

    def __init__(self, eng, sem):
        self.eng, self.sem, self.n, self.off = eng, sem, 0, 0

    def did(self, ins):
        ins.then_inc(self.sem, 1)
        self.n += 1
        return self.n

    def wait(self, at=None):
        self.eng.wait_ge(self.sem, self.off + (self.n if at is None else at))

    def body(self, i, per):
        self.off, self.start, self.per = i * per, self.n, per

    def end(self, count):
        assert self.n - self.start == self.per, (self.n - self.start, self.per)
        self.n, self.off = self.start + self.per * count, 0


def at(ap3, i):
    if isinstance(i, int):
        return ap3[:, i, :]
    return ap3[:, bass.ds(i, 1), :].rearrange("p o n -> p (o n)")


def at4(ap4, i):
    if isinstance(i, int):
        return ap4[:, i, :, :]
    return ap4[:, bass.ds(i, 1), :, :].rearrange("p o a b -> p (o a) b")


def row(ap3, i):
    if isinstance(i, int):
        return ap3[i]
    return ap3[bass.ds(i, 1), :, :].rearrange("o p n -> p (o n)")


def build(nc, t):
    with ExitStack() as ctx:
        sems = {}

        def sem(name):
            if name not in sems:
                sems[name] = ctx.enter_context(nc.semaphore(name))
            return sems[name]

        def sb(name, shape, dt=F32):
            return ctx.enter_context(nc.sbuf_tensor(name, shape, dt))

        under = ExitStack()
        rb = lambda name, shape, dt=F32: under.enter_context(nc.sbuf_tensor(name, shape, dt))
        st_in = rb("st_in", [P, NB, P])
        st_out = rb("st_out", [P, NB, P])
        kt = rb("kt", [P, 3, P])
        vt = rb("vt", [P, 3, P])
        qd = rb("qd", [P, P])
        qz = rb("qz", [P, NB * (STOK + NT)])
        am = rb("am", [P, 2, P])
        am_s = rb("am_s", [STOK, STOK])
        s1 = rb("s1", [P, P])
        s2 = rb("s2", [P, P])
        vm = rb("vm", [STOK, NB, P])
        under.close()
        under = ExitStack()
        rb2 = lambda name, shape, dt=F32: under.enter_context(nc.sbuf_tensor(name, shape, dt))
        lg = rb2("lg", [P, 2, NKV, KEYS_S])
        pT = rb2("pT", [P, 2, 6 * P])
        under.close()
        xn_hi = sb("xn_hi", [P, KC, TOK], F32R)
        xn_lo = sb("xn_lo", [P, KC, TOK], F32R)
        x = sb("x", [P, KC, TOK])
        f = sb("f", [P, KC, TOK])
        w_raw = sb("w_raw", [P, 2, 2048])
        w_hi = [sb(f"w_hi{s}", [P, 2048], F32R) for s in range(2)]
        w_lo = [sb(f"w_lo{s}", [P, 2048], F32R) for s in range(2)]
        a_raw = sb("a_raw", [P, 2, 1024])
        a_hi = [sb(f"a_hi{s}", [P, 1024], F32R) for s in range(2)]
        a_lo = [sb(f"a_lo{s}", [P, 1024], F32R) for s in range(2)]
        modT = sb("modT", [P, 2 * CH_L, NCOND])
        ada_row = sb("ada_row", [32 + 2 * NCOND, ADA_COLS])
        c2 = sb("c2", [P, KC, 2 * NCOND], F32R)
        b_ada = sb("b_ada", [P, 2 * CH_L])
        g_pre = sb("g_pre", [P, 6, KC])
        g_post = sb("g_post", [P, 6, KC])
        rstd = sb("rstd", [P, TOK])
        rtmp = sb("rtmp", [P, TOK])
        rrec = sb("rrec", [P, TOK])
        sqacc = sb("sqacc", [P, TOK])
        sq2 = sb("sq2", [P, 2, TOK])
        ident = sb("ident", [P, P])
        ones_d = sb("ones_d", [P, P])
        sel2 = sb("sel2", [32 + 2 * NCOND, 2 * NCOND])
        spl8 = sb("spl8", [P, KC])
        spl8n = sb("spl8n", [P, KC])
        pages = sb("pages", [1, 2 * NB], I32)
        cT = sb("cT", [P, KC, NCOND])
        cS = sb("cS", [P, KC, NCOND])
        lam = sb("lam", [P, KC])
        sp = [sb(f"sp{i}", [P, KC]) for i in range(5)]
        ps = ctx.enter_context(nc.psum_tensor("ps", [P, 8, 512], F32))
        B_ADA, B_MOD, B_STAT = 4, 5, 6

        def phase():
            stack = ExitStack()
            return stack, lambda name, shape, dt=F32: stack.enter_context(nc.sbuf_tensor(name, shape, dt))

        stack, pb = phase()
        mid_hi = pb("mid_hi", [P, FC, TOK], F32R)
        mid_lo = pb("mid_lo", [P, FC, TOK], F32R)
        sil = pb("sil", [P, 2, TOK])
        hbuf = pb("hbuf", [P, 2, TOK])
        stack.close()
        stack, pb = phase()
        sqx = pb("sqx", [P, KC, TOK])
        stack.close()
        stack, pb = phase()
        proj = pb("proj", [P, EVEN_BLOCKS, TOK])
        perm = pb("perm", [P, 2, P])
        kidxp = pb("kidxp", [P, NB, PAST])
        kpage = pb("kpage", [P, NB, PAST])
        vpage = pb("vpage", [P, NB, 2, P])
        bias_p = pb("bias_p", [P, 2, PTOK])
        bias_s = pb("bias_s", [STOK, KEYS_S])
        bias_r = pb("bias_r", [P, 2, KEYS_S])
        score_s = pb("score_s", [STOK, KEYS_S + PAD_S])
        rep_s = pb("rep_s", [STOK, 2, P])
        sel_s = pb("sel_s", [P, 2, STOK])
        hmask = pb("hmask", [P, NIH])
        qiz = pb("qiz", [P, NB, 4, NT])
        qsm = pb("qsm", [P, NB, NR, NT])
        wi_tok = pb("wi_tok", [P, 3, NIH])
        wis = pb("wis", [P, 2, NIH])
        wis1 = pb("wis1", [P, 2])
        vtok = pb("vtok", [P, 3, P])
        top8 = pb("top8", [P, 8])
        nmx = pb("nmx", [P, 2, NKV])
        sm = pb("sm", [P, 2, NKV])
        rsm = pb("rsm", [P, 2, NKV])
        qdec = pb("qdec", [P, RH, TOK])
        dec_p = pb("dec_p", [P, RH, P])
        dec_s = pb("dec_s", [STOK, RH, STOK])
        kdec = pb("kdec", [P, 2, RH])
        bmask = pb("bmask", [STOK, NB])
        ones_h = pb("ones_h", [P, P])
        stack.close()
        ropet, rope_a, rope_b = f[:, 0:4, :], f[:, 4:6, :], f[:, 6:8, :]
        relu_p = proj[:, B_RQK:B_RQK + 4, 0:PTOK]
        relu_s = proj[:, B_RQK + 4:B_RQK + 6, :]
        score_p = proj[:, B_RQK + 6:B_RQK + 8, 0:PTOK]
        stack, pb = phase()
        gate = pb("gate", [P, KC, TOK])
        conv = pb("conv", [P, KC, TOK])
        ra = pb("ra", [P, KC, TOK])
        ib = pb("ib", [P, KC, TOK])
        xc = pb("xc", [P, 2, XW])
        wrg = pb("wrg", [P, 2 * KC, P])
        cw = pb("cw", [P, KC, CONVW])
        cb = pb("cb", [P, KC, 1])
        cst = pb("cst", [P, KC, NB, 3])
        brg = pb("brg", [P, 2, KC])
        h0 = pb("h0", [P, KC, NB])
        tails = pb("tails", [P, KC, NCOND, 3])
        tah = pb("tah", [P, KC, NB])
        hlast = pb("hlast", [P, KC, NCOND])
        stack.close()
        gtmp = f

        w_landed = [[sem(f"w_landed{s}{h}") for h in range(2)] for s in range(2)]
        w_high = sem("w_high")
        w_split = sem("w_split")
        w_used = sem("w_used")
        a_landed = [sem(f"a_landed{s}") for s in range(2)]
        a_high, a_split, a_used = sem("a_high"), sem("a_split"), sem("a_used")
        row_ready = sem("row_ready")
        row_zero = sem("row_zero")
        sel_done = sem("sel_done")
        mod_ready = sem("mod_ready")
        coef_ready = sem("coef_ready")
        sil_ready = sem("sil_ready")
        gu_free = sem("gu_free")
        mid_high = sem("mid_high")
        mid_ready = sem("mid_ready")
        half_used = sem("half_used")
        sq_ready = sem("sq_ready")
        y_evac = sem("y_evac")
        stat_done, rec_ready, rstd_ready = sem("stat_done"), sem("rec_ready"), sem("rstd_ready")
        x_ready = sem("x_ready")
        sqx_ready = sem("sqx_ready")
        xr_ready = sem("xr_ready")
        xmod_ready = sem("xmod_ready")
        xn_high = sem("xn_high")
        xn_ready = sem("xn_ready")
        const_in = sem("const_in")
        c_in, c_silu, c_high, c_split = sem("c_in"), sem("c_silu"), sem("c_high"), sem("c_split")
        sp_e, sp_done = sem("sp_e"), sem("sp_done")
        lam_in = sem("lam_in")
        out_done = sem("out_done")
        dve_step = sem("dve_step")
        act_step = sem("act_step")

        SUB = {"down0": 0, "even_out": 1, "down1": 2, "down2": 3, "odd_out": 4, "down3": 5}
        PREP = {"gate0": 0, "even_in": 1, "even_out": 2, "gate1": 3, "gate2": 4, "odd_in": 5,
                "odd_out": 6, "gate3": 7}
        PNORM = {"gate0": 0, "even_in": 1, "gate1": 2, "gate2": 3, "odd_in": 4, "gate3": 5}

        def scale_at(sub, k):
            return CH_L * (sub // 3) + (3 * (sub % 3) + 1) * KC + k

        def shift_at(sub, k):
            return CH_L * (sub // 3) + (3 * (sub % 3)) * KC + k

        def gate_at(sub, k):
            return CH_L * (sub // 3) + (3 * (sub % 3) + 2) * KC + k

        def halves(width):
            return slice(0, 1024), slice(1024, width)

        DOWN_LOOPS = {0: ((0, 4, True),), 1: ((0, 4, True),), 2: ((0, 2, True), (2, 4, False)), 3: ((0, 4, False),)}

        def down_loops(eng, ff, body):
            if ff == 2:
                body(0, True)
                body(1, True)
                body(2, False)
            else:
                with eng.Fori(0, KC // 2 - 1) as i:
                    body(i, ff < 2)
            body(KC // 2 - 1, ff < 2, True)

        def per_sample(ap2):
            return ap2.unsqueeze(2).to_broadcast([P, NB, NT])

        def tokens(ap2):
            return ap2.rearrange("p (b t) -> p b t", b=NB)


        p_evac = sem("p_evac")
        rope_mm = sem("rope_mm")
        rope_done = sem("rope_done")
        perm_in, rope_in = sem("perm_in"), sem("rope_in")
        even_in_dma = sem("even_in_dma")
        PB = 4
        tr_k, tr_v = sem("tr_k"), sem("tr_v")
        kt_ready, vt_ready = sem("kt_ready"), sem("vt_ready")
        att_done, am_ready = sem("att_done"), sem("am_ready")
        kv_done, s1_ready = sem("kv_done"), sem("s1_ready")
        qd_ready, vm_ready = sem("qd_ready"), sem("vm_ready")
        st_landed, o_done, osq_ready = sem("st_landed"), sem("o_done"), sem("osq_ready")
        kvs_done, st_ready, s2_ready = sem("kvs_done"), sem("st_ready"), sem("s2_ready")
        st_stored = sem("st_stored")
        ret_in = sem("ret_in")
        ostat_done, orec_ready, orstd_ready = sem("ostat_done"), sem("orec_ready"), sem("orstd_ready")
        o_ready = sem("o_ready")
        vw_tr, vw_ready = sem("vw_tr"), sem("vw_ready")
        qiz_ready, wis_mm, wis_ready = sem("qiz_ready"), sem("wis_mm"), sem("wis_ready")
        ix_done, relu_ready, relu_used = sem("ix_done"), sem("relu_ready"), sem("relu_used")
        weighed, ixs_done, bias_ready = sem("weighed"), sem("ixs_done"), sem("bias_ready")
        rep_done, rep_ready = sem("rep_done"), sem("rep_ready")
        lg_done, lg_ready, exp_ready, pr_ready = sem("lg_done"), sem("lg_ready"), sem("exp_ready"), sem("pr_ready")
        pt_done, pt_ready, pv_done, pv_out = sem("pt_done"), sem("pt_ready"), sem("pv_done"), sem("pv_out")
        kvo_stored, rg_silu = sem("kvo_stored"), sem("rg_silu")
        EVEN_DMAS = 7 + 4 * 2 * NB
        RK = [B_RQK + 2 * h + 1 for h in range(RH)]
        RQ = [B_RQK + 2 * h for h in range(RH)]
        CHUNKS = ((0, P), (P, P), (PTOK, STOK))
        UNITS = [("p", qt, j) for qt in range(2) for j in range(NR)] + [("s", bh, 0) for bh in range(2)]

        def unit_keys(u):
            kind, a, _ = UNITS[u]
            return P * (a + 1) if kind == "p" else KEYS_S

        def unit_chunks(u):
            nk = unit_keys(u)
            return [(c, min(P, nk - P * c)) for c in range(-(-nk // P))]

        def gp_even(gp):
            gp.wait_ge(w_used, CR + W_BASE["even_in"])
            gp.dma_start(perm[:, :, :], t["perm"]).then_inc(perm_in, 16)
            for dst, src in ((bias_p[:, :, :], t["bias_p"]), (bias_s[:, :], t["bias_s"]),
                             (rep_s[:, :, :], t["rep_s"]), (sel_s[:, :, :], t["sel_s"]),
                             (hmask[:, :], t["hmask"]), (dec_p[:, :, :], t["dec_p"]),
                             (qdec[:, :, :], t["qdec"])):
                gp.dma_start(dst, src).then_inc(even_in_dma, 16)
            gp.dma_start(ones_h[:, :], t["ones_h"]).then_inc(perm_in, 16)
            gp.wait_ge(xn_ready, 8 * (PREP["even_in"] + 1))
            gp.dma_start(ropet, t["rope"]).then_inc(rope_in, 16)
            for b in range(NB):
                for pg in range(2):
                    page = gp.value_load(pages[0:1, 2 * b + pg:2 * b + pg + 1], min_val=0, max_val=N_PHYS - 1)
                    keys = slice(PAGE * pg, PAGE * (pg + 1))
                    for half in range(2):
                        gp.dma_start(kidxp[HD * half:HD * (half + 1), b, keys],
                                     row(t["kidx_pages"], page)).then_inc(even_in_dma, 16)
                    gp.dma_start(kpage[:, b, keys], row(t["k_pages"], page)).then_inc(even_in_dma, 16)
                    gp.dma_start(vpage[:, b, pg, :], row(t["v_pages"], page)).then_inc(even_in_dma, 16)
            gp.wait_ge(p_evac, PB + EVEN_BLOCKS)
            gp.wait_ge(rope_done, CR + 2 * 8)
            for dst, src in ((kdec[:, :, :], t["kdec"]), (bmask[:, :], t["bmask"]), (dec_s[:, :, :], t["dec_s"])):
                gp.dma_start(dst, src).then_inc(ret_in, 16)
            gp.dma_start(t["k_o"], proj[:, B_K, :]).then_inc(kvo_stored, 16)
            gp.dma_start(t["v_o"], proj[:, B_V, :]).then_inc(kvo_stored, 16)
            gp.dma_start(t["ki_o"], proj[0:HD, B_KI, :]).then_inc(kvo_stored, 16)
            for h in range(RH):
                if h:
                    gp.wait_ge(st_ready, h)
                gp.dma_start(st_in[:, :, :], t["state_ret"][:, h].rearrange("b d v -> d b v"))\
                  .then_inc(st_landed, 16)
                if h:
                    store_states(gp, h - 1)
            store_states(gp, RH - 1)

        def store_states(gp, h):
            gp.wait_ge(s2_ready, h + 1)
            gp.dma_start(t["ret_p"][h], s2[:, :]).then_inc(st_stored, 16)
            gp.wait_ge(st_ready, h + 1)
            gp.dma_start(t["ret_s"][:, h].rearrange("b d v -> d b v"), st_out[:, :, :]).then_inc(st_stored, 16)

        def pe_even(pe, three_passes, w_half):
            base = W_BASE["even_in"]

            def rotate(b, bank, kind):
                pe.wait_ge(p_evac, PB + b + 1)
                pe.wait_ge(rope_done, CR + b - 1)
                pe.matmul(ps[:, 4 + bank, 0:TOK], perm[:, kind, :], at(proj, b), start=True, stop=True)\
                  .then_inc(rope_mm, 1)

            def tile(i, j, first, kind):
                s = (base + j) % 2
                for h in range(2):
                    w_half(base + 2 * i + j, h)
                    b = 4 * i + 2 * j + h
                    pe.wait_ge(p_evac, PB + b - 3)
                    for k in range(KC):
                        if first and j == h == 0:
                            pe.wait_ge(xn_ready, 8 * PREP["even_in"] + k + 1)
                        last = three_passes(ps[:, (2 * j + h) % 4, 0:TOK], s, (h * KC + k) * P, xn_hi[:, k, :],
                                            xn_lo[:, k, :], k == 0, k == KC - 1)
                    last.then_inc(half_used if h == 0 else w_used, 1)
                    if kind is not None and 2 * j + h > 0:
                        rotate(b - 1, (h + 1) % 2, kind)
            pe.wait_ge(mod_ready, 1 + (A_BASE["down0"] + KC) // 2)
            pe.wait_ge(perm_in, 32)
            tile(0, 0, True, 0)
            tile(0, 1, False, 0)
            rotate(3, 1, 0)
            for kind, lo, hi in ((0, 1, 2), (1, 2, 4)):
                with pe.Fori(lo, hi) as i:
                    tile(i, 0, False, kind)
                    tile(i, 1, False, kind)
                    rotate(4 * i + 3, 1, kind)
            with pe.Fori(4, 6) as i:
                tile(i, 0, False, None)
                tile(i, 1, False, None)
            tile(6, 0, False, None)

            pe.wait_ge(p_evac, PB + EVEN_BLOCKS)
            pe.wait_ge(rope_done, CR + 16)
            for h in range(RH):
                rq, rk, rv = proj[:, RQ[h], :], proj[:, RK[h], :], proj[:, B_RV + h, :]
                if h:
                    pe.wait_ge(kt_ready, h)
                    pe.wait_ge(vt_ready, h)
                    pe.wait_ge(am_ready, h)
                for bank, src, done in ((0, rk, tr_k), (1, rv, tr_v)):
                    for c, (c0, n) in enumerate(CHUNKS):
                        last = pe.transpose(ps[0:n, bank, c * P:(c + 1) * P], src[:, c0:c0 + n], ident[:, :])
                    last.then_inc(done, 1)
                for c in range(2):
                    pe.matmul(ps[:, 2, c * P:(c + 1) * P], rk[:, c * P:(c + 1) * P], rq[:, c * P:(c + 1) * P],
                              start=True, stop=True)
                pe.matmul(ps[0:STOK, 2, PTOK:TOK], rk[:, PTOK:TOK], rq[:, PTOK:TOK], start=True, stop=True)\
                  .then_inc(att_done, 1)
                pe.wait_ge(kt_ready, h + 1)
                pe.wait_ge(vt_ready, h + 1)
                if h:
                    pe.wait_ge(s2_ready, h)
                for c in range(2):
                    last = pe.matmul(ps[:, 4, c * P:(c + 1) * P], kt[:, c, :], vt[:, c, :], start=True, stop=True)
                last.then_inc(kv_done, 1)
                pe.wait_ge(vm_ready, h + 1)
                if h:
                    pe.wait_ge(st_ready, h)
                for i in range(2):
                    last = pe.matmul(ps[:, 5 + i, :], kt[0:STOK, 2, :],
                                     vm[:, 4 * i:4 * i + 4, :].rearrange("p b v -> p (b v)"), start=True, stop=True)
                last.then_inc(kvs_done, 1)
                pe.wait_ge(am_ready, h + 1)
                if h:
                    pe.wait_ge(osq_ready, h)
                pe.matmul(ps[:, 3, 0:P], vt[:, 0, :], am[:, 0, :], start=True, stop=True)
                pe.matmul(ps[:, 3, P:2 * P], vt[:, 1, :], am[:, 1, :], start=True, stop=False)
                pe.wait_ge(s1_ready, h + 1)
                pe.wait_ge(qd_ready, h + 1)
                pe.matmul(ps[:, 3, P:2 * P], s1[:, :], qd[:, :], start=False, stop=True)
                pe.wait_ge(st_landed, 16 * (h + 1))
                for b in range(NB):
                    pe.matmul(ps[:, 3, PTOK:TOK], st_in[:, b, :], qz[:, STOK * b:STOK * (b + 1)],
                              start=(b == 0), stop=False)
                pe.matmul(ps[:, 3, PTOK:TOK], vt[0:STOK, 2, :], am_s[:, :], start=False, stop=True)\
                  .then_inc(o_done, 1)
            pe.wait_ge(osq_ready, RH)
            pe.wait_ge(perm_in, 32)
            for h in range(RH):
                last = pe.matmul(ps[:, h, 0:TOK], ones_h[:, :], proj[:, RQ[h], :], start=True, stop=True)
            last.then_inc(ostat_done, 1)

            pe.wait_ge(even_in_dma, 16 * EVEN_DMAS)
            pe.wait_ge(st_ready, RH)
            for c, (c0, n) in enumerate(CHUNKS):
                pe.transpose(ps[0:n, 7, NIH * c:NIH * (c + 1)], proj[0:NIH, B_WI, c0:c0 + n], ident[0:NIH, 0:NIH])
                last = pe.transpose(ps[0:n, 6, P * c:P * (c + 1)], proj[:, B_V, c0:c0 + n], ident[:, :])
            last.then_inc(vw_tr, 1)
            pe.wait_ge(vw_ready, 1)
            for bh in range(2):
                last = pe.matmul(ps[:, 5, NIH * bh:NIH * (bh + 1)], rep_s[:, bh, :], wi_tok[0:STOK, 2, :],
                                 start=True, stop=True)
            last.then_inc(wis_mm, 1)
            pe.wait_ge(orec_ready, 1)
            for qt in range(2):
                for h in range(NIH):
                    rows = slice(HD * (h % 2), HD * (h % 2 + 1))
                    if qt:
                        pe.wait_ge(relu_ready, h + 1)
                    pe.matmul(ps[:, h, 0:P * (qt + 1)], proj[rows, B_QI + h // 2, P * qt:P * (qt + 1)],
                              proj[rows, B_KI, 0:P * (qt + 1)], start=True, stop=True).then_inc(ix_done, 1)
            pe.wait_ge(qiz_ready, 1)
            for bh in range(2):
                pe.wait_ge(relu_ready, NIH + bh + 1)
                for b4 in range(4):
                    b = 4 * bh + b4
                    rows = slice(32 * b4, 32 * (b4 + 1))
                    qb = qiz[:, b, :, :].rearrange("p x t -> p (x t)")
                    pe.matmul(ps[rows, bh, 0:PAST], qb, kidxp[:, b, :], start=True, stop=True)
                    last = pe.matmul(ps[rows, bh, PAST:KEYS_S], qb, proj[:, B_KI, PTOK:TOK], start=True, stop=True)
                last.then_inc(ix_done, 1)
            pe.wait_ge(weighed, 1)
            for bh in range(2):
                last = pe.matmul(ps[0:STOK, 4, 0:KEYS_S], sel_s[:, bh, :], relu_s[:, bh, :],
                                 start=(bh == 0), stop=(bh == 1))
            last.then_inc(ixs_done, 1)
            pe.wait_ge(bias_ready, 3)
            pe.wait_ge(wis_ready, 1)
            for bh in range(2):
                last = pe.matmul(ps[:, 4 + bh, 0:KEYS_S], rep_s[:, bh, :], bias_s[:, :], start=True, stop=True)
            last.then_inc(rep_done, 1)

            def logits(u):
                kind, a, j = UNITS[u]
                bank = 2 * (u % 2)
                if u >= 2:
                    pe.wait_ge(lg_ready, u - 1)
                else:
                    pe.wait_ge(relu_ready, 2 * NIH + 2)
                for g in range(NKV):
                    rows = slice(HD * g, HD * (g + 1))
                    if kind == "p":
                        last = pe.matmul(ps[:, bank + g, 0:unit_keys(u)], proj[rows, B_Q + j, P * a:P * (a + 1)],
                                         proj[rows, B_K, 0:unit_keys(u)], start=True, stop=True)
                        continue
                    for b4 in range(4):
                        b = 4 * a + b4
                        out = slice(32 * b4, 32 * (b4 + 1))
                        qb = qsm[rows, b, :, :].rearrange("p r t -> p (r t)")
                        pe.matmul(ps[out, bank + g, 0:PAST], qb, kpage[rows, b, :], start=True, stop=True)
                        last = pe.matmul(ps[out, bank + g, PAST:KEYS_S], qb, proj[rows, B_K, PTOK:TOK],
                                         start=True, stop=True)
                last.then_inc(lg_done, 1)

            logits(0)
            pe.wait_ge(rep_ready, 1)
            for u in range(len(UNITS)):
                if u + 1 < len(UNITS):
                    logits(u + 1)
                kind, a, j = UNITS[u]
                pe.wait_ge(pr_ready, u + 1)
                if u:
                    pe.wait_ge(pt_ready, u)
                for c, n in unit_chunks(u):
                    for g in range(NKV):
                        col = (2 * c + g) * P
                        last = pe.transpose(ps[0:n, 4 + col // 512, col % 512:col % 512 + P],
                                            lg[:, u % 2, g, P * c:P * c + n], ident[:, :])
                last.then_inc(pt_done, 1)
                pe.wait_ge(pt_ready, u + 1)
                if u:
                    pe.wait_ge(pv_out, u if kind == "p" else 8)
                pt = pT[:, u % 2, :].rearrange("p (c g n) -> p c g n", c=3, g=NKV)
                chunks = unit_chunks(u)
                if kind == "p":
                    for g in range(NKV):
                        for c, n in chunks:
                            last = pe.matmul(ps[HD * g:HD * (g + 1), 6, 0:P], vtok[:, c, HD * g:HD * (g + 1)],
                                             pt[:, c, g, :], start=(c == 0), stop=(c == len(chunks) - 1))
                else:
                    for b4 in range(4):
                        b = 4 * a + b4
                        own = slice(32 * b4, 32 * (b4 + 1))
                        for c, n in chunks:
                            v = vpage[:, b, c, :] if c < 2 else vtok[0:STOK, 2, :]
                            last = pe.matmul(ps[:, 7, 64 * b:64 * (b + 1)], v, pt[0:n, c, :, own],
                                             start=(c == 0), stop=(c == 2))
                last.then_inc(pv_done, 1)

        def act_even(act, steps, split_w, n_half):
            base = W_BASE["even_in"]

            def tile(i, j, kind):
                n_half[0] = (base + j + 1) // 2 + i
                split_w(base + 2 * i + j + 1, (base + j + 1) % 2)
                for h in range(2):
                    b = 4 * i + 2 * j + h
                    if h == 0:
                        act.wait_ge(half_used, 2 * i + j + 1)
                    else:
                        act.wait_ge(w_used, CR + base + 2 * i + j + 1)
                    scale = float(np.float32(P ** -0.5)) if kind == 1 and h == 1 else 1.0
                    act.activation(at(proj, b), ps[:, 2 * j + h, 0:TOK], ACT.Copy, scale=scale).then_inc(p_evac, 1)

            act.sem_inc(p_evac, PB)
            for kind, lo, hi in ((0, 0, 2), (1, 2, 4), (None, 4, 6)):
                with act.Fori(lo, hi) as i:
                    tile(i, 0, kind)
                    tile(i, 1, kind)
            tile(6, 0, None)

            act.wait_ge(p_evac, PB + EVEN_BLOCKS)
            act.activation(proj[:, B_RG:B_RG + RH, :], proj[:, B_RG:B_RG + RH, :], ACT.Silu).then_inc(rg_silu, 1)
            act.wait_ge(ret_in, 16 * 3)
            for h in range(RH):
                act.wait_ge(tr_k, h + 1)
                if h:
                    act.wait_ge(kvs_done, h)
                act.activation(kt[:, 0:2, :], ps[:, 0, 0:2 * P].rearrange("p (c n) -> p c n", c=2), ACT.Copy,
                               scale=kdec[:, 0, h:h + 1])
                act.activation(kt[0:STOK, 2, :], ps[0:STOK, 0, 2 * P:3 * P], ACT.Copy,
                               scale=kdec[0:STOK, 1, h:h + 1]).then_inc(kt_ready, 1)
                act.wait_ge(kv_done, h + 1)
                if h:
                    act.wait_ge(s2_ready, h)
                act.activation(s1[:, :], ps[:, 4, 0:P], ACT.Copy).then_inc(s1_ready, 1)
                act.wait_ge(o_done, h + 1)
                act.activation(f[:, 4 + h, :], ps[:, 3, 0:TOK], ACT.Copy)
                act.activation(proj[:, RQ[h], :], ps[:, 3, 0:TOK], ACT.Square).then_inc(osq_ready, 1)
            act.wait_ge(orec_ready, 1)
            act.activation(proj[:, B_RQK:B_RQK + 8:2, :], proj[:, B_RQK + 1:B_RQK + 8:2, :], ACT.Sqrt)\
               .then_inc(orstd_ready, 1)

            act.wait_ge(vw_tr, 1)
            act.activation(wi_tok[:, 0:2, :], ps[:, 7, 0:2 * NIH].rearrange("p (c n) -> p c n", c=2), ACT.Copy,
                           scale=0.5)
            act.activation(wi_tok[0:STOK, 2, :], ps[0:STOK, 7, 2 * NIH:3 * NIH], ACT.Copy, scale=0.5)
            act.activation(vtok[:, 0:2, :], ps[:, 6, 0:2 * P].rearrange("p (c n) -> p c n", c=2), ACT.Copy)
            act.activation(vtok[0:STOK, 2, :], ps[0:STOK, 6, 2 * P:3 * P], ACT.Copy).then_inc(vw_ready, 1)
            act.wait_ge(o_ready, 1)
            for qt in range(2):
                for h in range(NIH):
                    act.wait_ge(ix_done, NIH * qt + h + 1)
                    if qt:
                        act.wait_ge(relu_used, h + 1)
                    act.activation(relu_p[:, h, 0:P * (qt + 1)], ps[:, h, 0:P * (qt + 1)], ACT.Relu,
                                   scale=HD ** -0.5).then_inc(relu_ready, 1)
            for bh in range(2):
                act.wait_ge(ix_done, 2 * NIH + bh + 1)
                act.activation(relu_s[:, bh, :], ps[:, bh, 0:KEYS_S], ACT.Relu, scale=HD ** -0.5)\
                   .then_inc(relu_ready, 1)
            act.wait_ge(rep_done, 1)
            act.activation(bias_r[:, :, :], ps[:, 4:6, 0:KEYS_S], ACT.Copy).then_inc(rep_ready, 1)
            for u in range(len(UNITS)):
                kind, a, j = UNITS[u]
                act.wait_ge(lg_ready, u + 1)
                for g in range(NKV):
                    row_ = lg[:, u % 2, g, 0:unit_keys(u)]
                    last = act.activation(row_, row_, ACT.Exp, bias=nmx[:, u % 2, g:g + 1],
                                          accum_out=sm[:, u % 2, g:g + 1])
                last.then_inc(exp_ready, 1)
                act.wait_ge(pt_done, u + 1)
                if u >= 2:
                    act.wait_ge(pv_done, u - 1)
                chunks = unit_chunks(u)
                wide = min(len(chunks), 2) * 2 * P
                if len(chunks) == 3:
                    act.activation(pT[:, u % 2, 0:4 * P], ps[:, 4, 0:4 * P], ACT.Copy)
                    act.activation(pT[0:STOK, u % 2, 4 * P:6 * P], ps[0:STOK, 5, 0:2 * P], ACT.Copy)\
                       .then_inc(pt_ready, 1)
                else:
                    act.activation(pT[:, u % 2, 0:wide], ps[:, 4, 0:wide], ACT.Copy).then_inc(pt_ready, 1)
            act.wait_ge(st_stored, 32 * RH)
            act.wait_ge(kvo_stored, 16 * 3)
            act.wait_ge(o_ready, 2)
            act.wait_ge(pv_done, len(UNITS))
            for k in range(KC):
                act.activation(xn_hi[:, k, :], f[:, k, :], ACT.Copy).then_inc(xn_high, 1)

        def dve_even(dve, steps, split_w):
            base = W_BASE["even_in"]

            def rotate(b, par, kind):
                dve.wait_ge(p_evac, PB + b + 1)
                src = at(proj, b)
                dve.tensor_tensor(rope_a[:, par, :], src, ropet[:, 2 * kind, :], ALU.mult)
                dve.wait_ge(rope_mm, b + 1)
                steps.did(dve.tensor_tensor(rope_b[:, par, :], ps[:, 4 + par, 0:TOK], ropet[:, 2 * kind + 1, :],
                                            ALU.mult))
                steps.wait()
                dve.tensor_tensor(src, rope_a[:, par, :], rope_b[:, par, :], ALU.add).then_inc(rope_done, 1)

            dve.sem_inc(rope_done, CR)
            dve.wait_ge(rope_in, 16)
            for kind, lo, hi in ((0, 0, 2), (1, 2, 4), (None, 4, 6)):
                with dve.Fori(lo, hi) as i:
                    if kind is not None:
                        steps.body(i - lo, 4)
                    for j in range(2):
                        split_w(base + 2 * i + j + 1, (base + j + 1) % 2)
                        if kind is not None:
                            for h in range(2):
                                rotate(4 * i + 2 * j + h, h, kind)
                if kind is not None:
                    steps.end(hi - lo)
            split_w(base + 13, (base + 13) % 2)

            dve.wait_ge(p_evac, PB + EVEN_BLOCKS)
            dve.wait_ge(rope_done, CR + 16)
            dve.wait_ge(ret_in, 16 * 3)
            dve.wait_ge(even_in_dma, 16 * EVEN_DMAS)
            steps.did(dve.memset(qz[:, :], 0.0))
            steps.wait()
            for h in range(RH):
                dve.wait_ge(tr_v, h + 1)
                if h:
                    dve.wait_ge(o_done, h)
                dve.tensor_copy(vt[:, 0:2, :], ps[:, 1, 0:2 * P].rearrange("p (c n) -> p c n", c=2))
                dve.tensor_copy(vt[0:STOK, 2, :], ps[0:STOK, 1, 2 * P:3 * P]).then_inc(vt_ready, 1)
                dve.tensor_tensor(qd[:, :], proj[:, RQ[h], P:2 * P], qdec[:, h, P:2 * P], ALU.mult)
                dve.tensor_tensor(qz[:, :].rearrange("p (b w) -> p b w", b=NB)[:, :, 0:NT],
                                  tokens(proj[:, RQ[h], PTOK:TOK]), tokens(qdec[:, h, PTOK:TOK]), ALU.mult)\
                   .then_inc(qd_ready, 1)
                dve.wait_ge(att_done, h + 1)
                dve.tensor_tensor(am[:, :, :], ps[:, 2, 0:2 * P].rearrange("p (c n) -> p c n", c=2),
                                  dec_p[:, h, :].unsqueeze(1).to_broadcast([P, 2, P]), ALU.mult)
                dve.tensor_tensor(am_s[:, :], ps[0:STOK, 2, PTOK:TOK], dec_s[:, h, :], ALU.mult)\
                   .then_inc(am_ready, 1)
                dve.wait_ge(vt_ready, h + 1)
                if h:
                    dve.wait_ge(kvs_done, h)
                dve.tensor_tensor(vm[:, :, :], vt[0:STOK, 2, :].unsqueeze(1).to_broadcast([STOK, NB, P]),
                                  bmask[:, :].unsqueeze(2).to_broadcast([STOK, NB, P]), ALU.mult)\
                   .then_inc(vm_ready, 1)
                dve.wait_ge(s1_ready, h + 1)
                if h:
                    dve.wait_ge(st_stored, 32 * h)
                dve.scalar_tensor_tensor(s2[:, :], s1[:, :], CDEC_P[h], ps[:, 4, P:2 * P], ALU.mult, ALU.add)\
                   .then_inc(s2_ready, 1)
                dve.wait_ge(kvs_done, h + 1)
                dve.wait_ge(st_landed, 16 * (h + 1))
                dve.wait_ge(o_done, h + 1)
                for i in range(2):
                    last = dve.scalar_tensor_tensor(st_out[:, 4 * i:4 * i + 4, :], st_in[:, 4 * i:4 * i + 4, :],
                                                    CDEC_S[h], ps[:, 5 + i, :].rearrange("p (b v) -> p b v", b=4),
                                                    ALU.mult, ALU.add)
                last.then_inc(st_ready, 1)
            dve.wait_ge(ostat_done, 1)
            steps.did(dve.tensor_scalar(proj[:, B_RQK:B_RQK + 8:2, :], ps[:, 0:4, 0:TOK], EPS, None, ALU.add))
            steps.wait()
            dve.reciprocal(proj[:, B_RQK + 1:B_RQK + 8:2, :], proj[:, B_RQK:B_RQK + 8:2, :]).then_inc(orec_ready, 1)
            steps.did(dve.memset(qiz[:, :, :, :], 0.0))
            dve.memset(score_s[:, KEYS_S:KEYS_S + PAD_S], WINS)
            steps.wait()
            for r in range(NR):
                dve.tensor_copy(qsm[:, :, r, :], tokens(proj[:, B_Q + r, PTOK:TOK]))
            for s in range(2):
                rows = slice(HD * s, HD * (s + 1))
                for c in range(2):
                    last = dve.tensor_copy(qiz[rows, :, 2 * s + c, :], tokens(proj[rows, B_QI + c, PTOK:TOK]))
            last.then_inc(qiz_ready, 1)
            dve.wait_ge(orstd_ready, 1)
            dve.wait_ge(rg_silu, 1)
            steps.did(dve.tensor_tensor(f[:, 4:8, :], f[:, 4:8, :], proj[:, B_RQK:B_RQK + 8:2, :], ALU.mult))
            steps.wait()
            dve.tensor_tensor(f[:, 4:8, :], f[:, 4:8, :], proj[:, B_RG:B_RG + RH, :], ALU.mult).then_inc(o_ready, 1)

            dve.wait_ge(wis_mm, 1)
            dve.wait_ge(vw_ready, 1)
            steps.did(dve.tensor_tensor(wis[:, :, :], ps[:, 5, 0:2 * NIH].rearrange("p (b h) -> p b h", b=2),
                                        hmask[:, :].unsqueeze(1).to_broadcast([P, 2, NIH]), ALU.mult))
            steps.wait()
            dve.reduce_sum(wis1[:, :], wis[:, :, :], axis=AX).then_inc(wis_ready, 1)
            dve.wait_ge(wis_ready, 1)

            def keep_top(work, bias, rounds):
                for r in range(rounds):
                    steps.did(dve.max(top8[0:work.shape[0], :], work))
                    steps.wait()
                    steps.did(dve.match_replace(work, top8[0:work.shape[0], :], work, TAKEN))
                    steps.wait()
                seen = work[:, 0:bias.shape[1]]
                steps.did(dve.tensor_scalar(seen, seen, -2.0e38, NEG, ALU.is_gt, ALU.mult))
                steps.wait()
                dve.tensor_tensor(bias, bias, seen, ALU.add).then_inc(bias_ready, 1)

            for qt in range(2):
                nk = P * (qt + 1)
                acc = score_p[:, qt, 0:nk]
                for h in range(NIH):
                    dve.wait_ge(relu_ready, NIH * qt + h + 1)
                    ins = dve.scalar_tensor_tensor(acc, relu_p[:, h, 0:nk], wi_tok[:, qt, h:h + 1],
                                                   bias_p[:, qt, 0:nk] if h == 0 else acc, ALU.mult, ALU.add)
                    ins.then_inc(relu_used, 1)
                    dve.wait_ge(relu_used, NIH * qt + h + 1)
                keep_top(acc, bias_p[:, qt, 0:nk], TOPK_P // 8)
            for bh in range(2):
                dve.wait_ge(relu_ready, 2 * NIH + bh + 1)
                last = dve.tensor_scalar(relu_s[:, bh, :], relu_s[:, bh, :], wis1[:, bh:bh + 1], None, ALU.mult)
            last.then_inc(weighed, 1)
            dve.wait_ge(ixs_done, 1)
            steps.did(dve.tensor_tensor(score_s[:, 0:KEYS_S], ps[0:STOK, 4, 0:KEYS_S], bias_s[:, :], ALU.add))
            steps.wait()
            keep_top(score_s[:, :], bias_s[:, :], (TOPK_S + PAD_S) // 8)

            def soft(u):
                kind, a, j = UNITS[u]
                nk = unit_keys(u)
                bank = 2 * (u % 2)
                bias = bias_p[:, a, 0:nk] if kind == "p" else bias_r[:, a, :]
                dve.wait_ge(lg_done, u + 1)
                if u >= 2:
                    dve.wait_ge(pt_done, u - 1)
                if u == len(UNITS) - 2:
                    dve.wait_ge(rep_ready, 1)
                steps.did(dve.scalar_tensor_tensor(lg[:, u % 2, :, 0:nk], ps[:, bank:bank + 2, 0:nk], HD ** -0.5,
                                                   bias.unsqueeze(1).to_broadcast([P, NKV, nk]), ALU.mult, ALU.add))
                steps.wait()
                dve.reduce_max(nmx[:, u % 2, :], lg[:, u % 2, :, 0:nk], axis=AX, negate=True).then_inc(lg_ready, 1)

            def leave(u):
                kind, a, j = UNITS[u]
                dve.wait_ge(pv_done, u + 1)
                if kind == "p":
                    dve.tensor_copy(f[:, j, P * a:P * (a + 1)], ps[:, 6, 0:P]).then_inc(pv_out, 1)
                elif a == 1:
                    for g in range(NKV):
                        rows = slice(HD * g, HD * (g + 1))
                        src = ps[rows, 7, :].rearrange("p (b g r t) -> p g b r t", b=NB, g=NKV, r=NR)
                        for r in range(NR):
                            last = dve.tensor_copy(tokens(f[rows, r, PTOK:TOK]), src[:, g, :, r, :])
                    last.then_inc(o_ready, 1)

            dve.wait_ge(st_stored, 32 * RH)
            dve.wait_ge(bias_ready, 3)
            soft(0)
            for u in range(len(UNITS)):
                if u + 1 < len(UNITS):
                    soft(u + 1)
                nk = unit_keys(u)
                dve.wait_ge(exp_ready, u + 1)
                steps.did(dve.reciprocal(rsm[:, u % 2, :], sm[:, u % 2, :]))
                steps.wait()
                for g in range(NKV):
                    last = dve.tensor_scalar(lg[:, u % 2, g, 0:nk], lg[:, u % 2, g, 0:nk], rsm[:, u % 2, g:g + 1],
                                             None, ALU.mult)
                last.then_inc(pr_ready, 1)
                if u:
                    leave(u - 1)
            leave(len(UNITS) - 1)
            for k in range(KC):
                dve.wait_ge(xn_high, 8 * PREP["even_out"] + k + 1)
                dve.tensor_tensor(xn_lo[:, k, :], f[:, k, :], xn_hi[:, k, :].bitcast(F32), ALU.subtract)\
                   .then_inc(xn_ready, 1)

        odd_in_dma = sem("odd_in_dma")
        xc_ready = sem("xc_ready")
        conv_ready = sem("conv_ready")
        rg_done, rg_act = sem("rg_done"), sem("rg_act")
        tanh_ready, aa_ready = sem("tanh_ready"), sem("aa_ready")
        m2_ready, mult_ready, b_ready = sem("m2_ready"), sem("mult_ready"), sem("b_ready")
        gelu_ready, y_ready, odd_stored = sem("gelu_ready"), sem("y_ready"), sem("odd_stored")
        tails_ready, hl_ready = sem("tails_ready"), sem("hl_ready")

        def gp_odd(gp):
            gp.wait_ge(w_used, CR + W_BASE["odd_in"])
            for dst, src in ((cst[:, :, :, :], t["conv_state"]), (cw[:, :, :], t["conv_w"]), (cb[:, :, :], t["conv_b"]),
                             (brg[:, :, :], t["b_rg"]), (h0[:, :, :], t["h0"]), (wrg[:, :, :], t["w_rg"])):
                gp.dma_start(dst, src).then_inc(odd_in_dma, 16)
            gp.wait_ge(tails_ready, 1)
            gp.dma_start(t["tails"], tails[:, :, :, :]).then_inc(odd_stored, 16)
            gp.wait_ge(hl_ready, 1)
            gp.dma_start(t["hlast"], hlast[:, :, :]).then_inc(odd_stored, 16)
            gp.wait_ge(odd_stored, 32)

        def pe_odd(pe, three_passes, w_half):
            base = W_BASE["odd_in"]

            def tile(i, j, first=False):
                s = (base + j) % 2
                c = 2 * i + j
                pe.wait_ge(xc_ready, CR + c - 1)
                for h in range(2):
                    w_half(base + c, h)
                    for k in range(KC):
                        if first and h == 0:
                            pe.wait_ge(xn_ready, 8 * PREP["odd_in"] + k + 1)
                        last = three_passes(ps[:, 2 * j + h, 0:TOK], s, (h * KC + k) * P, xn_hi[:, k, :],
                                            xn_lo[:, k, :], k == 0, k == KC - 1)
                    last.then_inc(half_used if h == 0 else w_used, 1)
            tile(0, 0, True)
            tile(0, 1)
            with pe.Fori(1, KC // 2) as i:
                tile(i, 0)
                tile(i, 1)
            pe.wait_ge(odd_in_dma, 16 * 6)
            for c in range(KC):
                pe.wait_ge(conv_ready, CR + c + 1)
                for h in range(2):
                    n = 2 * c + h
                    if n >= 4:
                        pe.wait_ge(rg_act, n - 3)
                    pe.matmul(ps[:, 4 + n % 4, 0:TOK], wrg[:, KC * h + c, :], conv[:, c, :], start=True, stop=True)\
                      .then_inc(rg_done, 1)

        def act_odd(act, steps, split_w, n_half):
            base = W_BASE["odd_in"]
            act.sem_inc(xc_ready, CR)
            act.wait_ge(odd_in_dma, 16 * 6)
            with act.Fori(0, KC // 2) as i:
                for j in range(2):
                    c = 2 * i + j
                    n_half[0] = (base + j + 1) // 2 + i
                    split_w(base + c + 1, (base + j + 1) % 2)
                    act.wait_ge(half_used, EVEN_IN_TILES + OUT_TILES + c + 1)
                    act.activation(at(gate, c), ps[:, 2 * j, 0:TOK], ACT.Copy)
                    act.wait_ge(w_used, CR + base + c + 1)
                    act.wait_ge(conv_ready, CR + c - 1)
                    act.activation(xc[:, j, 3:3 + PTOK], ps[:, 2 * j + 1, 0:PTOK], ACT.Copy)
                    act.activation(xc[:, j, PTOK + 3:XW].rearrange("p (b t) -> p b t", b=NB)[:, :, 3:3 + NT],
                                   ps[:, 2 * j + 1, PTOK:TOK].rearrange("p (b t) -> p b t", b=NB), ACT.Copy)\
                       .then_inc(xc_ready, 1)
            for c in range(KC):
                for h, dst in ((0, ra), (1, ib)):
                    act.wait_ge(rg_done, 2 * c + h + 1)
                    act.activation(dst[:, c, :], ps[:, 4 + (2 * c + h) % 4, 0:TOK], ACT.Sigmoid,
                                   bias=brg[:, h, c:c + 1]).then_inc(rg_act, 1)
            act.wait_ge(sp_done, 1)
            act.wait_ge(rg_act, 2 * KC)
            for c in range(KC):
                steps.did(act.activation(gtmp[:, c, :], ra[:, c, :], ACT.Tanh, scale=spl8n[:, c:c + 1]))
                steps.wait()
                act.activation(ra[:, c, :], ra[:, c, :], ACT.Exp, scale=spl8[:, c:c + 1]).then_inc(aa_ready, 1)
            for c in range(KC):
                act.wait_ge(m2_ready, c + 1)
                act.activation(gtmp[:, c, :], gtmp[:, c, :], ACT.Sqrt).then_inc(mult_ready, 1)
            for c in range(KC):
                act.activation(gate[:, c, :], gate[:, c, :], ACT.Gelu_apprx_tanh).then_inc(gelu_ready, 1)
            for k in range(KC):
                act.wait_ge(y_ready, k + 1)
                act.activation(xn_hi[:, k, :], f[:, k, :], ACT.Copy).then_inc(xn_high, 1)

        def dve_odd(dve, steps, split_w):
            base = W_BASE["odd_in"]
            dve.sem_inc(conv_ready, CR)
            dve.wait_ge(odd_in_dma, 16 * 6)
            for j in range(2):
                steps.did(dve.memset(xc[:, j, 0:3], 0.0))
            steps.wait()
            with dve.Fori(0, KC // 2) as i:
                steps.body(i, 2 * 6)
                for j in range(2):
                    c = 2 * i + j
                    split_w(base + c + 1, (base + j + 1) % 2)
                    seqs = xc[:, j, PTOK + 3:XW].rearrange("p (b t) -> p b t", b=NB)
                    steps.did(dve.tensor_copy(seqs[:, :, 0:3], at4(cst, c)))
                    dve.wait_ge(xc_ready, CR + c + 1)
                    steps.wait()
                    dst_p = at(conv, c)[:, 0:PTOK]
                    dst_s = at(conv, c)[:, PTOK:TOK].rearrange("p (b t) -> p b t", b=NB)
                    for tap in range(CONVW):
                        wt = at(cw, c)[:, tap:tap + 1]
                        src_p, src_s = xc[:, j, tap:tap + PTOK], seqs[:, :, tap:tap + NT]
                        if tap == 0:
                            bias = at(cb, c)
                            dve.tensor_scalar(dst_p, src_p, wt, bias, ALU.mult, ALU.add)
                            steps.did(dve.tensor_scalar(dst_s, src_s, wt, bias, ALU.mult, ALU.add))
                        else:
                            steps.wait()
                            dve.scalar_tensor_tensor(dst_p, src_p, wt, dst_p, ALU.mult, ALU.add)
                            steps.did(dve.scalar_tensor_tensor(dst_s, src_s, wt, dst_s, ALU.mult, ALU.add))
                    tl = at4(tails, c)
                    steps.did(dve.tensor_copy(tl[:, 0, :], xc[:, j, PTOK:PTOK + 3]))
                    dve.tensor_copy(tl[:, 1:NCOND, :], seqs[:, :, NT:NT + 3]).then_inc(conv_ready, 1)
            steps.end(KC // 2)
            dve.wait_ge(conv_ready, CR + KC)
            dve.sem_inc(tails_ready, 1)
            for c in range(KC):
                dve.wait_ge(rg_act, 2 * c + 2)
                steps.did(dve.tensor_tensor(ib[:, c, :], ib[:, c, :], conv[:, c, :], ALU.mult))
            for c in range(KC):
                dve.wait_ge(aa_ready, c + 1)
                if c == 0:
                    steps.wait()
                steps.did(dve.tensor_tensor(conv[:, c, :], ra[:, c, :], ra[:, c, :], ALU.mult))
                steps.wait()
                dve.scalar_tensor_tensor(gtmp[:, c, :], conv[:, c, :], 1.0, gtmp[:, c, :], ALU.add, ALU.mult)\
                   .then_inc(m2_ready, 1)
            first = lambda buf: buf[:, :, PTOK:TOK].rearrange("p c (b t) -> p c b t", b=NB)[:, :, :, 0]
            dve.wait_ge(mult_ready, KC)
            steps.did(dve.memset(gtmp[:, :, 0:1], 1.0))
            steps.did(dve.tensor_tensor(tah[:, :, :], first(ra), h0[:, :, :], ALU.mult))
            steps.wait()
            for c in range(KC):
                last = steps.did(dve.tensor_tensor(ib[:, c, :], ib[:, c, :], gtmp[:, c, :], ALU.mult))
            steps.wait()
            dve.memset(first(ra), 0.0)
            dve.memset(ra[:, :, 0:1], 0.0)
            steps.did(dve.tensor_tensor(first(ib), first(ib), tah[:, :, :], ALU.add))
            steps.wait()
            flat = lambda buf: buf[:, :, :].rearrange("p c n -> p (c n)")
            steps.did(dve.tensor_tensor_scan(flat(conv), flat(ra), flat(ib), 0.0, ALU.mult, ALU.add))
            steps.wait()
            for c in range(KC):
                dve.wait_ge(gelu_ready, c + 1)
                dve.tensor_tensor(f[:, c, :], conv[:, c, :], gate[:, c, :], ALU.mult).then_inc(y_ready, 1)
            dve.tensor_copy(hlast[:, :, 0:1], conv[:, :, PTOK - 1:PTOK])
            dve.tensor_copy(hlast[:, :, 1:NCOND], conv[:, :, PTOK:TOK].rearrange("p c (b t) -> p c b t", b=NB)[:, :, :, NT - 1])\
               .then_inc(hl_ready, 1)
            for k in range(KC):
                dve.wait_ge(xn_high, 8 * PREP["odd_out"] + k + 1)
                dve.tensor_tensor(xn_lo[:, k, :], f[:, k, :], xn_hi[:, k, :].bitcast(F32), ALU.subtract)\
                   .then_inc(xn_ready, 1)

        block = ctx.enter_context(nc.Block())

        @block.sync
        def _(sp_):
            def load_w(src, tile, n, width=2048):
                s = slot(n)
                for h, cols in enumerate(halves(width)):
                    if not (isinstance(n, int) and n < 2):
                        sp_.wait_ge(w_split, CR + 2 * n + h - 3)
                    sp_.dma_start(w_raw[:, s, cols], row(src, tile)[:, cols]).then_inc(w_landed[s][h], 16)

            def load_a(g):
                for h in range(2):
                    if not (isinstance(g, int) and g < 1):
                        sp_.wait_ge(a_split, CR + 2 * g + h - 1)
                    sp_.dma_start(a_raw[:, h, :], row(t["ada"], 2 * g + h)).then_inc(a_landed[h], 16)

            def slot(n):
                return n % 2 if isinstance(n, int) else n_slot[0]

            n_slot = [0]

            def at_slot(s):
                n_slot[0] = s

            sp_.dma_start(cT[:, :, :], t["cT"].rearrange("k p c -> p k c")).then_inc(c_in, 16)
            load_a(0)
            for dst, src in ((b_ada[:, :], t["b_ada"]), (g_pre[:, :, :], t["g_pre"]),
                             (g_post[:, :, :], t["g_post"]), (ident[:, :], t["ident"]),
                             (ones_d[:, :], t["ones_d"]), (sel2[:, :], t["sel2"]),
                             (pages[:, :], t["pages"])):
                sp_.dma_start(dst, src).then_inc(const_in, 16)
            sp_.dma_start(x[:, :, :], t["x"].rearrange("k p n -> p k n")).then_inc(const_in, 16)
            sp_.dma_start(lam[:, :], t["lam"]).then_inc(lam_in, 16)
            with sp_.Fori(1, A_FRONT) as g:
                load_a(g)

            def gate_loads(ff):
                stage = f"gate{ff}"
                for first, lo, hi in ((True, 0, 1), (False, 1, HFC)):
                    def body(i):
                        for j in range(2):
                            at_slot((W_BASE[stage] + j) % 2)
                            load_w(t["gu"], FC * ff + 2 * i + j, W_BASE[stage] + 2 * i + j)
                            if stage in A_BASE and not (ff == 1 and first and j == 0):
                                load_a(A_BASE[stage] + 2 * i + j)
                    if first:
                        body(0)
                    else:
                        with sp_.Fori(lo, hi) as i:
                            body(i)

            def down_loads(ff):
                stage = f"down{ff}"

                for lo, hi, ada in DOWN_LOOPS[ff]:
                    def body(i, first=False):
                        for m in range(2):
                            for h in range(2):
                                j = 2 * m + h
                                at_slot((W_BASE[stage] + j) % 2)
                                load_w(t["down"], 2 * KC * ff + 4 * i + j, W_BASE[stage] + 4 * i + j, HFC * P)
                            if ada and not (first and m == 0):
                                load_a(A_BASE[stage] + 2 * i + m)
                    if lo == 0 and stage == "down2":
                        body(0, True)
                        lo = 1
                    with sp_.Fori(lo, hi) as i:
                        body(i)
                if stage == "down0":
                    load_a(A_BASE["gate1"])
                elif stage == "down1":
                    load_a(A_BASE["down2"])

            def proj_loads(stage, first_tile, count):
                with sp_.Fori(0, count // 2) as i:
                    for j in range(2):
                        at_slot((W_BASE[stage] + j) % 2)
                        load_w(t["pj"], first_tile + 2 * i + j, W_BASE[stage] + 2 * i + j)
                if count % 2:
                    load_w(t["pj"], first_tile + count - 1, W_BASE[stage] + count - 1)

            gate_loads(0)
            down_loads(0)
            proj_loads("even_in", 0, EVEN_IN_TILES)
            proj_loads("even_out", EVEN_IN_TILES, OUT_TILES)
            gate_loads(1)
            down_loads(1)
            gate_loads(2)
            down_loads(2)
            proj_loads("odd_in", EVEN_IN_TILES + OUT_TILES, ODD_IN_TILES)
            proj_loads("odd_out", EVEN_IN_TILES + OUT_TILES + ODD_IN_TILES, OUT_TILES)
            gate_loads(3)
            down_loads(3)
            sp_.wait_ge(x_ready, 8 * 6)
            sp_.dma_start(t["y"].rearrange("k p n -> p k n"), x[:, :, :]).then_inc(out_done, 16)
            sp_.wait_ge(out_done, 16)

        @block.tensor
        def _(pe):
            def three_passes(out, s, w_at, xhi, xlo, start, stop):
                hi = w_hi[s][:, w_at:w_at + P]
                pe.matmul(out, hi, xhi, start=start, stop=False)
                pe.matmul(out, hi, xlo, start=False, stop=False)
                return pe.matmul(out, w_lo[s][:, w_at:w_at + P], xhi, start=False, stop=stop)

            def w_half(n, h):
                pe.wait_ge(w_split, CR + 2 * n + h + 1)

            def ada_product(g):
                pe.wait_ge(row_ready, 1 + g)
                for h in range(2):
                    pe.wait_ge(a_split, CR + 2 * g + h + 1)
                    for k in range(KC // 2):
                        for w in (a_hi, a_lo):
                            last = pe.matmul(ps[0:2 * NCOND, B_ADA, 0:ADA_COLS], c2[:, KC // 2 * h + k, :],
                                             w[h][:, k * ADA_COLS:(k + 1) * ADA_COLS],
                                             start=(h == k == 0 and w is a_hi),
                                             stop=(h == 1 and k == KC // 2 - 1 and w is a_lo))
                    last.then_inc(a_used, 1)

            def ada_transpose(q):
                pe.wait_ge(row_ready, 1 + 2 * q + 2)
                pe.wait_ge(mod_ready, 1 + q)
                for c in range(2):
                    last = pe.matmul(ps[:, B_MOD, 2 * c * NCOND:2 * (c + 1) * NCOND],
                                     ada_row[:, c * P:(c + 1) * P], sel2[:, :], start=True, stop=True)
                last.then_inc(sel_done, 1)

            def stat_x(prep):
                s = PNORM[prep]
                for k in range(KC):
                    pe.wait_ge(sqx_ready, 8 * s + k + 1)
                    last = pe.matmul(ps[:, B_STAT, 0:TOK], ones_d[:, :], sqx[:, k, :],
                                     start=(k == 0), stop=(k == KC - 1))
                last.then_inc(stat_done, 1)

            def stat_y(stage):
                pe.wait_ge(y_evac, CR + 8 * (SUB[stage] + 1))
                pe.matmul(ps[:, B_STAT, 0:TOK], ones_d[:, :], sqacc[:, :], start=True, stop=True)\
                  .then_inc(stat_done, 1)

            def gate_up(ff):
                stage = f"gate{ff}"

                def body(i, first=False):
                    for j in range(2):
                        n, p, s = W_BASE[stage] + 2 * i + j, FC * ff + 2 * i + j, (W_BASE[stage] + j) % 2
                        if stage in A_BASE:
                            ada_product(A_BASE[stage] + 2 * i + j)
                        pe.wait_ge(gu_free, CR + p - 1)
                        for b in range(2):
                            w_half(n, b)
                            for k in range(KC):
                                if first and j == b == 0:
                                    pe.wait_ge(xn_ready, 8 * PREP[stage] + k + 1)
                                last = three_passes(ps[:, 2 * j + b, 0:TOK], s, (b * KC + k) * P,
                                                    xn_hi[:, k, :], xn_lo[:, k, :], k == 0, k == KC - 1)
                        last.then_inc(w_used, 1)
                    if stage in A_BASE:
                        ada_transpose(A_BASE[stage] // 2 + i)

                body(0, True)
                with pe.Fori(1, HFC) as i:
                    body(i)

            def down(ff):
                stage = f"down{ff}"
                pe.wait_ge(mid_ready, FC * (ff + 1))
                for lo, hi, ada in DOWN_LOOPS[ff]:
                    with pe.Fori(lo, hi) as i:
                        for m in range(2):
                            q = 8 * SUB[stage] + 2 * i + m
                            if ada:
                                ada_product(A_BASE[stage] + 2 * i + m)
                            pe.wait_ge(y_evac, CR + q - 1)
                            for h in range(2):
                                j = 2 * m + h
                                s, n = (W_BASE[stage] + j) % 2, W_BASE[stage] + 4 * i + j
                                for k in range(HFC):
                                    if k in (0, KC):
                                        w_half(n, k // KC)
                                    c = HFC * h + k
                                    last = three_passes(ps[:, m, 0:TOK], s, k * P, mid_hi[:, c, :],
                                                        mid_lo[:, c, :], c == 0, c == FC - 1)
                                last.then_inc(w_used, 1)
                        if ada:
                            ada_transpose(A_BASE[stage] // 2 + i)

            def out_projection(stage):
                def body(i, first=False):
                    for j in range(2):
                        s = (W_BASE[stage] + j) % 2
                        for b in range(2):
                            w_half(W_BASE[stage] + 2 * i + j, b)
                            q = 8 * SUB[stage] + 4 * i + 2 * j + b
                            pe.wait_ge(y_evac, CR + q - 1)
                            for k in range(KC):
                                if first and j == b == 0:
                                    pe.wait_ge(xn_ready, 8 * PREP[stage] + k + 1)
                                last = three_passes(ps[:, b, 0:TOK], s, (b * KC + k) * P, xn_hi[:, k, :],
                                                    xn_lo[:, k, :], k == 0, k == KC - 1)
                            last.then_inc(half_used if b == 0 else w_used, 1)

                body(0, True)
                with pe.Fori(1, 2) as i:
                    body(i)

            for s_, v in ((w_used, CR), (a_used, CR), (sel_done, 1)):
                pe.sem_inc(s_, v)
            pe.wait_ge(const_in, 16 * 8)
            pe.wait_ge(c_split, 1)
            pe.wait_ge(row_zero, 1)
            with pe.Fori(0, A_FRONT // 2) as q:
                for j in range(2):
                    ada_product(2 * q + j)
                ada_transpose(q)
            stat_x("gate0")
            gate_up(0)
            down(0)
            stat_y("down0")
            stat_x("even_in")
            pe_even(pe, three_passes, w_half)
            out_projection("even_out")
            stat_y("even_out")
            stat_x("gate1")
            gate_up(1)
            down(1)
            stat_y("down1")
            stat_x("gate2")
            gate_up(2)
            down(2)
            stat_y("down2")
            stat_x("odd_in")
            pe_odd(pe, three_passes, w_half)
            out_projection("odd_out")
            stat_y("odd_out")
            stat_x("gate3")
            gate_up(3)
            down(3)
            stat_y("down3")

        @block.scalar
        def _(act):
            def split_w(n, s, width=2048):
                act.wait_ge(w_used, CR + n - 1)
                for h, cols in enumerate(halves(width)):
                    act.wait_ge(w_landed[s][h], 16 * (half_of(n) + 1))
                    act.activation(w_hi[s][:, cols], w_raw[:, s, cols], ACT.Copy).then_inc(w_high, 1)

            def half_of(n):
                return n // 2 if isinstance(n, int) else n_half[0]

            n_half = [0]

            def split_a(g):
                for h in range(2):
                    act.wait_ge(a_landed[h], 16 * (g + 1))
                    act.wait_ge(a_used, CR + 2 * g + h - 1)
                    act.activation(a_hi[h][:, :], a_raw[:, h, :], ACT.Copy).then_inc(a_high, 1)

            def ada_copy(q, j):
                act.wait_ge(a_used, CR + 4 * q + 2 * j + 2)
                if j == 0:
                    act.wait_ge(sel_done, 1 + q)
                act.activation(ada_row[32 * j:32 * j + 2 * NCOND, :], ps[0:2 * NCOND, B_ADA, 0:ADA_COLS],
                               ACT.Copy).then_inc(row_ready, 1)

            def root(s):
                act.wait_ge(rec_ready, s)
                act.activation(rstd[:, :], rrec[:, :], ACT.Sqrt).then_inc(rstd_ready, 1)

            def squares_x(prep):
                s = PNORM[prep]
                for k in range(KC):
                    if s:
                        act.wait_ge(x_ready, 8 * (s - 1) + k + 1)
                    act.activation(sqx[:, k, :], x[:, k, :], ACT.Square).then_inc(sqx_ready, 1)

            def modulate(prep):
                j, sub = PREP[prep], PNORM[prep]
                act.wait_ge(coef_ready, 2 * sub + 1)
                for k in range(KC):
                    act.wait_ge(xr_ready, 8 * sub + k + 1)
                    steps.did(act.activation(f[:, k, 0:PTOK], f[:, k, 0:PTOK], ACT.Identity,
                                             scale=modT[:, scale_at(sub, k), 0:1],
                                             bias=modT[:, shift_at(sub, k), 0:1]))
                    steps.wait()
                    act.wait_ge(xmod_ready, 8 * sub + k + 1)
                    act.activation(xn_hi[:, k, :], f[:, k, :], ACT.Copy).then_inc(xn_high, 1)

            def gate_up(ff):
                stage = f"gate{ff}"
                with act.Fori(0, HFC) as i:
                    for j in range(2):
                        n, p = W_BASE[stage] + 2 * i + j, FC * ff + 2 * i + j
                        n_half[0] = (W_BASE[stage] + j + 1) // 2 + i
                        split_w(n + 1, (W_BASE[stage] + j + 1) % 2)
                        if stage in A_BASE:
                            ada_copy(A_BASE[stage] // 2 + i, j)
                        if stage in A_BASE:
                            split_a(A_BASE[stage] + 2 * i + j + 1)
                        act.wait_ge(w_used, CR + n + 1)
                        act.wait_ge(gu_free, CR + p - 1)
                        act.activation(sil[:, j, :], ps[:, 2 * j, 0:TOK], ACT.Silu).then_inc(sil_ready, 1)
                        act.wait_ge(gu_free, CR + p + 1)
                        act.activation(at(mid_hi, 2 * i + j), hbuf[:, j, :], ACT.Copy).then_inc(mid_high, 1)

            def leave(stage, q, b, m):
                act.wait_ge(y_evac, CR + q - 1)
                act.activation(at(f, m)[:, 0:PTOK], ps[:, b, 0:PTOK], ACT.Copy,
                               scale=gate_of(stage, m)[:, 0:1])
                act.activation(sq2[:, b, :], ps[:, b, 0:TOK], ACT.Square).then_inc(sq_ready, 1)

            def gate_of(stage, m):
                return at(modT, gate_at(SUB[stage], 0) + m)

            def down(ff):
                stage = f"down{ff}"
                act.wait_ge(coef_ready, 2 * SUB[stage] + 2)

                def body(i, ada, last=False):
                    for m in range(2):
                        for h in range(2):
                            j = 2 * m + h
                            if not (last and ff == N_FFN - 1 and j == 3):
                                n_half[0] = (W_BASE[stage] + j + 1) // 2 + 2 * i
                                split_w(W_BASE[stage] + 4 * i + j + 1, (W_BASE[stage] + j + 1) % 2,
                                        2048 if last and j == 3 else HFC * P)
                        if ada:
                            ada_copy(A_BASE[stage] // 2 + i, m)
                            if not (stage == "down2" and i == 1 and m == 1):
                                split_a(A_BASE[stage] + 2 * i + m + 1)
                        act.wait_ge(w_used, CR + W_BASE[stage] + 4 * i + 2 * m + 2)
                        leave(stage, 8 * SUB[stage] + 2 * i + m, m, 2 * i + m)

                down_loops(act, ff, body)

            def out_projection(stage, done):
                act.wait_ge(coef_ready, 2 * SUB[stage] + 2)
                with act.Fori(0, 2) as i:
                    for j in range(2):
                        n_half[0] = (W_BASE[stage] + j + 1) // 2 + i
                        split_w(W_BASE[stage] + 2 * i + j + 1, (W_BASE[stage] + j + 1) % 2)
                        act.wait_ge(half_used, done + 2 * i + j + 1)
                        leave(stage, 8 * SUB[stage] + 4 * i + 2 * j, 0, 4 * i + 2 * j)
                        act.wait_ge(w_used, CR + W_BASE[stage] + 2 * i + j + 1)
                        leave(stage, 8 * SUB[stage] + 4 * i + 2 * j + 1, 1, 4 * i + 2 * j + 1)

            steps = Steps(act, act_step)
            for s_, v in ((mid_high, CR), (row_ready, 1)):
                act.sem_inc(s_, v)
            act.wait_ge(c_in, 16)
            steps.did(act.activation(cS[:, :, :], cT[:, :, :], ACT.Silu))
            steps.wait()
            act.activation(c2[:, :, 0:NCOND], cS[:, :, :], ACT.Copy).then_inc(c_high, 1)
            split_a(0)
            act.wait_ge(row_zero, 1)
            act.wait_ge(const_in, 16 * 8)
            squares_x("gate0")
            act.wait_ge(sp_e, 1)
            steps.did(act.activation(sp[1][:, :], sp[0][:, :], ACT.Exp, scale=-1.0))
            with act.Fori(0, A_FRONT // 2) as q:
                for j in range(2):
                    ada_copy(q, j)
                    split_a(2 * q + j + 1)
            n_half[0] = 0
            split_w(0, 0)
            root(1)
            modulate("gate0")
            gate_up(0)
            down(0)
            root(2)
            squares_x("even_in")
            root(3)
            modulate("even_in")
            act_even(act, steps, split_w, n_half)
            out_projection("even_out", EVEN_IN_TILES)
            root(4)
            squares_x("gate1")
            root(5)
            modulate("gate1")
            gate_up(1)
            down(1)
            root(6)
            squares_x("gate2")
            root(7)
            modulate("gate2")
            gate_up(2)
            down(2)
            root(8)
            squares_x("odd_in")
            root(9)
            modulate("odd_in")
            act_odd(act, steps, split_w, n_half)
            out_projection("odd_out", EVEN_IN_TILES + OUT_TILES + ODD_IN_TILES)
            root(10)
            squares_x("gate3")
            root(11)
            modulate("gate3")
            act.wait_ge(odd_stored, 32)
            gate_up(3)
            down(3)
            root(12)

        @block.vector
        def _(dve):
            def split_w(n, s, width=2048):
                for h, cols in enumerate(halves(width)):
                    dve.wait_ge(w_high, 2 * n + h + 1)
                    dve.tensor_tensor(w_lo[s][:, cols], w_raw[:, s, cols], w_hi[s][:, cols].bitcast(F32),
                                      ALU.subtract).then_inc(w_split, 1)

            def split_a(g):
                for h in range(2):
                    dve.wait_ge(a_high, 2 * g + h + 1)
                    dve.tensor_tensor(a_lo[h][:, :], a_raw[:, h, :], a_hi[h][:, :].bitcast(F32), ALU.subtract)\
                       .then_inc(a_split, 1)

            def ada_bias(q):
                dve.wait_ge(sel_done, 1 + q + 1)
                if isinstance(q, int):
                    dst, bias = modT[:, 4 * q:4 * q + 4, :], b_ada[:, 4 * q:4 * q + 4]
                else:
                    dst, bias = modT[:, bass.ds(4 * q, 4), :], b_ada[:, bass.ds(4 * q, 4)]
                dve.tensor_tensor(dst.rearrange("p (g c) n -> p c g n", g=2),
                                  ps[:, B_MOD, 0:4 * NCOND].rearrange("p (c g n) -> p c g n", c=2, g=2),
                                  bias.rearrange("p (g c) -> p c g", g=2).unsqueeze(3)
                                  .to_broadcast([P, 2, 2, NCOND]), ALU.add).then_inc(mod_ready, 1)

            def scale_factors(sub):
                dve.wait_ge(mod_ready, 1 + MOD_GROUPS(sub, 1) // 2)
                m = modT[:, scale_at(sub, 0):scale_at(sub, KC), :]
                dve.scalar_tensor_tensor(m, m, 1.0, g_pre[:, sub, :].unsqueeze(2).to_broadcast([P, KC, NCOND]),
                                         ALU.add, ALU.mult).then_inc(coef_ready, 1)
                dve.wait_ge(coef_ready, 2 * sub + 1)

            def gate_factors(sub):
                dve.wait_ge(mod_ready, 1 + MOD_GROUPS(sub, 2) // 2)
                m = modT[:, gate_at(sub, 0):gate_at(sub, KC), :]
                dve.scalar_tensor_tensor(m, m, 1.0 if sub % 3 == 1 else 0.5,
                                         g_post[:, sub, :].unsqueeze(2).to_broadcast([P, KC, NCOND]),
                                         ALU.mult, ALU.mult).then_inc(coef_ready, 1)
                dve.wait_ge(coef_ready, 2 * sub + 2)

            def MOD_GROUPS(sub, which):
                return GROUPS * (sub // 3) + 4 * (3 * (sub % 3) + which + 1)

            def reciprocal_of_mean(s):
                dve.wait_ge(stat_done, s)
                steps.did(dve.tensor_scalar(rtmp[:, :], ps[:, B_STAT, 0:TOK], EPS, None, ALU.add))
                steps.wait()
                dve.reciprocal(rrec[:, :], rtmp[:, :]).then_inc(rec_ready, 1)
                dve.wait_ge(rstd_ready, s)

            def add_residual(stage):
                def add(k):
                    steps.wait(marks[k])
                    dve.tensor_tensor(x[:, k, :], x[:, k, :], f[:, k, :], ALU.add).then_inc(x_ready, 1)
                marks = []
                for k in range(KC):
                    marks.append(steps.did(dve.tensor_tensor(f[:, k, :], f[:, k, :], rstd[:, :], ALU.mult)))
                    if k:
                        add(k - 1)
                add(KC - 1)

            def normed(prep):
                j, sub = PREP[prep], PNORM[prep]

                def low(k):
                    dve.wait_ge(xn_high, 8 * j + k + 1)
                    dve.tensor_tensor(xn_lo[:, k, :], f[:, k, :], xn_hi[:, k, :].bitcast(F32), ALU.subtract)\
                       .then_inc(xn_ready, 1)
                if sub:
                    dve.wait_ge(x_ready, 8 * sub)
                for k in range(KC):
                    dve.tensor_tensor(f[:, k, :], x[:, k, :], rstd[:, :], ALU.mult).then_inc(xr_ready, 1)
                    dve.wait_ge(xr_ready, 8 * sub + k + 1)
                    fs = tokens(f[:, k, PTOK:TOK])
                    steps.did(dve.tensor_tensor(fs, fs, per_sample(modT[:, scale_at(sub, k), 1:NCOND]), ALU.mult))
                    steps.wait()
                    dve.tensor_tensor(fs, fs, per_sample(modT[:, shift_at(sub, k), 1:NCOND]), ALU.add)\
                       .then_inc(xmod_ready, 1)
                    if k:
                        low(k - 1)
                low(KC - 1)

            def gate_up(ff):
                stage = f"gate{ff}"
                with dve.Fori(0, HFC) as i:
                    for j in range(2):
                        n, p = W_BASE[stage] + 2 * i + j, FC * ff + 2 * i + j
                        split_w(n + 1, (W_BASE[stage] + j + 1) % 2)
                        if stage in A_BASE:
                            split_a(A_BASE[stage] + 2 * i + j + 1)
                        dve.wait_ge(sil_ready, p + 1)
                        dve.wait_ge(mid_high, CR + p - 1)
                        dve.tensor_tensor(hbuf[:, j, :], ps[:, 2 * j + 1, 0:TOK], sil[:, j, :], ALU.mult)\
                           .then_inc(gu_free, 1)
                        dve.wait_ge(mid_high, CR + p + 1)
                        dve.tensor_tensor(at(mid_lo, 2 * i + j), hbuf[:, j, :],
                                          at(mid_hi, 2 * i + j).bitcast(F32), ALU.subtract).then_inc(mid_ready, 1)
                    if stage in A_BASE:
                        ada_bias(A_BASE[stage] // 2 + i)

            def leave(stage, q, b, m):
                dve.wait_ge(sq_ready, q + 1)
                dve.tensor_tensor(tokens(at(f, m)[:, PTOK:TOK]), tokens(ps[:, b, PTOK:TOK]),
                                  per_sample(at(modT, gate_at(SUB[stage], 0) + m)[:, 1:NCOND]), ALU.mult)
                dve.wait_ge(y_evac, CR + q)
                dve.tensor_tensor(sqacc[:, :], sqacc[:, :], sq2[:, b, :], ALU.add).then_inc(y_evac, 1)

            def start_sum():
                steps.did(dve.memset(sqacc[:, :], 0.0))
                steps.wait()

            def down(ff):
                stage = f"down{ff}"
                gate_factors(SUB[stage])
                start_sum()

                def body(i, ada, last=False):
                    for m in range(2):
                        for h in range(2):
                            j = 2 * m + h
                            if not (last and ff == N_FFN - 1 and j == 3):
                                split_w(W_BASE[stage] + 4 * i + j + 1, (W_BASE[stage] + j + 1) % 2,
                                        2048 if last and j == 3 else HFC * P)
                        if ada and not (stage == "down2" and i == 1 and m == 1):
                            split_a(A_BASE[stage] + 2 * i + m + 1)
                        dve.wait_ge(w_used, CR + W_BASE[stage] + 4 * i + 2 * m + 2)
                        leave(stage, 8 * SUB[stage] + 2 * i + m, m, 2 * i + m)
                    if ada:
                        ada_bias(A_BASE[stage] // 2 + i)

                down_loops(dve, ff, body)

            def out_projection(stage, done):
                gate_factors(SUB[stage])
                start_sum()
                with dve.Fori(0, 2) as i:
                    for j in range(2):
                        split_w(W_BASE[stage] + 2 * i + j + 1, (W_BASE[stage] + j + 1) % 2)
                        dve.wait_ge(half_used, done + 2 * i + j + 1)
                        leave(stage, 8 * SUB[stage] + 4 * i + 2 * j, 0, 4 * i + 2 * j)
                        dve.wait_ge(w_used, CR + W_BASE[stage] + 2 * i + j + 1)
                        leave(stage, 8 * SUB[stage] + 4 * i + 2 * j + 1, 1, 4 * i + 2 * j + 1)

            def softplus():
                z, u, w, s2_, acc = sp
                dve.wait_ge(lam_in, 16)
                steps.did(dve.tensor_scalar(w[:, :], lam[:, :], -1.0, None, ALU.mult))
                steps.wait()
                dve.tensor_tensor(z[:, :], w[:, :], lam[:, :], ALU.max).then_inc(sp_e, 1)
                dve.wait_ge(act_step, 2)
                steps.did(dve.tensor_scalar(s2_[:, :], u[:, :], 2.0, None, ALU.add))
                steps.wait()
                steps.did(dve.reciprocal(acc[:, :], s2_[:, :]))
                steps.wait()
                steps.did(dve.tensor_tensor(u[:, :], u[:, :], acc[:, :], ALU.mult))
                steps.wait()
                steps.did(dve.tensor_tensor(s2_[:, :], u[:, :], u[:, :], ALU.mult))
                steps.wait()
                steps.did(dve.tensor_scalar(acc[:, :], s2_[:, :], 1.0 / 19.0, None, ALU.mult))
                steps.wait()
                for odd in range(17, 1, -2):
                    steps.did(dve.scalar_tensor_tensor(acc[:, :], acc[:, :], 1.0 / odd, s2_[:, :],
                                                       ALU.add, ALU.mult))
                    steps.wait()
                steps.did(dve.scalar_tensor_tensor(acc[:, :], acc[:, :], 1.0, u[:, :], ALU.add, ALU.mult))
                steps.did(dve.tensor_scalar(w[:, :], w[:, :], 0.0, None, ALU.max))
                steps.wait()
                steps.did(dve.scalar_tensor_tensor(acc[:, :], acc[:, :], 2.0, w[:, :], ALU.mult, ALU.add))
                steps.wait()
                steps.did(dve.tensor_scalar(spl8[:, :], acc[:, :], -8.0, None, ALU.mult))
                dve.tensor_scalar(spl8n[:, :], acc[:, :], 8.0, None, ALU.mult).then_inc(sp_done, 1)

            steps = Steps(dve, dve_step)
            for s_, v in ((w_split, CR), (a_split, CR), (gu_free, CR), (y_evac, CR), (mod_ready, 1)):
                dve.sem_inc(s_, v)
            dve.wait_ge(c_high, 1)
            dve.tensor_tensor(c2[:, :, NCOND:2 * NCOND], cS[:, :, :], c2[:, :, 0:NCOND].bitcast(F32),
                              ALU.subtract).then_inc(c_split, 1)
            split_a(0)
            dve.memset(ada_row[:, :], 0.0).then_inc(row_zero, 1)
            softplus()
            dve.wait_ge(const_in, 16 * 8)
            with dve.Fori(0, A_FRONT // 2) as q:
                for j in range(2):
                    split_a(2 * q + j + 1)
                ada_bias(q)
            split_w(0, 0)
            scale_factors(0)
            reciprocal_of_mean(1)
            normed("gate0")
            gate_up(0)
            down(0)
            scale_factors(1)
            reciprocal_of_mean(2)
            add_residual("down0")
            reciprocal_of_mean(3)
            normed("even_in")
            dve_even(dve, steps, split_w)
            out_projection("even_out", EVEN_IN_TILES)
            scale_factors(2)
            reciprocal_of_mean(4)
            add_residual("even_out")
            reciprocal_of_mean(5)
            normed("gate1")
            gate_up(1)
            down(1)
            scale_factors(3)
            reciprocal_of_mean(6)
            add_residual("down1")
            reciprocal_of_mean(7)
            normed("gate2")
            gate_up(2)
            down(2)
            scale_factors(4)
            reciprocal_of_mean(8)
            add_residual("down2")
            reciprocal_of_mean(9)
            normed("odd_in")
            dve_odd(dve, steps, split_w)
            out_projection("odd_out", EVEN_IN_TILES + OUT_TILES + ODD_IN_TILES)
            scale_factors(5)
            reciprocal_of_mean(10)
            add_residual("odd_out")
            reciprocal_of_mean(11)
            normed("gate3")
            dve.wait_ge(odd_stored, 32)
            gate_up(3)
            down(3)
            reciprocal_of_mean(12)
            add_residual("down3")

        @block.gpsimd
        def _(gp):
            gp.wait_ge(const_in, 16 * 8)
            gp_even(gp)
            gp_odd(gp)


def tables():
    pos = np.concatenate([np.arange(PTOK), np.tile(PAST + np.arange(NT), NB)]).astype(np.float32)
    step = np.concatenate([np.arange(PTOK) % P, np.tile(np.arange(NT), NB)]).astype(np.float32)
    own = np.repeat(np.arange(NB), NT)
    tok = np.tile(np.arange(NT), NB)
    two = np.tile(np.eye(NCOND), (2, 1))
    out = {"ident": np.eye(P), "ones_d": np.full((P, P), 1.0 / D), "ones_h": np.full((P, P), 1.0 / P),
           "sel2": np.block([[two, 0 * two], [np.zeros((32 - 2 * NCOND, 2 * NCOND))], [0 * two, two]])}
    perm = np.zeros((P, 2, P))
    rope = np.zeros((P, 4, TOK))
    rope[:, 0] = 1.0
    inv_a = np.power(np.float32(500000.0), -np.arange(0, 16, 2, dtype=np.float32) / np.float32(16))
    inv_r = np.power(np.float32(10000.0), -np.linspace(0.0, 1.0, 64, dtype=np.float32))
    for kind, starts, half, inv in ((0, (0, HD), 8, inv_a), (1, (0,), 64, inv_r)):
        ang = pos[None, :] * inv.astype(np.float32)[:, None]
        for s in starts:
            for i in range(half):
                perm[s + half + i, kind, s + i] = -1.0
                perm[s + i, kind, s + half + i] = 1.0
            for o in (s, s + half):
                rope[o:o + half, 2 * kind] = np.cos(ang)
                rope[o:o + half, 2 * kind + 1] = np.sin(ang)
    out["perm"], out["rope"] = perm, rope
    lg = np.array(LN_G)
    i = np.arange(P)
    diff = i[None, :] - i[:, None]
    out["dec_p"] = np.where(diff >= 0, np.exp(np.maximum(diff, 0) * lg[:, None, None]), 0.0).transpose(1, 0, 2)
    same = (own[:, None] == own[None, :]) & (tok[None, :] >= tok[:, None])
    ds = np.maximum(tok[None, :] - tok[:, None], 0)
    out["dec_s"] = np.where(same, np.exp(ds * lg[:, None, None]), 0.0).transpose(1, 0, 2)
    out["qdec"] = np.broadcast_to(np.exp((step[None, :] + 1.0) * lg[:, None]), (P, RH, TOK))
    kd = np.zeros((P, 2, RH))
    kd[:, 0] = np.exp((P - 1.0 - i[:, None]) * lg[None, :])
    kd[0:STOK, 1] = np.exp((NT - 1.0 - tok[:, None]) * lg[None, :])
    out["kdec"] = kd
    out["bmask"] = (own[:, None] == np.arange(NB)[None, :])
    q = np.arange(PTOK).reshape(2, P)
    out["bias_p"] = np.where(np.arange(PTOK)[None, None, :] <= q[:, :, None], 0.0, NEG).transpose(1, 0, 2)
    bs = np.zeros((STOK, KEYS_S))
    bs[:, PAST:] = np.where((own[:, None] == own[None, :]) & (tok[None, :] <= tok[:, None]), 0.0, NEG)
    out["bias_s"] = bs
    b4, xx, tt = np.meshgrid(np.arange(4), np.arange(4), np.arange(NT), indexing="ij")
    b4, xx, tt = b4.ravel(), xx.ravel(), tt.ravel()
    sel = np.zeros((P, 2, STOK))
    for bh in range(2):
        sel[np.arange(P), bh, NT * (4 * bh + b4) + tt] = 1.0
    out["sel_s"], out["rep_s"] = sel, sel.transpose(2, 1, 0)
    head = 2 * (xx % 2) + xx // 2
    out["hmask"] = (head[:, None] == np.arange(NIH)[None, :])
    return {k: np.ascontiguousarray(v, dtype=np.float32) for k, v in out.items()}


def blocks_of(w, cols, n_blocks):
    w = np.pad(np.asarray(w)[:, cols], ((0, 0), (0, n_blocks * P - len(cols))))
    return w.reshape(KC, P, n_blocks // 2, 2, P).transpose(2, 1, 3, 0, 4).reshape(n_blocks // 2, P, 2 * KC * P)


def lay_out(a):
    d = dict(tables())
    d["x"] = np.concatenate([a["x_prompt"].reshape(PTOK, D), a["x_sample"].reshape(STOK, D)]).T.reshape(KC, P, TOK)
    d["cT"] = np.concatenate([a["c_prompt"], a["c_sample"]]).T.reshape(KC, P, NCOND)
    d["lam"] = a["rg_lambda"].reshape(KC, P).T
    d["b_ada"] = a["b_ada"].reshape(2 * CH_L, P).T
    d["g_pre"] = a["g_pre"].reshape(6, KC, P).transpose(2, 0, 1)
    d["g_post"] = a["g_post"].reshape(6, KC, P).transpose(2, 0, 1)
    d["pages"] = a["page_table"].reshape(1, 2 * NB).astype(np.int32)
    w = a["w_ada"].reshape(2, 2, KC // 2, P, GROUPS, ADA_COLS)
    d["ada"] = w.transpose(0, 4, 1, 3, 2, 5).reshape(2 * GROUPS * 2, P, KC // 2 * ADA_COLS)
    gu = np.stack([a["w_ffn_gate"].reshape(N_FFN, KC, P, FC, P), a["w_ffn_up"].reshape(N_FFN, KC, P, FC, P)])
    d["gu"] = gu.transpose(1, 4, 3, 0, 2, 5).reshape(N_FFN * FC, P, 2 * KC * P)
    wd = a["w_ffn_down"].reshape(N_FFN, 2, HFC, P, KC, P)
    d["down"] = wd.transpose(0, 4, 1, 3, 2, 5).reshape(N_FFN * 2 * KC, P, HFC * P)
    at_ = np.cumsum([0, 512, 128, 128, 256, 4, 64, 512, 512, 512])
    q0, k0, v0, qi0, wi0, ki0, rq0, rk0, rv0, rg0 = at_
    r = lambda s, n: list(range(s, s + n))
    cols = []
    for j in range(NR):
        cols += r(q0 + HD * j, HD) + r(q0 + HD * (NR + j), HD)
    cols += r(k0, P) + r(qi0, 2 * P) + r(ki0, HD) * 2
    for h in range(RH):
        cols += r(rq0 + P * h, P) + r(rk0 + P * h, P)
    w = a["w_in_even"][0]
    wi = np.zeros((D, P), w.dtype)
    wi[:, 0:NIH] = w[:, wi0:wi0 + NIH]
    even = np.concatenate([w[:, cols], w[:, r(v0, P)], wi, w[:, r(rv0, 4 * P)], w[:, r(rg0, 4 * P)]], axis=1)
    rows = []
    for j in range(NR):
        rows += r(HD * j, HD) + r(HD * (NR + j), HD)
    rows += r(512, 512)
    odd = a["w_in_odd"][0]
    cols = sum([r(P * c, P) + r(D + P * c, P) for c in range(KC)], [])
    every = np.arange(D)
    d["pj"] = np.concatenate([blocks_of(even, np.arange(even.shape[1]), EVEN_BLOCKS),
                              blocks_of(a["w_out_even"][0][rows], every, KC),
                              blocks_of(odd, cols, 2 * KC), blocks_of(a["w_out_odd"][0], every, KC)])
    d["kidx_pages"] = a["cache_kidx"][0].transpose(0, 2, 1)
    d["k_pages"] = a["cache_k"][0].reshape(N_PHYS, PAGE, P).transpose(0, 2, 1)
    d["v_pages"] = a["cache_v"][0].reshape(N_PHYS, PAGE, P)
    d["state_ret"] = a["state_ret"][0]
    d["conv_state"] = a["state_conv"][0].reshape(NB, 3, KC, P).transpose(3, 2, 0, 1)
    d["conv_w"] = a["conv_w"][0].reshape(CONVW, KC, P).transpose(2, 1, 0)
    d["conv_b"] = a["conv_b"][0].reshape(KC, P, 1).transpose(1, 0, 2)
    d["b_rg"] = np.stack([a["b_rg_a"][0].reshape(KC, P), a["b_rg_x"][0].reshape(KC, P)]).transpose(2, 0, 1)
    d["h0"] = a["state_rglru"][0].reshape(NB, KC, P).transpose(2, 1, 0)
    d["w_rg"] = np.concatenate([a["w_rg_a"][0], a["w_rg_x"][0]]).transpose(1, 0, 2)
    return {k: np.ascontiguousarray(v) for k, v in d.items()}


OUTS = {"y": (KC, P, TOK), "k_o": (P, TOK), "v_o": (P, TOK), "ki_o": (HD, TOK), "ret_p": (RH, P, P),
        "ret_s": (NB, RH, P, P), "tails": (P, KC, NCOND, 3), "hlast": (P, KC, NCOND)}


def kernel(**inputs):
    import concourse.bacc as bacc
    from concourse.bass_utils import run_bass_kernel_spmd

    nc = bacc.Bacc("TRN2", target_bir_lowering=False, num_devices=1)
    arrays = lay_out({k: np.asarray(v) for k, v in inputs.items()})
    aps, feed = {}, {}
    for name, a in arrays.items():
        feed[f"in_{name}"] = a
        aps[name] = nc.dram_tensor(f"in_{name}", a.shape, mybir.dt.from_np(a.dtype), kind="ExternalInput").ap()
    for name, shape in OUTS.items():
        aps[name] = nc.dram_tensor(f"out_{name}", shape, F32, kind="ExternalOutput").ap()
    build(nc, aps)
    r = run_bass_kernel_spmd(nc, [feed], core_ids=[0]).results[0]
    r = {k: np.asarray(r[f"out_{k}"]) for k in OUTS}
    y = r["y"].reshape(D, TOK).T

    def heads(o, n):
        o = o.T
        return (o[:PTOK].reshape((1, 1, PTOK) + n).copy(), o[PTOK:].reshape((1, NB, NT) + n).copy())

    k_p, k_s = heads(r["k_o"], (NKV, HD))
    v_p, v_s = heads(r["v_o"], (NKV, HD))
    ki_p, ki_s = heads(r["ki_o"], (HD,))
    tails = r["tails"].transpose(2, 3, 1, 0).reshape(NCOND, 3, D)
    hl = r["hlast"].transpose(2, 1, 0).reshape(NCOND, D)
    return (y[:PTOK].reshape(1, PTOK, D).copy(), y[PTOK:].reshape(NB, NT, D).copy(), k_p, v_p, ki_p,
            r["ret_p"][None, None], tails[None, 0:1].copy(), hl[None, 0:1].copy(),
            k_s, v_s, ki_s, r["ret_s"][None], tails[None, 1:].copy(), hl[None, 1:].copy())
```

```python
from contextlib import ExitStack

import numpy as np
import concourse.bass as bass
from concourse import mybir

P = 128
F32 = mybir.dt.float32
F32R = mybir.dt.float32r
I32 = mybir.dt.int32
ALU = mybir.AluOpType
ACT = mybir.ActivationFunctionType
AX = mybir.AxisListType.X

D = 1024
KC = D // P
PTOK = 256
NB, NT = 8, 8
STOK = NB * NT
TOK = PTOK + STOK
NCOND = 1 + NB
FF = 2816
FC = FF // P
HFC = FC // 2
N_FFN = 4
NMOD = 9
ADA_COLS = 256
GROUPS = NMOD * D // ADA_COLS
CH_L = NMOD * KC
EPS = 1e-6
PAST = 256
PAGE = 128
N_PHYS = 20
HD = 64
NH, NKV = 8, 2
NR = NH // NKV
NIH = 4
RH = 4
TOPK_P = 64
TOPK_S = 66
KEYS_S = PAST + STOK
PAD_S = -TOPK_S % 8
NEG, TAKEN, WINS = -1.0e30, -3.0e38, 3.0e38
LN_G = [float(np.log1p(-(2.0 ** (-5.0 - h)))) for h in range(RH)]
CDEC_P = [float(np.exp(np.float32(128 * g))) for g in LN_G]
CDEC_S = [float(np.exp(np.float32(NT * g))) for g in LN_G]
CONVW = 4
XW = (PTOK + 3) + NB * (NT + 3)
GELU_SCALE = 2.0 * float(np.sqrt(2.0 / np.pi))

B_Q, B_K, B_QI, B_KI = 0, 4, 5, 7
B_V, B_WI = 8, 9
B_RQK = 10
B_RV, B_RG = 18, 22
EVEN_BLOCKS = 26

A_FRONT = 8

EVEN_IN_TILES = EVEN_BLOCKS // 2
OUT_TILES = KC // 2
ODD_IN_TILES = KC
W_BASE = {}
_n = 0
for _stage, _count in (("front", A_FRONT), ("gate0", FC), ("down0", 2 * KC), ("even_in", EVEN_IN_TILES),
                       ("even_out", OUT_TILES), ("gate1", FC), ("down1", 2 * KC),
                       ("gate2", FC), ("down2", 2 * KC), ("odd_in", ODD_IN_TILES),
                       ("odd_out", OUT_TILES), ("gate3", FC), ("down3", 2 * KC)):
    W_BASE[_stage] = _n
    _n += _count
W_TILES = _n
A_BASE = {"gate0": 8, "down0": 30, "gate1": 38, "down1": 60, "down2": 68}
A_GROUPS = 2 * GROUPS
CR = 2


class Steps:

    def __init__(self, eng, sem):
        self.eng, self.sem, self.n = eng, sem, 0

    def did(self, ins):
        ins.then_inc(self.sem, 1)
        self.n += 1
        return self.n

    def wait(self, at=None):
        self.eng.wait_ge(self.sem, self.n if at is None else at)


def at(ap3, i):
    if isinstance(i, int):
        return ap3[:, i, :]
    return ap3[:, bass.ds(i, 1), :].rearrange("p o n -> p (o n)")


def at4(ap4, i):
    if isinstance(i, int):
        return ap4[:, i, :, :]
    return ap4[:, bass.ds(i, 1), :, :].rearrange("p o a b -> p (o a) b")


def row(ap3, i):
    if isinstance(i, int):
        return ap3[i]
    return ap3[bass.ds(i, 1), :, :].rearrange("o p n -> p (o n)")


def build(nc, t):
    with ExitStack() as ctx:
        sems = {}

        def sem(name):
            if name not in sems:
                sems[name] = ctx.enter_context(nc.semaphore(name))
            return sems[name]

        def sb(name, shape, dt=F32):
            return ctx.enter_context(nc.sbuf_tensor(name, shape, dt))

        under = ExitStack()
        rb = lambda name, shape, dt=F32: under.enter_context(nc.sbuf_tensor(name, shape, dt))
        st_in = rb("st_in", [P, NB, P])
        st_out = rb("st_out", [P, NB, P])
        kt = rb("kt", [P, 3, P])
        vt = rb("vt", [P, 3, P])
        qd = rb("qd", [P, P])
        qz = rb("qz", [P, NB * (STOK + NT)])
        am = rb("am", [P, 2, P])
        am_s = rb("am_s", [STOK, STOK])
        s1 = rb("s1", [P, P])
        s2 = rb("s2", [P, P])
        vm = rb("vm", [STOK, NB, P])
        under.close()
        xn_hi = sb("xn_hi", [P, KC, TOK], F32R)
        xn_lo = sb("xn_lo", [P, KC, TOK], F32R)
        x = sb("x", [P, KC, TOK])
        f = sb("f", [P, KC, TOK])
        w_raw = sb("w_raw", [P, 2, 2048])
        w_hi = [sb(f"w_hi{s}", [P, 2048], F32R) for s in range(2)]
        w_lo = [sb(f"w_lo{s}", [P, 2048], F32R) for s in range(2)]
        under = ExitStack()
        lg = rb("lg", [P, 2, NKV, KEYS_S])
        pT = rb("pT", [P, 2, 6 * P])
        relu = rb("relu", [P, 2, 4 * P])
        score_p = rb("score_p", [P, 3 * P])
        bias_r = rb("bias_r", [P, 2, KEYS_S])
        under.close()
        a_raw = sb("a_raw", [P, 2, 1024])
        a_hi = [sb(f"a_hi{s}", [P, 1024], F32R) for s in range(2)]
        a_lo = [sb(f"a_lo{s}", [P, 1024], F32R) for s in range(2)]
        modT = sb("modT", [P, 2 * CH_L, NCOND])
        ada_row = sb("ada_row", [32 + 2 * NCOND, ADA_COLS])
        c2 = sb("c2", [P, KC, 2 * NCOND], F32R)
        b_ada = sb("b_ada", [P, 2 * CH_L])
        g_pre = sb("g_pre", [P, 6, KC])
        g_post = sb("g_post", [P, 6, KC])
        rstd = sb("rstd", [P, TOK])
        rms = sb("rms", [P, TOK])
        eps = sb("eps", [P, 1])
        sqacc = sb("sqacc", [P, TOK])
        sq2 = sb("sq2", [P, 2, TOK])
        ident = sb("ident", [P, P])
        ones_d = sb("ones_d", [P, P])
        sel2 = sb("sel2", [32 + 2 * NCOND, 2 * NCOND])
        spl8 = sb("spl8", [P, KC])
        spl8n = sb("spl8n", [P, KC])
        pages = sb("pages", [1, 2 * NB], I32)
        cT = sb("cT", [P, KC, NCOND])
        cS = sb("cS", [P, KC, NCOND])
        lam = sb("lam", [P, KC])
        sp = [sb(f"sp{i}", [P, KC]) for i in range(5)]
        ps = ctx.enter_context(nc.psum_tensor("ps", [P, 8, 512], F32))
        B_ADA, B_MOD, B_STAT = (4, 7), 5, 6

        def phase():
            stack = ExitStack()
            return stack, lambda name, shape, dt=F32: stack.enter_context(nc.sbuf_tensor(name, shape, dt))

        stack, pb = phase()
        mid_hi = pb("mid_hi", [P, FC, TOK], F32R)
        mid_lo = pb("mid_lo", [P, FC, TOK], F32R)
        sil = pb("sil", [P, 2, TOK])
        hbuf = pb("hbuf", [P, 2, TOK])
        stack.close()
        stack, pb = phase()
        sqx = pb("sqx", [P, KC, TOK])
        stack.close()
        stack, pb = phase()
        proj = pb("proj", [P, EVEN_BLOCKS, TOK])
        perm = pb("perm", [P, 2, P])
        cached = pb("cached", [P, NB, 3, PAST])
        bias_p = pb("bias_p", [P, 2, PTOK])
        bias_s = pb("bias_s", [STOK, KEYS_S])
        score_s = pb("score_s", [STOK, KEYS_S + PAD_S])
        rep_s = pb("rep_s", [STOK, 2, P])
        sel_s = pb("sel_s", [P, 2, STOK])
        hmask = pb("hmask", [P, NIH])
        qiz = pb("qiz", [P, NB, 4, NT])
        qsm = pb("qsm", [P, NB, NR, NT])
        wi_tok = pb("wi_tok", [P, 3, NIH])
        wis = pb("wis", [P, 2, NIH])
        wis1 = pb("wis1", [P, 2])
        vtok = pb("vtok", [P, 3, P])
        top8 = pb("top8", [P, 8])
        nmx = pb("nmx", [P, 2, NKV])
        sm = pb("sm", [P, 2, NKV])
        rsm = pb("rsm", [P, 2, NKV])
        qdec = pb("qdec", [P, RH, P + STOK])
        dec_p = pb("dec_p", [P, RH, P])
        dec_s = pb("dec_s", [STOK, RH, STOK])
        kdec = pb("kdec", [P, 2, RH])
        bmask = pb("bmask", [STOK, NB])
        ones_h = pb("ones_h", [P, P])
        stack.close()
        ropet, rope_a, rope_b = f[:, 0:4, :], f[:, 4:6, :], f[:, 6:8, :]
        stack, pb = phase()
        gate = pb("gate", [P, KC, TOK])
        conv = pb("conv", [P, KC, TOK])
        ra = pb("ra", [P, KC, TOK])
        ib = pb("ib", [P, KC, TOK])
        xc = pb("xc", [P, 2, XW])
        wrg = pb("wrg", [P, 2 * KC, P])
        cw = pb("cw", [P, KC, CONVW])
        cb = pb("cb", [P, KC, 1])
        cst = pb("cst", [P, KC, NB, 3])
        brg = pb("brg", [P, 2, KC])
        b0 = pb("b0", [P, KC, 1])
        h0 = pb("h0", [P, KC, NB])
        tails = pb("tails", [P, KC, NCOND, 3])
        tah = pb("tah", [P, KC, NB])
        hlast = pb("hlast", [P, KC, NCOND])
        stack.close()
        gtmp = f

        w_landed = [[sem(f"w_landed{s}{h}") for h in range(2)] for s in range(2)]
        w_high = sem("w_high")
        w_split = sem("w_split")
        w_used = sem("w_used")
        a_landed = [sem(f"a_landed{s}") for s in range(2)]
        a_high, a_split, a_used = sem("a_high"), sem("a_split"), sem("a_used")
        row_ready = sem("row_ready")
        row_zero = sem("row_zero")
        sel_done = sem("sel_done")
        mod_ready = sem("mod_ready")
        coef_ready = sem("coef_ready")
        sil_ready = sem("sil_ready")
        gu_free = sem("gu_free")
        mid_high = sem("mid_high")
        mid_ready = sem("mid_ready")
        half_used = sem("half_used")
        sq_ready = sem("sq_ready")
        y_evac = sem("y_evac")
        stat_done, rms_ready, rstd_ready = sem("stat_done"), sem("rms_ready"), sem("rstd_ready")
        x_ready = sem("x_ready")
        sqx_ready = sem("sqx_ready")
        xr_ready = sem("xr_ready")
        xmod_ready = sem("xmod_ready")
        xn_high = sem("xn_high")
        xn_ready = sem("xn_ready")
        const_in, sel_in, bada_in = sem("const_in"), sem("sel_in"), sem("bada_in")
        c_in, c_silu, c_high, c_split = sem("c_in"), sem("c_silu"), sem("c_high"), sem("c_split")
        sp_e, sp_done = sem("sp_e"), sem("sp_done")
        lam_in = sem("lam_in")
        out_done = sem("out_done")
        dve_step = sem("dve_step")
        act_step = sem("act_step")

        SUB = {"down0": 0, "even_out": 1, "down1": 2, "down2": 3, "odd_out": 4, "down3": 5}
        PREP = {"gate0": 0, "even_in": 1, "even_out": 2, "gate1": 3, "gate2": 4, "odd_in": 5,
                "odd_out": 6, "gate3": 7}
        PNORM = {"gate0": 0, "even_in": 1, "gate1": 2, "gate2": 3, "odd_in": 4, "gate3": 5}

        def scale_at(sub, k):
            return CH_L * (sub // 3) + (3 * (sub % 3) + 1) * KC + k

        def shift_at(sub, k):
            return CH_L * (sub // 3) + (3 * (sub % 3)) * KC + k

        def gate_at(sub, k):
            return CH_L * (sub // 3) + (3 * (sub % 3) + 2) * KC + k

        def halves(width):
            return slice(0, 1024), slice(1024, width)

        DOWN_LOOPS = {0: ((0, 4, True),), 1: ((0, 4, True),), 2: ((0, 2, True), (2, 4, False)), 3: ((0, 4, False),)}

        def down_loops(eng, ff, body):
            if ff == 2:
                body(0, True)
                body(1, True)
                body(2, False)
            else:
                with eng.Fori(0, KC // 2 - 1) as i:
                    body(i, ff < 2)
            body(KC // 2 - 1, ff < 2, True)

        def per_sample(ap2):
            return ap2.unsqueeze(2).to_broadcast([P, NB, NT])

        def tokens(ap2):
            return ap2.rearrange("p (b t) -> p b t", b=NB)


        p_evac = sem("p_evac")
        rope_mm = sem("rope_mm")
        rope_done = sem("rope_done")
        perm_in, rope_in = sem("perm_in"), sem("rope_in")
        even_in_dma = sem("even_in_dma")
        PB = 4
        vw_tr, vw_ready = sem("vw_tr"), sem("vw_ready")
        qiz_ready, wis_mm, wis_ready = sem("qiz_ready"), sem("wis_mm"), sem("wis_ready")
        ix_row, lg_row = sem("ix_row"), sem("lg_row")
        ix_done = sem("ix_done")
        relu_ready = sem("relu_ready")
        relu_used = sem("relu_used")
        weighed, ixs_done, bias_ready = sem("weighed"), sem("ixs_done"), sem("bias_ready")
        tr_k, tr_v = sem("tr_k"), sem("tr_v")
        kt_ready, vt_ready = sem("kt_ready"), sem("vt_ready")
        att_done, am_ready = sem("att_done"), sem("am_ready")
        kv_done, s1_ready = sem("kv_done"), sem("s1_ready")
        qd_ready, vm_ready = sem("qd_ready"), sem("vm_ready")
        st_landed, o_done, osq_ready = sem("st_landed"), sem("o_done"), sem("osq_ready")
        kvs_done, st_ready, s2_ready = sem("kvs_done"), sem("st_ready"), sem("s2_ready")
        st_stored = sem("st_stored")
        ostat_done, ovar_ready = sem("ostat_done"), sem("ovar_ready")
        orec_ready, orstd_ready = sem("orec_ready"), sem("orstd_ready")
        o_ready = sem("o_ready")
        rep_done, rep_ready = sem("rep_done"), sem("rep_ready")
        lg_done, lg_ready, exp_ready, pr_ready = sem("lg_done"), sem("lg_ready"), sem("exp_ready"), sem("pr_ready")
        pt_done, pt_ready, pv_done, pv_out = sem("pt_done"), sem("pt_ready"), sem("pv_done"), sem("pv_out")
        kvo_stored = sem("kvo_stored")
        EVEN_DMAS = 10 + 2 * NB
        RQ = [B_RQK + 2 * h for h in range(RH)]
        RK = [B_RQK + 2 * h + 1 for h in range(RH)]
        CHUNKS = ((0, P), (P, P), (PTOK, STOK))
        UNITS = [("p", qt, j) for qt in range(2) for j in range(NR)] + [("s", bh, 0) for bh in range(2)]
        N_PU = 2 * NR

        def unit_keys(u):
            kind, a, _ = UNITS[u]
            return P * (a + 1) if kind == "p" else KEYS_S

        def unit_chunks(u):
            nk = unit_keys(u)
            return [(c, min(P, nk - P * c)) for c in range(-(-nk // P))]

        def logit_banks(u):
            nk = unit_keys(u)
            if UNITS[u][0] == "p":
                return ps[:, 4 + u % 2, 0:NKV * nk].rearrange("p (g n) -> p g n", g=NKV)
            first = 4 if u == N_PU else 0
            return ps[:, first:first + 2, 0:nk]

        def gp_even(gp):
            gp.wait_ge(w_used, CR + W_BASE["even_in"])
            gp.dma_start(perm[:, :, :], t["perm"]).then_inc(perm_in, 16)
            for dst, src in ((bias_p[:, :, :], t["bias_p"]), (bias_s[:, :], t["bias_s"]),
                             (rep_s[:, :, :], t["rep_s"]), (sel_s[:, :, :], t["sel_s"]),
                             (hmask[:, :], t["hmask"]), (dec_p[:, :, :], t["dec_p"]),
                             (qdec[:, :, :], t["qdec"]), (kdec[:, :, :], t["kdec"]),
                             (bmask[:, :], t["bmask"]), (dec_s[:, :, :], t["dec_s"])):
                gp.dma_start(dst, src).then_inc(even_in_dma, 16)
            gp.dma_start(ones_h[:, :], t["ones_h"]).then_inc(perm_in, 16)
            gp.wait_ge(xn_ready, 8 * (PREP["even_in"] + 1))
            gp.dma_start(ropet, t["rope"]).then_inc(rope_in, 16)
            for b in range(NB):
                for pg in range(2):
                    page = gp.value_load(pages[0:1, 2 * b + pg:2 * b + pg + 1], min_val=0, max_val=N_PHYS - 1)
                    gp.dma_start(cached[:, b, :, PAGE * pg:PAGE * (pg + 1)],
                                 row(t["pages_kv"], page).rearrange("p (x n) -> p x n", x=3)).then_inc(even_in_dma, 16)
            gp.wait_ge(p_evac, PB + EVEN_BLOCKS)
            gp.wait_ge(rope_done, CR + 16)
            for h in range(RH):
                if h:
                    gp.wait_ge(st_ready, h)
                gp.dma_start(st_in[:, :, :], t["state_ret"][:, h].rearrange("b d v -> d b v"))\
                  .then_inc(st_landed, 16)
                if h == 0:
                    gp.dma_start(t["k_o"], proj[:, B_K, :]).then_inc(kvo_stored, 16)
                    gp.dma_start(t["v_o"], proj[:, B_V, :]).then_inc(kvo_stored, 16)
                    gp.dma_start(t["ki_o"], proj[0:HD, B_KI, :]).then_inc(kvo_stored, 16)
                else:
                    store_states(gp, h - 1)
            store_states(gp, RH - 1)

        def store_states(gp, h):
            gp.wait_ge(s2_ready, h + 1)
            gp.dma_start(t["ret_p"][h], s2[:, :]).then_inc(st_stored, 16)
            gp.wait_ge(st_ready, h + 1)
            gp.dma_start(t["ret_s"][:, h].rearrange("b d v -> d b v"), st_out[:, :, :]).then_inc(st_stored, 16)

        def pe_even(pe, three_passes, w_half, both_blocks):
            base = W_BASE["even_in"]

            def rotate(b, r, kind):
                pe.wait_ge(p_evac, PB + b + 1)
                pe.wait_ge(rope_done, CR + r - 1)
                pe.matmul(ps[:, 4 + r % 2, 0:TOK], perm[:, kind, :], proj[:, b, :], start=True, stop=True)\
                  .then_inc(rope_mm, 1)

            def block_of(n, b, bank, slot_, h):
                w_half(n, h)
                pe.wait_ge(p_evac, PB + b - 3)
                for k in range(KC):
                    last = three_passes(ps[:, bank, 0:TOK], slot_, (h * KC + k) * P, xn_hi[:, k, :],
                                        xn_lo[:, k, :], k == 0, k == KC - 1)
                last.then_inc(half_used if h == 0 else w_used, 1)

            def value_columns():
                pe.wait_ge(p_evac, PB + B_WI + 1)
                for c, (c0, n) in enumerate(CHUNKS):
                    pe.transpose(ps[0:n, 6, P * c:P * (c + 1)], proj[:, B_V, c0:c0 + n], ident[:, :])
                    last = pe.transpose(ps[0:n, 6, 3 * P + NIH * c:3 * P + NIH * (c + 1)],
                                        proj[0:NIH, B_WI, c0:c0 + n], ident[0:NIH, 0:NIH])
                last.then_inc(vw_tr, 1)

            def index_prompt(qt, heads, bank):
                for x_, h in enumerate(heads):
                    rows = slice(HD * (h % 2), HD * (h % 2 + 1))
                    nk = P * (qt + 1)
                    if x_:
                        pe.wait_ge(ix_row, ix_n[0])
                    last = pe.matmul(ps[:, bank, nk * x_:nk * (x_ + 1)], proj[rows, B_QI + h // 2, P * qt:P * (qt + 1)],
                                     proj[rows, B_KI, 0:nk], start=True, stop=True)
                    if x_ < len(heads) - 1:
                        last.then_inc(ix_row, 1)
                        ix_n[0] += 1
                last.then_inc(ix_done, 1)

            def index_samples(bh):
                for b4 in range(4):
                    b = 4 * bh + b4
                    rows = slice(32 * b4, 32 * (b4 + 1))
                    qb = qiz[:, b, :, :].rearrange("p x t -> p (x t)")
                    pe.matmul(ps[rows, 6 + bh, 0:PAST], qb, cached[:, b, 0, :], start=True, stop=True)
                    last = pe.matmul(ps[rows, 6 + bh, PAST:KEYS_S], qb, proj[:, B_KI, PTOK:TOK], start=True, stop=True)
                last.then_inc(ix_done, 1)

            ix_n = [0]

            def after(b):
                if b == 10:
                    value_columns()
                elif b == 11:
                    pe.wait_ge(rope_done, CR + 8)
                    index_prompt(0, range(NIH), 7)
                elif b == 12:
                    pe.wait_ge(even_in_dma, 16 * EVEN_DMAS)
                    pe.wait_ge(vw_ready, 1)
                    for bh in range(2):
                        last = pe.matmul(ps[:, 6, NIH * bh:NIH * (bh + 1)], rep_s[:, bh, :], wi_tok[0:STOK, 2, :],
                                         start=True, stop=True)
                    last.then_inc(wis_mm, 1)
                elif b == 13:
                    pe.wait_ge(wis_ready, 1)
                    index_prompt(1, (0, 1), 6)
                    pe.wait_ge(relu_ready, 1)
                    index_prompt(1, (2, 3), 7)
                elif b == 17:
                    pe.wait_ge(qiz_ready, 1)
                    for bh in range(2):
                        pe.wait_ge(relu_ready, 2 + bh)
                        index_samples(bh)
                elif b == 19:
                    pe.wait_ge(weighed, 1)
                    for bh in range(2):
                        last = pe.matmul(ps[0:STOK, 6, 0:KEYS_S], sel_s[:, bh, :], relu[:, 1 - bh, 0:KEYS_S],
                                         start=(bh == 0), stop=(bh == 1))
                    last.then_inc(ixs_done, 1)

            pe.wait_ge(mod_ready, 1 + (A_BASE["down0"] + KC) // 2)
            pe.wait_ge(perm_in, 32)
            both_blocks("even_in", base % 2, (0, 1), True).then_inc(w_used, 1)
            for b in range(1, EVEN_BLOCKS):
                if b > 1:
                    block_of(base + b // 2, b, b % 4, (base + b // 2) % 2, b % 2)
                if b <= 8:
                    rotate(b - 1, b - 1, 0)
                elif B_RQK < b <= B_RQK + 8:
                    rotate(b - 1, b - 1 - (B_RQK - 8), 1)
                after(b)

            def spread(h):
                rq, rk, rv = proj[:, RQ[h], :], proj[:, RK[h], :], proj[:, B_RV + h, :]
                if h:
                    pe.wait_ge(st_ready, h)
                    pe.wait_ge(s2_ready, h)
                for bank, src, done in ((0, rk, tr_k), (1, rv, tr_v)):
                    for c, (c0, n) in enumerate(CHUNKS):
                        last = pe.transpose(ps[0:n, bank, c * P:(c + 1) * P], src[:, c0:c0 + n], ident[:, :])
                    last.then_inc(done, 1)
                for c in range(2):
                    pe.matmul(ps[:, 2, c * P:(c + 1) * P], rk[:, c * P:(c + 1) * P], rq[:, c * P:(c + 1) * P],
                              start=True, stop=True)
                pe.matmul(ps[0:STOK, 2, PTOK:TOK], rk[:, PTOK:TOK], rq[:, PTOK:TOK], start=True, stop=True)\
                  .then_inc(att_done, 1)

            def head_stat(h):
                pe.wait_ge(osq_ready, h + 1)
                pe.matmul(ps[:, 3, 0:TOK], ones_h[:, :], proj[:, RQ[h], :], start=True, stop=True)\
                  .then_inc(ostat_done, 1)

            def inner(h):
                pe.wait_ge(am_ready, h + 1)
                pe.wait_ge(kt_ready, h + 1)
                pe.wait_ge(vt_ready, h + 1)
                for c in range(2):
                    last = pe.matmul(ps[:, 2, c * P:(c + 1) * P], kt[:, c, :], vt[:, c, :], start=True, stop=True)
                last.then_inc(kv_done, 1)
                if h:
                    pe.wait_ge(ovar_ready, h)
                pe.matmul(ps[:, 3, 0:P], vt[:, 0, :], am[:, 0, :], start=True, stop=True)
                pe.matmul(ps[:, 3, P:2 * P], vt[:, 1, :], am[:, 1, :], start=True, stop=False)
                pe.wait_ge(s1_ready, h + 1)
                pe.wait_ge(qd_ready, h + 2)
                pe.matmul(ps[:, 3, P:2 * P], s1[:, :], qd[:, :], start=False, stop=True)
                pe.wait_ge(vm_ready, h + 1)
                for i in range(2):
                    last = pe.matmul(ps[:, i, :], kt[0:STOK, 2, :],
                                     vm[:, 4 * i:4 * i + 4, :].rearrange("p b v -> p (b v)"), start=True, stop=True)
                last.then_inc(kvs_done, 1)

            def cross(h):
                pe.wait_ge(st_landed, 16 * (h + 1))
                for b in range(NB):
                    pe.matmul(ps[:, 3, PTOK:TOK], st_in[:, b, :], qz[:, STOK * b:STOK * (b + 1)],
                              start=(b == 0), stop=False)
                pe.matmul(ps[:, 3, PTOK:TOK], vt[0:STOK, 2, :], am_s[:, :], start=False, stop=True)\
                  .then_inc(o_done, 1)

            def logits(u):
                kind, a, j = UNITS[u]
                out_ = logit_banks(u)
                if kind == "p" and u >= 2:
                    pe.wait_ge(lg_ready, u - 1)
                elif u == N_PU:
                    pe.wait_ge(lg_ready, u)
                elif u == N_PU + 1:
                    pe.wait_ge(rep_ready, 1)
                for g in range(NKV):
                    rows = slice(HD * g, HD * (g + 1))
                    if kind == "p":
                        if g:
                            pe.wait_ge(lg_row, lg_n[0])
                        last = pe.matmul(out_[:, g, :], proj[rows, B_Q + j, P * a:P * (a + 1)],
                                         proj[rows, B_K, 0:unit_keys(u)], start=True, stop=True)
                        if g == 0:
                            last.then_inc(lg_row, 1)
                            lg_n[0] += 1
                        continue
                    for b4 in range(4):
                        b = 4 * a + b4
                        out = slice(32 * b4, 32 * (b4 + 1))
                        qb = qsm[rows, b, :, :].rearrange("p r t -> p (r t)")
                        pe.matmul(out_[out, g, 0:PAST], qb, cached[rows, b, 1, :], start=True, stop=True)
                        last = pe.matmul(out_[out, g, PAST:KEYS_S], qb, proj[rows, B_K, PTOK:TOK],
                                         start=True, stop=True)
                last.then_inc(lg_done, 1)

            lg_n = [0]

            def turn(u):
                pe.wait_ge(pr_ready, u + 1)
                if u:
                    pe.wait_ge(pt_ready, u)
                if u == N_PU:
                    pe.wait_ge(s2_ready, RH)
                for c, n in unit_chunks(u):
                    for g in range(NKV):
                        col = (2 * (c % 2) + g) * P
                        last = pe.transpose(ps[0:n, 2 if c == 2 else 6, col:col + P],
                                            lg[:, u % 2, g, P * c:P * c + n], ident[:, :])
                last.then_inc(pt_done, 1)

            def weigh(u):
                kind, a, j = UNITS[u]
                pe.wait_ge(pt_ready, u + 1)
                if u:
                    pe.wait_ge(pv_out, min(u, N_PU))
                pt = pT[:, u % 2, :].rearrange("p (c g n) -> p c g n", c=3, g=NKV)
                chunks = unit_chunks(u)
                if kind == "p":
                    for g in range(NKV):
                        for c, n in chunks:
                            last = pe.matmul(ps[HD * g:HD * (g + 1), 7, 0:P], vtok[:, c, HD * g:HD * (g + 1)],
                                             pt[:, c, g, :], start=(c == 0), stop=(c == len(chunks) - 1))
                else:
                    for b4 in range(4):
                        b = 4 * a + b4
                        own = slice(32 * b4, 32 * (b4 + 1))
                        for c, n in chunks:
                            v = cached[:, b, 2, P * c:P * (c + 1)] if c < 2 else vtok[0:STOK, 2, :]
                            last = pe.matmul(ps[:, 7, 64 * b:64 * (b + 1)], v, pt[0:n, c, :, own],
                                             start=(c == 0), stop=(c == 2))
                last.then_inc(pv_done, 1)

            pe.wait_ge(p_evac, PB + EVEN_BLOCKS)
            pe.wait_ge(rope_done, CR + 16)
            logits(0)
            for h in range(RH):
                spread(h)
                if h:
                    head_stat(h - 1)
                logits(2 * h + 1)
                turn(2 * h)
                inner(h)
                weigh(2 * h)
                cross(h)
                logits(2 * h + 2)
                turn(2 * h + 1)
                weigh(2 * h + 1)
            pe.wait_ge(bias_ready, 3)
            pe.wait_ge(st_ready, RH)
            for bh in range(2):
                last = pe.matmul(ps[:, bh, 0:KEYS_S], rep_s[:, bh, :], bias_s[:, :], start=True, stop=True)
            last.then_inc(rep_done, 1)
            head_stat(RH - 1)
            logits(N_PU + 1)
            for u in (N_PU, N_PU + 1):
                turn(u)
                weigh(u)

        def act_even(act, steps, split_w, n_half):
            base = W_BASE["even_in"]

            def evacuate(t_, j, b, kinds):
                if t_:
                    split_w(base + t_ + 1, (base + j + 1) % 2)
                for h in range(2):
                    if h == 0:
                        act.wait_ge(half_used, t_ + 1)
                    else:
                        act.wait_ge(w_used, CR + base + t_ + 1)
                    act.activation(proj[:, b + h, :], ps[:, 2 * j + h, 0:TOK], kinds[h][0], scale=kinds[h][1])\
                       .then_inc(p_evac, 1)

            plain = (ACT.Copy, 1.0)
            key = (ACT.Copy, float(np.float32(P ** -0.5)))
            for b in range(0, EVEN_BLOCKS, 2):
                kinds = ((plain, key) if B_RQK <= b < B_RQK + 8 else
                         ((ACT.Silu, 1.0),) * 2 if b >= B_RG else (plain, plain))
                evacuate(b // 2, b // 2 % 2, b, kinds)
                if b == 10:
                    act.wait_ge(vw_tr, 1)
                    act.activation(wi_tok[:, 0:2, :], ps[:, 6, 3 * P:3 * P + 2 * NIH]
                                   .rearrange("p (c n) -> p c n", c=2), ACT.Copy, scale=0.5)
                    act.activation(wi_tok[0:STOK, 2, :], ps[0:STOK, 6, 3 * P + 2 * NIH:3 * P + 3 * NIH], ACT.Copy,
                                   scale=0.5)
                    act.activation(vtok[:, 0:2, :], ps[:, 6, 0:2 * P].rearrange("p (c n) -> p c n", c=2), ACT.Copy)
                    act.activation(vtok[0:STOK, 2, :], ps[0:STOK, 6, 2 * P:3 * P], ACT.Copy).then_inc(vw_ready, 1)
                    rectify(act, 0)
                elif b == 12:
                    rectify(act, 1)
                    rectify(act, 2)
                elif b == 16:
                    rectify(act, 3)
                    rectify(act, 4)

            def spread(h):
                act.wait_ge(tr_k, h + 1)
                if h:
                    act.wait_ge(kvs_done, h)
                act.activation(kt[:, 0:2, :], ps[:, 0, 0:2 * P].rearrange("p (c n) -> p c n", c=2), ACT.Copy,
                               scale=kdec[:, 0, h:h + 1])
                act.activation(kt[0:STOK, 2, :], ps[0:STOK, 0, 2 * P:3 * P], ACT.Copy,
                               scale=kdec[0:STOK, 1, h:h + 1]).then_inc(kt_ready, 1)

            def exponents(u):
                act.wait_ge(lg_ready, u + 1)
                for g in range(NKV):
                    row_ = lg[:, u % 2, g, 0:unit_keys(u)]
                    last = act.activation(row_, row_, ACT.Exp, bias=nmx[:, u % 2, g:g + 1],
                                          accum_out=sm[:, u % 2, g:g + 1])
                last.then_inc(exp_ready, 1)

            def turned(u):
                act.wait_ge(pt_done, u + 1)
                if u >= 2:
                    act.wait_ge(pv_done, u - 1)
                chunks = unit_chunks(u)
                wide = min(len(chunks), 2) * 2 * P
                last = act.activation(pT[:, u % 2, 0:wide], ps[:, 6, 0:wide], ACT.Copy)
                if len(chunks) == 3:
                    last = act.activation(pT[0:STOK, u % 2, 4 * P:6 * P], ps[0:STOK, 2, 0:2 * P], ACT.Copy)
                last.then_inc(pt_ready, 1)

            act.wait_ge(p_evac, PB + EVEN_BLOCKS)
            act.wait_ge(even_in_dma, 16 * EVEN_DMAS)
            for h in range(RH):
                spread(h)
                exponents(2 * h)
                act.wait_ge(kv_done, h + 1)
                if h:
                    act.wait_ge(s2_ready, h)
                act.activation(s1[:, :], ps[:, 2, 0:P], ACT.Copy).then_inc(s1_ready, 1)
                turned(2 * h)
                exponents(2 * h + 1)
                act.wait_ge(o_done, h + 1)
                act.activation(f[:, 4 + h, :], ps[:, 3, 0:TOK], ACT.Copy)
                act.activation(proj[:, RQ[h], :], ps[:, 3, 0:TOK], ACT.Square).then_inc(osq_ready, 1)
                turned(2 * h + 1)
            act.wait_ge(rep_done, 1)
            act.activation(bias_r[:, :, :], ps[:, 0:2, 0:KEYS_S], ACT.Copy).then_inc(rep_ready, 1)
            for u in (N_PU, N_PU + 1):
                exponents(u)
                turned(u)
            act.wait_ge(orec_ready, RH)
            act.activation(proj[:, B_RQK:B_RQK + 8:2, :], proj[:, B_RQK + 1:B_RQK + 8:2, :], ACT.Sqrt)\
               .then_inc(orstd_ready, 1)
            act.wait_ge(st_stored, 32 * RH)
            act.wait_ge(kvo_stored, 16 * 3)
            act.wait_ge(pv_done, len(UNITS))
            for k in range(KC):
                if k % 4 == 0:
                    act.wait_ge(o_ready, k // 4 + 1)
                act.activation(xn_hi[:, k, :], f[:, k, :], ACT.Copy).then_inc(xn_high, 1)

        def rectify(act, x_):
            act.wait_ge(ix_done, x_ + 1)
            if x_ >= 2:
                act.wait_ge(relu_used, x_ - 1)
            bank, width = ((7, 4 * P), (6, 4 * P), (7, 4 * P), (6, KEYS_S), (7, KEYS_S))[x_]
            act.activation(relu[:, x_ % 2, 0:width], ps[:, bank, 0:width], ACT.Relu, scale=HD ** -0.5)\
               .then_inc(relu_ready, 1)

        def dve_even(dve, steps, split_w, softplus):
            base = W_BASE["even_in"]

            def rotate(b, r, par, kind):
                dve.wait_ge(p_evac, PB + b + 1)
                src = proj[:, b, :]
                dve.tensor_tensor(rope_a[:, par, :], src, ropet[:, 2 * kind, :], ALU.mult)
                dve.wait_ge(rope_mm, r + 1)
                steps.did(dve.tensor_tensor(rope_b[:, par, :], ps[:, 4 + par, 0:TOK], ropet[:, 2 * kind + 1, :],
                                            ALU.mult))
                steps.wait()
                dve.tensor_tensor(src, rope_a[:, par, :], rope_b[:, par, :], ALU.add).then_inc(rope_done, 1)

            def top(work, rounds):
                for r in range(rounds):
                    steps.did(dve.max(top8[0:work.shape[0], :], work))
                    steps.wait()
                    steps.did(dve.match_replace(work, top8[0:work.shape[0], :], work, TAKEN))
                    steps.wait()

            def mask(work, bias):
                seen = work[:, 0:bias.shape[1]]
                steps.did(dve.tensor_scalar(seen, seen, -2.0e38, NEG, ALU.is_gt, ALU.mult))
                steps.wait()
                dve.tensor_tensor(bias, bias, seen, ALU.add).then_inc(bias_ready, 1)

            def score(qt, x_, heads):
                nk = P * (qt + 1)
                dve.wait_ge(relu_ready, x_ + 1)
                for y_, h in enumerate(heads):
                    last = dve.scalar_tensor_tensor(scores[qt], relu[:, x_ % 2, nk * y_:nk * (y_ + 1)],
                                                    wi_tok[:, qt, h:h + 1], bias_p[:, qt, 0:nk] if h == 0
                                                    else scores[qt], ALU.mult, ALU.add)
                    if y_ < len(heads) - 1:
                        steps.did(last)
                        steps.wait()
                last.then_inc(relu_used, 1)
                dve.wait_ge(relu_used, x_ + 1)

            scores = score_p[:, 0:P], score_p[:, P:3 * P]
            score_rounds = (TOPK_S + PAD_S) // 8
            dve.wait_ge(rope_in, 16)
            for b in range(0, EVEN_BLOCKS, 2):
                if b:
                    split_w(base + b // 2 + 1, (base + b // 2 + 1) % 2)
                if b < 8:
                    rotate(b, b, 0, 0)
                    rotate(b + 1, b + 1, 1, 0)
                if b == 8:
                    steps.did(dve.memset(qiz[:, :, :, :], 0.0))
                    steps.did(dve.memset(score_s[:, KEYS_S:KEYS_S + PAD_S], WINS))
                    steps.wait()
                    dve.wait_ge(rope_done, CR + 8)
                    for r in range(NR):
                        dve.tensor_copy(qsm[:, :, r, :], tokens(proj[:, B_Q + r, PTOK:TOK]))
                    for s in range(2):
                        rows = slice(HD * s, HD * (s + 1))
                        for c in range(2):
                            last = dve.tensor_copy(qiz[rows, :, 2 * s + c, :], tokens(proj[rows, B_QI + c, PTOK:TOK]))
                    last.then_inc(qiz_ready, 1)
                    softplus()
                    dve.wait_ge(even_in_dma, 16 * EVEN_DMAS)
                elif b == 12:
                    dve.wait_ge(wis_mm, 1)
                    steps.did(dve.tensor_tensor(wis[:, :, :], ps[:, 6, 0:2 * NIH].rearrange("p (b h) -> p b h", b=2),
                                                hmask[:, :].unsqueeze(1).to_broadcast([P, 2, NIH]), ALU.mult))
                    steps.wait()
                    dve.reduce_sum(wis1[:, :], wis[:, :, :], axis=AX).then_inc(wis_ready, 1)
                    score(0, 0, range(NIH))
                if B_RQK <= b < B_RQK + 8:
                    rotate(b, b - B_RQK + 8, 0, 1)
                    rotate(b + 1, b - B_RQK + 9, 1, 1)
                if b == 12:
                    top(scores[0], 3)
                elif b == 14:
                    score(1, 1, (0, 1))
                    score(1, 2, (2, 3))
                    top(scores[0], 2)
                elif b == 16:
                    top(scores[0], 3)
                    mask(scores[0], bias_p[:, 0, 0:P])
                elif b == 18:
                    dve.wait_ge(wis_ready, 1)
                    for bh in range(2):
                        dve.wait_ge(relu_ready, 4 + bh)
                        last = dve.tensor_scalar(relu[:, 1 - bh, 0:KEYS_S], relu[:, 1 - bh, 0:KEYS_S],
                                                 wis1[:, bh:bh + 1], None, ALU.mult)
                    last.then_inc(weighed, 1)
                    top(scores[1], 3)
                elif b == 20:
                    dve.wait_ge(ixs_done, 1)
                    steps.did(dve.tensor_tensor(score_s[:, 0:KEYS_S], ps[0:STOK, 6, 0:KEYS_S], bias_s[:, :], ALU.add))
                    steps.wait()
                    top(scores[1], 3)
                elif b == 22:
                    top(scores[1], 2)
                    mask(scores[1], bias_p[:, 1, :])
                    top(score_s[:, :], 3)
                elif b == 24:
                    top(score_s[:, :], score_rounds - 3)
                    mask(score_s[:, :], bias_s[:, :])

            def spread(h):
                dve.wait_ge(tr_v, h + 1)
                if h:
                    dve.wait_ge(o_done, h)
                dve.tensor_copy(vt[:, 0:2, :], ps[:, 1, 0:2 * P].rearrange("p (c n) -> p c n", c=2))
                dve.tensor_copy(vt[0:STOK, 2, :], ps[0:STOK, 1, 2 * P:3 * P]).then_inc(vt_ready, 1)
                dve.tensor_tensor(qd[:, :], proj[:, RQ[h], P:2 * P], qdec[:, h, 0:P], ALU.mult)
                dve.tensor_tensor(qz[:, :].rearrange("p (b w) -> p b w", b=NB)[:, :, 0:NT],
                                  tokens(proj[:, RQ[h], PTOK:TOK]), tokens(qdec[:, h, P:P + STOK]), ALU.mult)\
                   .then_inc(qd_ready, 1)
                dve.wait_ge(att_done, h + 1)
                dve.tensor_tensor(am[:, :, :], ps[:, 2, 0:2 * P].rearrange("p (c n) -> p c n", c=2),
                                  dec_p[:, h, :].unsqueeze(1).to_broadcast([P, 2, P]), ALU.mult)
                dve.tensor_tensor(am_s[:, :], ps[0:STOK, 2, PTOK:TOK], dec_s[:, h, :], ALU.mult)\
                   .then_inc(am_ready, 1)

            def variance(h):
                dve.wait_ge(ostat_done, h + 1)
                dve.tensor_scalar(proj[:, RK[h], :], ps[:, 3, 0:TOK], EPS, None, ALU.add).then_inc(ovar_ready, 1)

            def invert(h):
                dve.wait_ge(ovar_ready, h + 1)
                dve.reciprocal(proj[:, RK[h], :], proj[:, RK[h], :]).then_inc(orec_ready, 1)

            def states(h):
                dve.wait_ge(kvs_done, h + 1)
                dve.wait_ge(st_landed, 16 * (h + 1))
                dve.wait_ge(o_done, h + 1)
                for i in range(2):
                    last = dve.scalar_tensor_tensor(st_out[:, 4 * i:4 * i + 4, :], st_in[:, 4 * i:4 * i + 4, :],
                                                    CDEC_S[h], ps[:, i, :].rearrange("p (b v) -> p b v", b=4),
                                                    ALU.mult, ALU.add)
                last.then_inc(st_ready, 1)

            def soft(u):
                kind, a, j = UNITS[u]
                nk = unit_keys(u)
                bias = bias_p[:, a, 0:nk] if kind == "p" else bias_r[:, a, :]
                dve.wait_ge(lg_done, u + 1)
                dve.wait_ge(bias_ready, a + 1 if kind == "p" else 3)
                if u >= 2:
                    dve.wait_ge(pt_done, u - 1)
                if u == N_PU:
                    dve.wait_ge(rep_ready, 1)
                steps.did(dve.scalar_tensor_tensor(lg[:, u % 2, :, 0:nk], logit_banks(u), HD ** -0.5,
                                                   bias.unsqueeze(1).to_broadcast([P, NKV, nk]), ALU.mult, ALU.add))
                steps.wait()
                dve.reduce_max(nmx[:, u % 2, :], lg[:, u % 2, :, 0:nk], axis=AX, negate=True).then_inc(lg_ready, 1)

            def divide(u):
                nk = unit_keys(u)
                dve.wait_ge(exp_ready, u + 1)
                steps.did(dve.reciprocal(rsm[:, u % 2, :], sm[:, u % 2, :]))
                steps.wait()
                for g in range(NKV):
                    last = dve.tensor_scalar(lg[:, u % 2, g, 0:nk], lg[:, u % 2, g, 0:nk], rsm[:, u % 2, g:g + 1],
                                             None, ALU.mult)
                last.then_inc(pr_ready, 1)

            def leave(u):
                kind, a, j = UNITS[u]
                dve.wait_ge(pv_done, u + 1)
                if kind == "p":
                    dve.tensor_copy(f[:, j, P * a:P * (a + 1)], ps[:, 7, 0:P]).then_inc(pv_out, 1)
                    return
                for g in range(NKV):
                    rows = slice(HD * g, HD * (g + 1))
                    src = ps[rows, 7, :].rearrange("p (b g r t) -> p g b r t", b=NB, g=NKV, r=NR)
                    for r in range(NR):
                        last = dve.tensor_copy(tokens(f[rows, r, PTOK:TOK]), src[:, g, :, r, :])
                last.then_inc(o_ready, 1)

            dve.wait_ge(p_evac, PB + EVEN_BLOCKS)
            dve.wait_ge(rope_done, CR + 16)
            dve.memset(qz[:, :], 0.0).then_inc(qd_ready, 1)
            dve.wait_ge(qd_ready, 1)
            soft(0)
            for h in range(RH):
                spread(h)
                if h:
                    variance(h - 1)
                divide(2 * h)
                dve.wait_ge(vt_ready, h + 1)
                if h:
                    dve.wait_ge(kvs_done, h)
                dve.tensor_tensor(vm[:, :, :], vt[0:STOK, 2, :].unsqueeze(1).to_broadcast([STOK, NB, P]),
                                  bmask[:, :].unsqueeze(2).to_broadcast([STOK, NB, P]), ALU.mult)\
                   .then_inc(vm_ready, 1)
                soft(2 * h + 1)
                dve.wait_ge(s1_ready, h + 1)
                if h:
                    dve.wait_ge(st_stored, 32 * h)
                dve.scalar_tensor_tensor(s2[:, :], s1[:, :], CDEC_P[h], ps[:, 2, P:2 * P], ALU.mult, ALU.add)\
                   .then_inc(s2_ready, 1)
                if h:
                    invert(h - 1)
                leave(2 * h)
                divide(2 * h + 1)
                if h < RH - 1:
                    soft(2 * h + 2)
                states(h)
                leave(2 * h + 1)
            variance(RH - 1)
            soft(N_PU)
            divide(N_PU)
            soft(N_PU + 1)
            invert(RH - 1)
            divide(N_PU + 1)
            steps.did(dve.tensor_tensor(f[:, 4:8, :], f[:, 4:8, :], proj[:, B_RG:B_RG + RH, :], ALU.mult))
            leave(N_PU + 1)

            def low(k):
                dve.wait_ge(xn_high, 8 * PREP["even_out"] + k + 1)
                dve.tensor_tensor(xn_lo[:, k, :], f[:, k, :], xn_hi[:, k, :].bitcast(F32), ALU.subtract)\
                   .then_inc(xn_ready, 1)

            steps.wait()
            dve.wait_ge(orstd_ready, 1)
            dve.tensor_tensor(f[:, 4:8, :], f[:, 4:8, :], proj[:, B_RQK:B_RQK + 8:2, :], ALU.mult).then_inc(o_ready, 1)
            for k in range(KC):
                low(k)

        odd_in_dma = sem("odd_in_dma")
        xc_ready = sem("xc_ready")
        conv_ready = sem("conv_ready")
        rg_done, rg_act = sem("rg_done"), sem("rg_act")
        tanh_ready, aa_ready = sem("tanh_ready"), sem("aa_ready")
        m2_ready, mult_ready, b_ready = sem("m2_ready"), sem("mult_ready"), sem("b_ready")
        gelu_ready, y_ready, odd_stored = sem("gelu_ready"), sem("y_ready"), sem("odd_stored")
        tails_ready, hl_ready = sem("tails_ready"), sem("hl_ready")

        def gp_odd(gp):
            gp.wait_ge(w_used, CR + W_BASE["odd_in"])
            for dst, src in ((cst[:, :, :, :], t["conv_state"]), (cw[:, :, :], t["conv_w"]), (cb[:, :, :], t["conv_b"]),
                             (brg[:, :, :], t["b_rg"]), (h0[:, :, :], t["h0"]), (wrg[:, :, :], t["w_rg"])):
                gp.dma_start(dst, src).then_inc(odd_in_dma, 16)
            gp.wait_ge(tails_ready, 1)
            gp.dma_start(t["tails"], tails[:, :, :, :]).then_inc(odd_stored, 16)
            gp.wait_ge(hl_ready, 1)
            gp.dma_start(t["hlast"], hlast[:, :, :]).then_inc(odd_stored, 16)
            gp.wait_ge(odd_stored, 32)

        def pe_odd(pe, three_passes, w_half, both_blocks):
            base = W_BASE["odd_in"]

            def tile(c):
                s, j = (base + c) % 2, c % 2
                pe.wait_ge(xc_ready, CR + c - 1)
                if c == 0:
                    both_blocks("odd_in", s, (0, 1), True).then_inc(w_used, 1)
                    return
                for h in range(2):
                    w_half(base + c, h)
                    for k in range(KC):
                        last = three_passes(ps[:, 2 * j + h, 0:TOK], s, (h * KC + k) * P, xn_hi[:, k, :],
                                            xn_lo[:, k, :], k == 0, k == KC - 1)
                    last.then_inc(half_used if h == 0 else w_used, 1)

            def gates(c):
                pe.wait_ge(conv_ready, CR + c + 1)
                for h in range(2):
                    n = 2 * c + h
                    if n >= 4:
                        pe.wait_ge(rg_act, n - 3)
                    pe.matmul(ps[:, 4 + n % 4, 0:TOK], wrg[:, KC * h + c, :], conv[:, c, :], start=True, stop=True)\
                      .then_inc(rg_done, 1)

            for c in range(KC):
                tile(c)
                if c == 0:
                    pe.wait_ge(odd_in_dma, 16 * 6)
                if c > 1:
                    gates(c - 2)
            gates(KC - 2)
            gates(KC - 1)

        def act_odd(act, steps, split_w, n_half):
            base = W_BASE["odd_in"]
            act.wait_ge(odd_in_dma, 16 * 6)

            def gates(c):
                for h, dst in ((0, ra), (1, ib)):
                    act.wait_ge(rg_done, 2 * c + h + 1)
                    act.activation(dst[:, c, :], ps[:, 4 + (2 * c + h) % 4, 0:TOK], ACT.Sigmoid,
                                   bias=brg[:, h, c:c + 1]).then_inc(rg_act, 1)

            for c in range(KC):
                j = c % 2
                if c:
                    split_w(base + c + 1, (base + c + 1) % 2)
                act.wait_ge(half_used, EVEN_IN_TILES + OUT_TILES + c + 1)
                act.activation(gate[:, c, :], ps[:, 2 * j, 0:TOK], ACT.Copy)
                act.wait_ge(w_used, CR + base + c + 1)
                act.wait_ge(conv_ready, CR + c - 1)
                act.activation(xc[:, j, 3:3 + PTOK], ps[:, 2 * j + 1, 0:PTOK], ACT.Copy)
                act.activation(xc[:, j, PTOK + 3:XW].rearrange("p (b t) -> p b t", b=NB)[:, :, 3:3 + NT],
                               ps[:, 2 * j + 1, PTOK:TOK].rearrange("p (b t) -> p b t", b=NB), ACT.Copy)\
                   .then_inc(xc_ready, 1)
                if c > 1:
                    gates(c - 2)
            gates(KC - 2)
            gates(KC - 1)
            act.wait_ge(sp_done, 1)
            act.wait_ge(rg_act, 2 * KC)
            for c in range(KC):
                steps.did(act.activation(gtmp[:, c, :], ra[:, c, :], ACT.Tanh, scale=spl8n[:, c:c + 1]))
                steps.wait()
                act.activation(ra[:, c, :], ra[:, c, :], ACT.Exp, scale=spl8[:, c:c + 1]).then_inc(aa_ready, 1)
            for c in range(KC):
                act.wait_ge(m2_ready, c + 1)
                act.activation(gtmp[:, c, :], gtmp[:, c, :], ACT.Sqrt).then_inc(mult_ready, 1)
            for c in range(KC):
                act.activation(gate[:, c, :], gate[:, c, :], ACT.Gelu_apprx_tanh).then_inc(gelu_ready, 1)
            for k in range(KC):
                act.wait_ge(y_ready, k + 1)
                act.activation(xn_hi[:, k, :], f[:, k, :], ACT.Copy).then_inc(xn_high, 1)

        def dve_odd(dve, steps, split_w):
            base = W_BASE["odd_in"]
            dve.wait_ge(odd_in_dma, 16 * 6)
            for j in range(2):
                steps.did(dve.memset(xc[:, j, 0:3], 0.0))
            steps.wait()

            def gated(c):
                dve.wait_ge(rg_act, 2 * c + 2)
                steps.did(dve.tensor_tensor(ib[:, c, :], ib[:, c, :], conv[:, c, :], ALU.mult))

            def convolve(c):
                j = c % 2
                seqs = xc[:, j, PTOK + 3:XW].rearrange("p (b t) -> p b t", b=NB)
                steps.did(dve.tensor_copy(seqs[:, :, 0:3], at4(cst, c)))
                dve.wait_ge(xc_ready, CR + c + 1)
                steps.wait()
                dst_p = at(conv, c)[:, 0:PTOK]
                dst_s = at(conv, c)[:, PTOK:TOK].rearrange("p (b t) -> p b t", b=NB)
                for tap in range(CONVW):
                    wt = at(cw, c)[:, tap:tap + 1]
                    src_p, src_s = xc[:, j, tap:tap + PTOK], seqs[:, :, tap:tap + NT]
                    if tap == 0:
                        bias = at(cb, c)
                        dve.tensor_scalar(dst_p, src_p, wt, bias, ALU.mult, ALU.add)
                        steps.did(dve.tensor_scalar(dst_s, src_s, wt, bias, ALU.mult, ALU.add))
                    else:
                        steps.wait()
                        dve.scalar_tensor_tensor(dst_p, src_p, wt, dst_p, ALU.mult, ALU.add)
                        steps.did(dve.scalar_tensor_tensor(dst_s, src_s, wt, dst_s, ALU.mult, ALU.add))
                tl = at4(tails, c)
                steps.did(dve.tensor_copy(tl[:, 0, :], xc[:, j, PTOK:PTOK + 3]))
                dve.tensor_copy(tl[:, 1:NCOND, :], seqs[:, :, NT:NT + 3]).then_inc(conv_ready, 1)

            for c in range(KC):
                if c:
                    split_w(base + c + 1, (base + c + 1) % 2)
                if c:
                    convolve(c - 1)
                if c > 2:
                    gated(c - 3)
            convolve(KC - 1)
            for c in range(KC - 3, KC):
                gated(c)
            steps.wait()
            steps.did(dve.tensor_copy(b0[:, :, :], ib[:, :, 0:1]))
            dve.wait_ge(conv_ready, CR + KC)
            dve.sem_inc(tails_ready, 1)
            for c in range(KC):
                dve.wait_ge(aa_ready, c + 1)
                if c == 0:
                    steps.wait()
                steps.did(dve.tensor_tensor(conv[:, c, :], ra[:, c, :], ra[:, c, :], ALU.mult))
                steps.wait()
                dve.scalar_tensor_tensor(gtmp[:, c, :], conv[:, c, :], 1.0, gtmp[:, c, :], ALU.add, ALU.mult)\
                   .then_inc(m2_ready, 1)
            first = lambda buf: buf[:, :, PTOK:TOK].rearrange("p c (b t) -> p c b t", b=NB)[:, :, :, 0]
            steps.did(dve.tensor_tensor(tah[:, :, :], first(ra), h0[:, :, :], ALU.mult))
            steps.wait()
            for c in range(KC):
                dve.wait_ge(mult_ready, c + 1)
                last = steps.did(dve.tensor_tensor(ib[:, c, :], ib[:, c, :], gtmp[:, c, :], ALU.mult))
            steps.wait()
            dve.memset(first(ra), 0.0)
            dve.memset(ra[:, :, 0:1], 0.0)
            steps.did(dve.tensor_copy(ib[:, :, 0:1], b0[:, :, :]))
            steps.did(dve.tensor_tensor(first(ib), first(ib), tah[:, :, :], ALU.add))
            steps.wait()
            flat = lambda buf: buf[:, :, :].rearrange("p c n -> p (c n)")
            steps.did(dve.tensor_tensor_scan(flat(conv), flat(ra), flat(ib), 0.0, ALU.mult, ALU.add))
            steps.wait()

            def low(k):
                dve.wait_ge(xn_high, 8 * PREP["odd_out"] + k + 1)
                dve.tensor_tensor(xn_lo[:, k, :], f[:, k, :], xn_hi[:, k, :].bitcast(F32), ALU.subtract)\
                   .then_inc(xn_ready, 1)
            for c in range(KC):
                dve.wait_ge(gelu_ready, c + 1)
                dve.tensor_tensor(f[:, c, :], conv[:, c, :], gate[:, c, :], ALU.mult).then_inc(y_ready, 1)
                if c:
                    low(c - 1)
            low(KC - 1)
            dve.tensor_copy(hlast[:, :, 0:1], conv[:, :, PTOK - 1:PTOK])
            dve.tensor_copy(hlast[:, :, 1:NCOND], conv[:, :, PTOK:TOK].rearrange("p c (b t) -> p c b t", b=NB)[:, :, :, NT - 1])\
               .then_inc(hl_ready, 1)

        block = ctx.enter_context(nc.Block())

        @block.sync
        def _(sp_):
            def load_w(src, tile, n, width=2048):
                s = slot(n)
                for h, cols in enumerate(halves(width)):
                    if not (isinstance(n, int) and n < 2):
                        sp_.wait_ge(w_split, CR + 2 * n + h - 3)
                    sp_.dma_start(w_raw[:, s, cols], row(src, tile)[:, cols]).then_inc(w_landed[s][h], 16)

            def load_a(g):
                for h in range(2):
                    if not (isinstance(g, int) and g == A_FRONT):
                        sp_.wait_ge(a_split, CR + 2 * (g - A_FRONT) + h - 1)
                    sp_.dma_start(a_raw[:, h, :], row(t["ada"], 2 * g + h)).then_inc(a_landed[h], 16)

            def slot(n):
                return n % 2 if isinstance(n, int) else n_slot[0]

            n_slot = [0]

            def at_slot(s):
                n_slot[0] = s

            def load_front(n):
                s = slot(n)
                for h, cols in enumerate(halves(2048)):
                    if not (isinstance(n, int) and n < 2):
                        sp_.wait_ge(w_split, CR + 2 * n + h - 3)
                    sp_.dma_start(w_raw[:, s, cols], row(t["ada"], 2 * n + h)).then_inc(w_landed[s][h], 16)

            sp_.dma_start(cT[:, :, :], t["cT"].rearrange("k p c -> p k c")).then_inc(c_in, 16)
            load_front(0)
            load_front(1)
            sp_.dma_start(lam[:, :], t["lam"]).then_inc(lam_in, 16)
            sp_.dma_start(sel2[:, :], t["sel2"]).then_inc(sel_in, 16)
            sp_.dma_start(b_ada[:, :], t["b_ada"]).then_inc(bada_in, 16)
            for dst, src in ((g_pre[:, :, :], t["g_pre"]),
                             (g_post[:, :, :], t["g_post"]), (ident[:, :], t["ident"]),
                             (ones_d[:, :], t["ones_d"]),
                             (pages[:, :], t["pages"])):
                sp_.dma_start(dst, src).then_inc(const_in, 16)
            with sp_.Fori(1, A_FRONT // 2) as q:
                for j in range(2):
                    at_slot(j)
                    load_front(2 * q + j)
            sp_.dma_start(x[:, :, :], t["x"].rearrange("k p n -> p k n")).then_inc(const_in, 16)
            load_a(A_FRONT)

            def gate_loads(ff):
                stage = f"gate{ff}"
                for first, lo, hi in ((True, 0, 1), (False, 1, HFC)):
                    def body(i):
                        for j in range(2):
                            at_slot((W_BASE[stage] + j) % 2)
                            load_w(t["gu"], FC * ff + 2 * i + j, W_BASE[stage] + 2 * i + j)
                            if stage in A_BASE and not (ff == 0 and first and j == 0):
                                load_a(A_BASE[stage] + 2 * i + j)
                    if first:
                        body(0)
                    else:
                        with sp_.Fori(lo, hi) as i:
                            body(i)

            def down_loads(ff):
                stage = f"down{ff}"

                for lo, hi, ada in DOWN_LOOPS[ff]:
                    def body(i, first=False):
                        for m in range(2):
                            for h in range(2):
                                j = 2 * m + h
                                at_slot((W_BASE[stage] + j) % 2)
                                load_w(t["down"], 2 * KC * ff + 4 * i + j, W_BASE[stage] + 4 * i + j, HFC * P)
                            if ada and not (first and m == 0):
                                load_a(A_BASE[stage] + 2 * i + m)
                    if lo == 0 and stage == "down2":
                        body(0, True)
                        lo = 1
                    with sp_.Fori(lo, hi) as i:
                        body(i)
                if stage == "down1":
                    load_a(A_BASE["down2"])

            def proj_loads(stage, first_tile, count):
                with sp_.Fori(0, count // 2) as i:
                    for j in range(2):
                        at_slot((W_BASE[stage] + j) % 2)
                        load_w(t["pj"], first_tile + 2 * i + j, W_BASE[stage] + 2 * i + j)
                if count % 2:
                    load_w(t["pj"], first_tile + count - 1, W_BASE[stage] + count - 1)

            gate_loads(0)
            down_loads(0)
            proj_loads("even_in", 0, EVEN_IN_TILES)
            proj_loads("even_out", EVEN_IN_TILES, OUT_TILES)
            gate_loads(1)
            down_loads(1)
            gate_loads(2)
            down_loads(2)
            proj_loads("odd_in", EVEN_IN_TILES + OUT_TILES, ODD_IN_TILES)
            proj_loads("odd_out", EVEN_IN_TILES + OUT_TILES + ODD_IN_TILES, OUT_TILES)
            gate_loads(3)
            down_loads(3)
            sp_.wait_ge(x_ready, 8 * 6)
            sp_.dma_start(t["y"].rearrange("k p n -> p k n"), x[:, :, :]).then_inc(out_done, 16)
            sp_.wait_ge(out_done, 16)

        @block.tensor
        def _(pe):
            def three_passes(out, s, w_at, xhi, xlo, start, stop):
                hi = w_hi[s][:, w_at:w_at + P]
                pe.matmul(out, hi, xhi, start=start, stop=False)
                pe.matmul(out, hi, xlo, start=False, stop=False)
                return pe.matmul(out, w_lo[s][:, w_at:w_at + P], xhi, start=False, stop=stop)

            def w_half(n, h):
                pe.wait_ge(w_split, CR + 2 * n + h + 1)

            def both_blocks(stage, s, banks, signal_half=False):
                w_half(W_BASE[stage], 0)
                w_half(W_BASE[stage], 1)
                for k in range(KC):
                    pe.wait_ge(xn_ready, 8 * PREP[stage] + k + 1)
                    for b in range(2):
                        last = three_passes(ps[:, banks[b], 0:TOK], s, (b * KC + k) * P, xn_hi[:, k, :],
                                            xn_lo[:, k, :], k == 0, k == KC - 1)
                        if k == KC - 1 and b == 0 and signal_half:
                            last.then_inc(half_used, 1)
                return last

            def ada_product(g, j, front=False):
                pe.wait_ge(row_ready, CR + g - 1)
                for h in range(2):
                    if front:
                        w_half(g, h)
                    else:
                        pe.wait_ge(a_split, CR + 2 * (g - A_FRONT) + h + 1)
                    for k in range(KC // 2):
                        at_ = ((KC // 2 * h if front else 0) + k) * ADA_COLS
                        for part, w in enumerate((w_hi[j], w_lo[j]) if front else (a_hi[h], a_lo[h])):
                            last = pe.matmul(ps[0:2 * NCOND, B_ADA[j], 0:ADA_COLS], c2[:, KC // 2 * h + k, :],
                                             w[:, at_:at_ + ADA_COLS], start=(h == k == part == 0),
                                             stop=(h == part == 1 and k == KC // 2 - 1))
                    if not front:
                        last.then_inc(a_used, 1)
                if front:
                    last.then_inc(w_used, 1)

            def ada_transpose(q):
                pe.wait_ge(row_ready, CR + 2 * q + 2)
                pe.wait_ge(mod_ready, 1 + q)
                for c in range(2):
                    last = pe.matmul(ps[:, B_MOD, 2 * c * NCOND:2 * (c + 1) * NCOND],
                                     ada_row[:, c * P:(c + 1) * P], sel2[:, :], start=True, stop=True)
                last.then_inc(sel_done, 1)

            def stat_x(prep):
                s = PNORM[prep]
                for k in range(KC):
                    pe.wait_ge(sqx_ready, 8 * s + k + 1)
                    last = pe.matmul(ps[:, B_STAT, 0:TOK], ones_d[:, :], sqx[:, k, :],
                                     start=(k == 0), stop=(k == KC - 1))
                last.then_inc(stat_done, 1)

            def stat_y(stage):
                pe.wait_ge(y_evac, CR + 8 * (SUB[stage] + 1))
                pe.matmul(ps[:, B_STAT, 0:TOK], ones_d[:, :], sqacc[:, :], start=True, stop=True)\
                  .then_inc(stat_done, 1)

            def gate_up(ff):
                stage = f"gate{ff}"

                def body(i, first=False):
                    for j in range(2):
                        n, p, s = W_BASE[stage] + 2 * i + j, FC * ff + 2 * i + j, (W_BASE[stage] + j) % 2
                        if stage in A_BASE:
                            ada_product(A_BASE[stage] + 2 * i + j, j)
                        pe.wait_ge(gu_free, CR + p - 1)
                        if first and j == 0:
                            both_blocks(stage, s, (0, 1)).then_inc(w_used, 1)
                        else:
                            for b in range(2):
                                w_half(n, b)
                                for k in range(KC):
                                    last = three_passes(ps[:, 2 * j + b, 0:TOK], s, (b * KC + k) * P,
                                                        xn_hi[:, k, :], xn_lo[:, k, :], k == 0, k == KC - 1)
                            last.then_inc(w_used, 1)
                    if stage in A_BASE:
                        ada_transpose(A_BASE[stage] // 2 + i)

                body(0, True)
                with pe.Fori(1, HFC) as i:
                    body(i)

            def down(ff):
                stage = f"down{ff}"
                pe.wait_ge(mid_ready, FC * (ff + 1))
                for lo, hi, ada in DOWN_LOOPS[ff]:
                    with pe.Fori(lo, hi) as i:
                        for m in range(2):
                            q = 8 * SUB[stage] + 2 * i + m
                            if ada:
                                ada_product(A_BASE[stage] + 2 * i + m, m)
                            pe.wait_ge(y_evac, CR + q - 1)
                            for h in range(2):
                                j = 2 * m + h
                                s, n = (W_BASE[stage] + j) % 2, W_BASE[stage] + 4 * i + j
                                for k in range(HFC):
                                    if k in (0, KC):
                                        w_half(n, k // KC)
                                    c = HFC * h + k
                                    last = three_passes(ps[:, m, 0:TOK], s, k * P, mid_hi[:, c, :],
                                                        mid_lo[:, c, :], c == 0, c == FC - 1)
                                last.then_inc(w_used, 1)
                        if ada:
                            ada_transpose(A_BASE[stage] // 2 + i)

            def out_projection(stage):
                def body(i, first=False):
                    for j in range(2):
                        s = (W_BASE[stage] + j) % 2
                        if first and j == 0:
                            pe.wait_ge(y_evac, CR + 8 * SUB[stage])
                            both_blocks(stage, s, (0, 1), True).then_inc(w_used, 1)
                            continue
                        for b in range(2):
                            w_half(W_BASE[stage] + 2 * i + j, b)
                            q = 8 * SUB[stage] + 4 * i + 2 * j + b
                            pe.wait_ge(y_evac, CR + q - 1)
                            for k in range(KC):
                                last = three_passes(ps[:, b, 0:TOK], s, (b * KC + k) * P, xn_hi[:, k, :],
                                                    xn_lo[:, k, :], k == 0, k == KC - 1)
                            last.then_inc(half_used if b == 0 else w_used, 1)

                body(0, True)
                with pe.Fori(1, 2) as i:
                    body(i)

            for s_, v in ((w_used, CR), (a_used, CR), (sel_done, 1)):
                pe.sem_inc(s_, v)
            pe.wait_ge(c_split, 1)
            pe.wait_ge(sel_in, 16)
            pe.wait_ge(row_zero, 1)
            with pe.Fori(0, A_FRONT // 2) as q:
                for j in range(2):
                    ada_product(2 * q + j, j, True)
                ada_transpose(q)
            pe.wait_ge(const_in, 16 * 6)
            stat_x("gate0")
            gate_up(0)
            down(0)
            stat_y("down0")
            stat_x("even_in")
            pe_even(pe, three_passes, w_half, both_blocks)
            out_projection("even_out")
            stat_y("even_out")
            stat_x("gate1")
            gate_up(1)
            down(1)
            stat_y("down1")
            stat_x("gate2")
            gate_up(2)
            down(2)
            stat_y("down2")
            stat_x("odd_in")
            pe_odd(pe, three_passes, w_half, both_blocks)
            out_projection("odd_out")
            stat_y("odd_out")
            stat_x("gate3")
            gate_up(3)
            down(3)
            stat_y("down3")

        @block.scalar
        def _(act):
            def split_w(n, s, width=2048):
                act.wait_ge(w_used, CR + n - 1)
                for h, cols in enumerate(halves(width)):
                    act.wait_ge(w_landed[s][h], 16 * (half_of(n) + 1))
                    act.activation(w_hi[s][:, cols], w_raw[:, s, cols], ACT.Copy).then_inc(w_high, 1)

            def half_of(n):
                return n // 2 if isinstance(n, int) else n_half[0]

            n_half = [0]

            def split_a(g):
                for h in range(2):
                    act.wait_ge(a_landed[h], 16 * (g - A_FRONT + 1))
                    act.wait_ge(a_used, CR + 2 * (g - A_FRONT) + h - 1)
                    act.activation(a_hi[h][:, :], a_raw[:, h, :], ACT.Copy).then_inc(a_high, 1)

            def ada_copy(q, j, front=False):
                if front:
                    act.wait_ge(w_used, CR + 2 * q + j + 1)
                else:
                    act.wait_ge(a_used, CR + 4 * q + 2 * (j - A_FRONT) + 2)
                if j == 0:
                    act.wait_ge(sel_done, 1 + q)
                act.activation(ada_row[32 * j:32 * j + 2 * NCOND, :], ps[0:2 * NCOND, B_ADA[j], 0:ADA_COLS],
                               ACT.Copy).then_inc(row_ready, 1)

            def ahead(stage):
                split_w(W_BASE[stage] + 1, (W_BASE[stage] + 1) % 2)

            def root(s):
                act.wait_ge(stat_done, s)
                act.activation(rms[:, :], ps[:, B_STAT, 0:TOK], ACT.Sqrt, bias=eps[:, 0:1]).then_inc(rms_ready, 1)

            def squares_x(prep):
                s = PNORM[prep]
                for k in range(KC):
                    if s:
                        act.wait_ge(x_ready, 8 * (s - 1) + k + 1)
                    act.activation(sqx[:, k, :], x[:, k, :], ACT.Square).then_inc(sqx_ready, 1)

            def modulate(prep):
                sub = PNORM[prep]
                act.wait_ge(coef_ready, 2 * sub + 1)
                for k in range(KC):
                    act.wait_ge(xr_ready, 8 * sub + k + 1)
                    steps.did(act.activation(f[:, k, 0:PTOK], f[:, k, 0:PTOK], ACT.Identity,
                                             scale=modT[:, scale_at(sub, k), 0:1],
                                             bias=modT[:, shift_at(sub, k), 0:1]))
                    steps.wait()
                    act.wait_ge(xmod_ready, 8 * sub + k + 1)
                    act.activation(xn_hi[:, k, :], f[:, k, :], ACT.Copy).then_inc(xn_high, 1)

            def gate_up(ff):
                stage = f"gate{ff}"
                def body(i, first=False):
                    for j in range(2):
                        n, p = W_BASE[stage] + 2 * i + j, FC * ff + 2 * i + j
                        if not (first and j == 0):
                            n_half[0] = (W_BASE[stage] + j + 1) // 2 + i
                            split_w(n + 1, (W_BASE[stage] + j + 1) % 2)
                        if stage in A_BASE:
                            ada_copy(A_BASE[stage] // 2 + i, j)
                            split_a(A_BASE[stage] + 2 * i + j + 1)
                        act.wait_ge(w_used, CR + n + 1)
                        act.wait_ge(gu_free, CR + p - 1)
                        act.activation(sil[:, j, :], ps[:, 2 * j, 0:TOK], ACT.Silu).then_inc(sil_ready, 1)
                        act.wait_ge(gu_free, CR + p + 1)
                        act.activation(at(mid_hi, 2 * i + j), hbuf[:, j, :], ACT.Copy).then_inc(mid_high, 1)

                body(0, True)
                with act.Fori(1, HFC) as i:
                    body(i)

            def leave(stage, q, b, m):
                act.wait_ge(y_evac, CR + q - 1)
                act.activation(at(f, m)[:, 0:PTOK], ps[:, b, 0:PTOK], ACT.Copy,
                               scale=gate_of(stage, m)[:, 0:1])
                act.activation(sq2[:, b, :], ps[:, b, 0:TOK], ACT.Square).then_inc(sq_ready, 1)

            def gate_of(stage, m):
                return at(modT, gate_at(SUB[stage], 0) + m)

            def down(ff):
                stage = f"down{ff}"
                act.wait_ge(coef_ready, 2 * SUB[stage] + 2)

                def body(i, ada, last=False):
                    for m in range(2):
                        for h in range(2):
                            j = 2 * m + h
                            if not (last and ff == N_FFN - 1 and j == 3):
                                n_half[0] = (W_BASE[stage] + j + 1) // 2 + 2 * i
                                split_w(W_BASE[stage] + 4 * i + j + 1, (W_BASE[stage] + j + 1) % 2,
                                        2048 if last and j == 3 else HFC * P)
                        if ada:
                            ada_copy(A_BASE[stage] // 2 + i, m)
                            if not (last and ff == 0 and m == 1 or stage == "down2" and i == 1 and m == 1):
                                split_a(A_BASE[stage] + 2 * i + m + 1)
                        act.wait_ge(w_used, CR + W_BASE[stage] + 4 * i + 2 * m + 2)
                        leave(stage, 8 * SUB[stage] + 2 * i + m, m, 2 * i + m)

                down_loops(act, ff, body)

            def out_projection(stage, done):
                act.wait_ge(coef_ready, 2 * SUB[stage] + 2)
                with act.Fori(0, 2) as i:
                    for j in range(2):
                        n_half[0] = (W_BASE[stage] + j + 1) // 2 + i
                        split_w(W_BASE[stage] + 2 * i + j + 1, (W_BASE[stage] + j + 1) % 2)
                        act.wait_ge(half_used, done + 2 * i + j + 1)
                        leave(stage, 8 * SUB[stage] + 4 * i + 2 * j, 0, 4 * i + 2 * j)
                        act.wait_ge(w_used, CR + W_BASE[stage] + 2 * i + j + 1)
                        leave(stage, 8 * SUB[stage] + 4 * i + 2 * j + 1, 1, 4 * i + 2 * j + 1)

            steps = Steps(act, act_step)
            for s_, v in ((mid_high, CR), (row_ready, CR), (p_evac, PB), (xc_ready, CR)):
                act.sem_inc(s_, v)
            act.wait_ge(c_in, 16)
            steps.did(act.activation(cS[:, :, :], cT[:, :, :], ACT.Silu))
            steps.wait()
            act.activation(c2[:, :, 0:NCOND], cS[:, :, :], ACT.Copy).then_inc(c_high, 1)
            n_half[0] = 0
            split_w(0, 0)
            act.wait_ge(row_zero, 1)
            with act.Fori(0, A_FRONT // 2) as q:
                for j in range(2):
                    n_half[0] = q + j
                    split_w(2 * q + j + 1, 1 - j)
                    ada_copy(q, j, True)
            act.wait_ge(sp_e, 1)
            steps.did(act.activation(sp[1][:, :], sp[0][:, :], ACT.Exp, scale=-1.0))
            act.wait_ge(const_in, 16 * 6)
            squares_x("gate0")
            split_a(A_FRONT)
            ahead("gate0")
            root(1)
            modulate("gate0")
            gate_up(0)
            down(0)
            ahead("even_in")
            root(2)
            squares_x("even_in")
            root(3)
            modulate("even_in")
            act_even(act, steps, split_w, n_half)
            out_projection("even_out", EVEN_IN_TILES)
            split_a(A_BASE["gate1"])
            ahead("gate1")
            root(4)
            squares_x("gate1")
            root(5)
            modulate("gate1")
            gate_up(1)
            down(1)
            ahead("gate2")
            root(6)
            squares_x("gate2")
            root(7)
            modulate("gate2")
            gate_up(2)
            down(2)
            ahead("odd_in")
            root(8)
            squares_x("odd_in")
            root(9)
            modulate("odd_in")
            act_odd(act, steps, split_w, n_half)
            out_projection("odd_out", EVEN_IN_TILES + OUT_TILES + ODD_IN_TILES)
            ahead("gate3")
            root(10)
            squares_x("gate3")
            root(11)
            modulate("gate3")
            act.wait_ge(odd_stored, 32)
            gate_up(3)
            down(3)
            root(12)

        @block.vector
        def _(dve):
            def split_w(n, s, width=2048):
                for h, cols in enumerate(halves(width)):
                    dve.wait_ge(w_high, 2 * n + h + 1)
                    dve.tensor_tensor(w_lo[s][:, cols], w_raw[:, s, cols], w_hi[s][:, cols].bitcast(F32),
                                      ALU.subtract).then_inc(w_split, 1)

            def split_a(g):
                for h in range(2):
                    dve.wait_ge(a_high, 2 * (g - A_FRONT) + h + 1)
                    dve.tensor_tensor(a_lo[h][:, :], a_raw[:, h, :], a_hi[h][:, :].bitcast(F32), ALU.subtract)\
                       .then_inc(a_split, 1)

            def ada_bias(q):
                dve.wait_ge(sel_done, 1 + q + 1)
                if isinstance(q, int):
                    dst, bias = modT[:, 4 * q:4 * q + 4, :], b_ada[:, 4 * q:4 * q + 4]
                else:
                    dst, bias = modT[:, bass.ds(4 * q, 4), :], b_ada[:, bass.ds(4 * q, 4)]
                dve.tensor_tensor(dst.rearrange("p (g c) n -> p c g n", g=2),
                                  ps[:, B_MOD, 0:4 * NCOND].rearrange("p (c g n) -> p c g n", c=2, g=2),
                                  bias.rearrange("p (g c) -> p c g", g=2).unsqueeze(3)
                                  .to_broadcast([P, 2, 2, NCOND]), ALU.add).then_inc(mod_ready, 1)

            def scale_factors(sub):
                dve.wait_ge(mod_ready, 1 + MOD_GROUPS(sub, 1) // 2)
                m = modT[:, scale_at(sub, 0):scale_at(sub, KC), :]
                dve.scalar_tensor_tensor(m, m, 1.0, g_pre[:, sub, :].unsqueeze(2).to_broadcast([P, KC, NCOND]),
                                         ALU.add, ALU.mult).then_inc(coef_ready, 1)
                dve.wait_ge(coef_ready, 2 * sub + 1)

            def gate_factors(sub):
                dve.wait_ge(mod_ready, 1 + MOD_GROUPS(sub, 2) // 2)
                m = modT[:, gate_at(sub, 0):gate_at(sub, KC), :]
                dve.scalar_tensor_tensor(m, m, 1.0 if sub % 3 == 1 else 0.5,
                                         g_post[:, sub, :].unsqueeze(2).to_broadcast([P, KC, NCOND]),
                                         ALU.mult, ALU.mult).then_inc(coef_ready, 1)
                dve.wait_ge(coef_ready, 2 * sub + 2)

            def MOD_GROUPS(sub, which):
                return GROUPS * (sub // 3) + 4 * (3 * (sub % 3) + which + 1)

            def ahead(stage):
                split_w(W_BASE[stage] + 1, (W_BASE[stage] + 1) % 2)

            def invert(s):
                dve.wait_ge(rms_ready, s)
                dve.reciprocal(rstd[:, :], rms[:, :]).then_inc(rstd_ready, 1)
                dve.wait_ge(rstd_ready, s)

            def add_residual(stage):
                def add(k):
                    steps.wait(marks[k])
                    dve.tensor_tensor(x[:, k, :], x[:, k, :], f[:, k, :], ALU.add).then_inc(x_ready, 1)
                marks = []
                for k in range(KC):
                    marks.append(steps.did(dve.tensor_tensor(f[:, k, :], f[:, k, :], rstd[:, :], ALU.mult)))
                    if k:
                        add(k - 1)
                add(KC - 1)

            def normed(prep):
                j, sub = PREP[prep], PNORM[prep]

                def low(k):
                    dve.wait_ge(xn_high, 8 * j + k + 1)
                    dve.tensor_tensor(xn_lo[:, k, :], f[:, k, :], xn_hi[:, k, :].bitcast(F32), ALU.subtract)\
                       .then_inc(xn_ready, 1)
                if sub:
                    dve.wait_ge(x_ready, 8 * sub)
                for k in range(KC):
                    dve.tensor_tensor(f[:, k, :], x[:, k, :], rstd[:, :], ALU.mult).then_inc(xr_ready, 1)
                    dve.wait_ge(xr_ready, 8 * sub + k + 1)
                    fs = tokens(f[:, k, PTOK:TOK])
                    steps.did(dve.tensor_tensor(fs, fs, per_sample(modT[:, scale_at(sub, k), 1:NCOND]), ALU.mult))
                    steps.wait()
                    dve.tensor_tensor(fs, fs, per_sample(modT[:, shift_at(sub, k), 1:NCOND]), ALU.add)\
                       .then_inc(xmod_ready, 1)
                    if k:
                        low(k - 1)
                low(KC - 1)

            def gate_up(ff):
                stage = f"gate{ff}"
                def body(i, first=False):
                    for j in range(2):
                        n, p = W_BASE[stage] + 2 * i + j, FC * ff + 2 * i + j
                        if not (first and j == 0):
                            split_w(n + 1, (W_BASE[stage] + j + 1) % 2)
                        if stage in A_BASE:
                            split_a(A_BASE[stage] + 2 * i + j + 1)
                        dve.wait_ge(sil_ready, p + 1)
                        dve.wait_ge(mid_high, CR + p - 1)
                        dve.tensor_tensor(hbuf[:, j, :], ps[:, 2 * j + 1, 0:TOK], sil[:, j, :], ALU.mult)\
                           .then_inc(gu_free, 1)
                        dve.wait_ge(mid_high, CR + p + 1)
                        dve.tensor_tensor(at(mid_lo, 2 * i + j), hbuf[:, j, :],
                                          at(mid_hi, 2 * i + j).bitcast(F32), ALU.subtract).then_inc(mid_ready, 1)
                    if stage in A_BASE:
                        ada_bias(A_BASE[stage] // 2 + i)

                body(0, True)
                with dve.Fori(1, HFC) as i:
                    body(i)

            def leave(stage, q, b, m):
                dve.wait_ge(sq_ready, q + 1)
                dve.tensor_tensor(tokens(at(f, m)[:, PTOK:TOK]), tokens(ps[:, b, PTOK:TOK]),
                                  per_sample(at(modT, gate_at(SUB[stage], 0) + m)[:, 1:NCOND]), ALU.mult)
                dve.wait_ge(y_evac, CR + q)
                dve.tensor_tensor(sqacc[:, :], sqacc[:, :], sq2[:, b, :], ALU.add).then_inc(y_evac, 1)

            def start_sum():
                steps.did(dve.memset(sqacc[:, :], 0.0))
                steps.wait()

            def down(ff):
                stage = f"down{ff}"
                gate_factors(SUB[stage])
                start_sum()

                def body(i, ada, last=False):
                    for m in range(2):
                        for h in range(2):
                            j = 2 * m + h
                            if not (last and ff == N_FFN - 1 and j == 3):
                                split_w(W_BASE[stage] + 4 * i + j + 1, (W_BASE[stage] + j + 1) % 2,
                                        2048 if last and j == 3 else HFC * P)
                        if ada and not (last and ff == 0 and m == 1 or stage == "down2" and i == 1 and m == 1):
                            split_a(A_BASE[stage] + 2 * i + m + 1)
                        dve.wait_ge(w_used, CR + W_BASE[stage] + 4 * i + 2 * m + 2)
                        leave(stage, 8 * SUB[stage] + 2 * i + m, m, 2 * i + m)
                    if ada:
                        ada_bias(A_BASE[stage] // 2 + i)

                down_loops(dve, ff, body)

            def out_projection(stage, done):
                gate_factors(SUB[stage])
                start_sum()
                with dve.Fori(0, 2) as i:
                    for j in range(2):
                        split_w(W_BASE[stage] + 2 * i + j + 1, (W_BASE[stage] + j + 1) % 2)
                        dve.wait_ge(half_used, done + 2 * i + j + 1)
                        leave(stage, 8 * SUB[stage] + 4 * i + 2 * j, 0, 4 * i + 2 * j)
                        dve.wait_ge(w_used, CR + W_BASE[stage] + 2 * i + j + 1)
                        leave(stage, 8 * SUB[stage] + 4 * i + 2 * j + 1, 1, 4 * i + 2 * j + 1)

            def softplus_start():
                z, w = sp[0], sp[2]
                dve.wait_ge(lam_in, 16)
                steps.did(dve.tensor_scalar(w[:, :], lam[:, :], -1.0, None, ALU.mult))
                steps.wait()
                dve.tensor_tensor(z[:, :], w[:, :], lam[:, :], ALU.max).then_inc(sp_e, 1)

            def softplus():
                u, w, s2_, acc = sp[1:]
                dve.wait_ge(act_step, 2)
                steps.did(dve.tensor_scalar(s2_[:, :], u[:, :], 2.0, None, ALU.add))
                steps.wait()
                steps.did(dve.reciprocal(acc[:, :], s2_[:, :]))
                steps.wait()
                steps.did(dve.tensor_tensor(u[:, :], u[:, :], acc[:, :], ALU.mult))
                steps.wait()
                steps.did(dve.tensor_tensor(s2_[:, :], u[:, :], u[:, :], ALU.mult))
                steps.wait()
                steps.did(dve.tensor_scalar(acc[:, :], s2_[:, :], 1.0 / 19.0, None, ALU.mult))
                steps.wait()
                for odd in range(17, 1, -2):
                    steps.did(dve.scalar_tensor_tensor(acc[:, :], acc[:, :], 1.0 / odd, s2_[:, :],
                                                       ALU.add, ALU.mult))
                    steps.wait()
                steps.did(dve.scalar_tensor_tensor(acc[:, :], acc[:, :], 1.0, u[:, :], ALU.add, ALU.mult))
                steps.did(dve.tensor_scalar(w[:, :], w[:, :], 0.0, None, ALU.max))
                steps.wait()
                steps.did(dve.scalar_tensor_tensor(acc[:, :], acc[:, :], 2.0, w[:, :], ALU.mult, ALU.add))
                steps.wait()
                steps.did(dve.tensor_scalar(spl8[:, :], acc[:, :], -8.0, None, ALU.mult))
                dve.tensor_scalar(spl8n[:, :], acc[:, :], 8.0, None, ALU.mult).then_inc(sp_done, 1)

            steps = Steps(dve, dve_step)
            for s_, v in ((w_split, CR), (a_split, CR), (gu_free, CR), (y_evac, CR), (mod_ready, 1),
                          (rope_done, CR), (conv_ready, CR)):
                dve.sem_inc(s_, v)
            dve.wait_ge(c_high, 1)
            dve.tensor_tensor(c2[:, :, NCOND:2 * NCOND], cS[:, :, :], c2[:, :, 0:NCOND].bitcast(F32),
                              ALU.subtract).then_inc(c_split, 1)
            dve.memset(eps[:, :], EPS)
            dve.memset(ada_row[:, :], 0.0).then_inc(row_zero, 1)
            split_w(0, 0)
            softplus_start()
            dve.wait_ge(bada_in, 16)
            with dve.Fori(0, A_FRONT // 2) as q:
                for j in range(2):
                    split_w(2 * q + j + 1, 1 - j)
                ada_bias(q)
            dve.wait_ge(const_in, 16 * 6)
            scale_factors(0)
            ahead("gate0")
            invert(1)
            split_a(A_FRONT)
            normed("gate0")
            gate_up(0)
            down(0)
            scale_factors(1)
            ahead("even_in")
            invert(2)
            add_residual("down0")
            invert(3)
            normed("even_in")
            dve_even(dve, steps, split_w, softplus)
            out_projection("even_out", EVEN_IN_TILES)
            scale_factors(2)
            ahead("gate1")
            invert(4)
            split_a(A_BASE["gate1"])
            add_residual("even_out")
            invert(5)
            normed("gate1")
            gate_up(1)
            down(1)
            scale_factors(3)
            ahead("gate2")
            invert(6)
            add_residual("down1")
            invert(7)
            normed("gate2")
            gate_up(2)
            down(2)
            scale_factors(4)
            ahead("odd_in")
            invert(8)
            add_residual("down2")
            invert(9)
            normed("odd_in")
            dve_odd(dve, steps, split_w)
            out_projection("odd_out", EVEN_IN_TILES + OUT_TILES + ODD_IN_TILES)
            scale_factors(5)
            ahead("gate3")
            invert(10)
            add_residual("odd_out")
            invert(11)
            normed("gate3")
            dve.wait_ge(odd_stored, 32)
            gate_up(3)
            down(3)
            invert(12)
            add_residual("down3")

        @block.gpsimd
        def _(gp):
            gp.wait_ge(const_in, 16 * 6)
            gp_even(gp)
            gp_odd(gp)


def tables():
    pos = np.concatenate([np.arange(PTOK), np.tile(PAST + np.arange(NT), NB)]).astype(np.float32)
    step = np.concatenate([np.arange(PTOK) % P, np.tile(np.arange(NT), NB)]).astype(np.float32)
    own = np.repeat(np.arange(NB), NT)
    tok = np.tile(np.arange(NT), NB)
    two = np.tile(np.eye(NCOND), (2, 1))
    out = {"ident": np.eye(P), "ones_d": np.full((P, P), 1.0 / D), "ones_h": np.full((P, P), 1.0 / P),
           "sel2": np.block([[two, 0 * two], [np.zeros((32 - 2 * NCOND, 2 * NCOND))], [0 * two, two]])}
    perm = np.zeros((P, 2, P))
    rope = np.zeros((P, 4, TOK))
    rope[:, 0] = 1.0
    inv_a = np.power(np.float32(500000.0), -np.arange(0, 16, 2, dtype=np.float32) / np.float32(16))
    inv_r = np.power(np.float32(10000.0), -np.linspace(0.0, 1.0, 64, dtype=np.float32))
    for kind, starts, half, inv in ((0, (0, HD), 8, inv_a), (1, (0,), 64, inv_r)):
        ang = pos[None, :] * inv.astype(np.float32)[:, None]
        for s in starts:
            for i in range(half):
                perm[s + half + i, kind, s + i] = -1.0
                perm[s + i, kind, s + half + i] = 1.0
            for o in (s, s + half):
                rope[o:o + half, 2 * kind] = np.cos(ang)
                rope[o:o + half, 2 * kind + 1] = np.sin(ang)
    out["perm"], out["rope"] = perm, rope
    lg = np.array(LN_G)
    i = np.arange(P)
    diff = i[None, :] - i[:, None]
    out["dec_p"] = np.where(diff >= 0, np.exp(np.maximum(diff, 0) * lg[:, None, None]), 0.0).transpose(1, 0, 2)
    same = (own[:, None] == own[None, :]) & (tok[None, :] >= tok[:, None])
    ds = np.maximum(tok[None, :] - tok[:, None], 0)
    out["dec_s"] = np.where(same, np.exp(ds * lg[:, None, None]), 0.0).transpose(1, 0, 2)
    out["qdec"] = np.broadcast_to(np.exp((step[None, P:] + 1.0) * lg[:, None]), (P, RH, P + STOK))
    kd = np.zeros((P, 2, RH))
    kd[:, 0] = np.exp((P - 1.0 - i[:, None]) * lg[None, :])
    kd[0:STOK, 1] = np.exp((NT - 1.0 - tok[:, None]) * lg[None, :])
    out["kdec"] = kd
    out["bmask"] = (own[:, None] == np.arange(NB)[None, :])
    q = np.arange(PTOK).reshape(2, P)
    out["bias_p"] = np.where(np.arange(PTOK)[None, None, :] <= q[:, :, None], 0.0, NEG).transpose(1, 0, 2)
    bs = np.zeros((STOK, KEYS_S))
    bs[:, PAST:] = np.where((own[:, None] == own[None, :]) & (tok[None, :] <= tok[:, None]), 0.0, NEG)
    out["bias_s"] = bs
    b4, xx, tt = np.meshgrid(np.arange(4), np.arange(4), np.arange(NT), indexing="ij")
    b4, xx, tt = b4.ravel(), xx.ravel(), tt.ravel()
    sel = np.zeros((P, 2, STOK))
    for bh in range(2):
        sel[np.arange(P), bh, NT * (4 * bh + b4) + tt] = 1.0
    out["sel_s"], out["rep_s"] = sel, sel.transpose(2, 1, 0)
    head = 2 * (xx % 2) + xx // 2
    out["hmask"] = (head[:, None] == np.arange(NIH)[None, :])
    return {k: np.ascontiguousarray(v, dtype=np.float32) for k, v in out.items()}


def blocks_of(w, cols, n_blocks):
    w = np.pad(np.asarray(w)[:, cols], ((0, 0), (0, n_blocks * P - len(cols))))
    return w.reshape(KC, P, n_blocks // 2, 2, P).transpose(2, 1, 3, 0, 4).reshape(n_blocks // 2, P, 2 * KC * P)


def lay_out(a):
    d = dict(tables())
    d["x"] = np.concatenate([a["x_prompt"].reshape(PTOK, D), a["x_sample"].reshape(STOK, D)]).T.reshape(KC, P, TOK)
    d["cT"] = np.concatenate([a["c_prompt"], a["c_sample"]]).T.reshape(KC, P, NCOND)
    d["lam"] = a["rg_lambda"].reshape(KC, P).T
    d["b_ada"] = a["b_ada"].reshape(2 * CH_L, P).T
    d["g_pre"] = a["g_pre"].reshape(6, KC, P).transpose(2, 0, 1)
    d["g_post"] = a["g_post"].reshape(6, KC, P).transpose(2, 0, 1)
    d["pages"] = a["page_table"].reshape(1, 2 * NB).astype(np.int32)
    w = a["w_ada"].reshape(2, 2, KC // 2, P, GROUPS, ADA_COLS)
    d["ada"] = w.transpose(0, 4, 1, 3, 2, 5).reshape(2 * GROUPS * 2, P, KC // 2 * ADA_COLS)
    gu = np.stack([a["w_ffn_gate"].reshape(N_FFN, KC, P, FC, P), a["w_ffn_up"].reshape(N_FFN, KC, P, FC, P)])
    d["gu"] = gu.transpose(1, 4, 3, 0, 2, 5).reshape(N_FFN * FC, P, 2 * KC * P)
    wd = a["w_ffn_down"].reshape(N_FFN, 2, HFC, P, KC, P)
    d["down"] = wd.transpose(0, 4, 1, 3, 2, 5).reshape(N_FFN * 2 * KC, P, HFC * P)
    at_ = np.cumsum([0, 512, 128, 128, 256, 4, 64, 512, 512, 512])
    q0, k0, v0, qi0, wi0, ki0, rq0, rk0, rv0, rg0 = at_
    r = lambda s, n: list(range(s, s + n))
    cols = []
    for j in range(NR):
        cols += r(q0 + HD * j, HD) + r(q0 + HD * (NR + j), HD)
    cols += r(k0, P) + r(qi0, 2 * P) + r(ki0, HD) * 2
    for h in range(RH):
        cols += r(rq0 + P * h, P) + r(rk0 + P * h, P)
    w = a["w_in_even"][0]
    wi = np.zeros((D, P), w.dtype)
    wi[:, 0:NIH] = w[:, wi0:wi0 + NIH]
    even = np.concatenate([w[:, cols[:8 * P]], w[:, r(v0, P)], wi, w[:, cols[8 * P:]], w[:, r(rv0, 4 * P)], w[:, r(rg0, 4 * P)]], axis=1)
    rows = []
    for j in range(NR):
        rows += r(HD * j, HD) + r(HD * (NR + j), HD)
    rows += r(512, 512)
    odd = a["w_in_odd"][0]
    cols = sum([r(P * c, P) + r(D + P * c, P) for c in range(KC)], [])
    every = np.arange(D)
    d["pj"] = np.concatenate([blocks_of(even, np.arange(even.shape[1]), EVEN_BLOCKS),
                              blocks_of(a["w_out_even"][0][rows], every, KC),
                              blocks_of(odd, cols, 2 * KC), blocks_of(a["w_out_odd"][0], every, KC)])
    kidx = a["cache_kidx"][0].transpose(0, 2, 1)
    d["pages_kv"] = np.concatenate([np.concatenate([kidx, kidx], axis=1),
                                    a["cache_k"][0].reshape(N_PHYS, PAGE, P).transpose(0, 2, 1),
                                    a["cache_v"][0].reshape(N_PHYS, PAGE, P)], axis=2)
    d["state_ret"] = a["state_ret"][0]
    d["conv_state"] = a["state_conv"][0].reshape(NB, 3, KC, P).transpose(3, 2, 0, 1)
    d["conv_w"] = a["conv_w"][0].reshape(CONVW, KC, P).transpose(2, 1, 0)
    d["conv_b"] = a["conv_b"][0].reshape(KC, P, 1).transpose(1, 0, 2)
    d["b_rg"] = np.stack([a["b_rg_a"][0].reshape(KC, P), a["b_rg_x"][0].reshape(KC, P)]).transpose(2, 0, 1)
    d["h0"] = a["state_rglru"][0].reshape(NB, KC, P).transpose(2, 1, 0)
    d["w_rg"] = np.concatenate([a["w_rg_a"][0], a["w_rg_x"][0]]).transpose(1, 0, 2)
    return {k: np.ascontiguousarray(v) for k, v in d.items()}


OUTS = {"y": (KC, P, TOK), "k_o": (P, TOK), "v_o": (P, TOK), "ki_o": (HD, TOK), "ret_p": (RH, P, P),
        "ret_s": (NB, RH, P, P), "tails": (P, KC, NCOND, 3), "hlast": (P, KC, NCOND)}


def kernel(**inputs):
    import concourse.bacc as bacc
    from concourse.bass_utils import run_bass_kernel_spmd

    nc = bacc.Bacc("TRN2", target_bir_lowering=False, num_devices=1)
    arrays = lay_out({k: np.asarray(v) for k, v in inputs.items()})
    aps, feed = {}, {}
    for name, a in arrays.items():
        feed[f"in_{name}"] = a
        aps[name] = nc.dram_tensor(f"in_{name}", a.shape, mybir.dt.from_np(a.dtype), kind="ExternalInput").ap()
    for name, shape in OUTS.items():
        aps[name] = nc.dram_tensor(f"out_{name}", shape, F32, kind="ExternalOutput").ap()
    build(nc, aps)
    r = run_bass_kernel_spmd(nc, [feed], core_ids=[0]).results[0]
    r = {k: np.asarray(r[f"out_{k}"]) for k in OUTS}
    y = r["y"].reshape(D, TOK).T

    def heads(o, n):
        o = o.T
        return (o[:PTOK].reshape((1, 1, PTOK) + n).copy(), o[PTOK:].reshape((1, NB, NT) + n).copy())

    k_p, k_s = heads(r["k_o"], (NKV, HD))
    v_p, v_s = heads(r["v_o"], (NKV, HD))
    ki_p, ki_s = heads(r["ki_o"], (HD,))
    tails = r["tails"].transpose(2, 3, 1, 0).reshape(NCOND, 3, D)
    hl = r["hlast"].transpose(2, 1, 0).reshape(NCOND, D)
    return (y[:PTOK].reshape(1, PTOK, D).copy(), y[PTOK:].reshape(NB, NT, D).copy(), k_p, v_p, ki_p,
            r["ret_p"][None, None], tails[None, 0:1].copy(), hl[None, 0:1].copy(),
            k_s, v_s, ki_s, r["ret_s"][None], tails[None, 1:].copy(), hl[None, 1:].copy())
```
